# Optimizing a Trainium2 kernel written in Bass

```python
import math
import jax, jax.numpy as jnp
from jax import lax
import numpy as np

D_MODEL = 1024
BATCH = 1
SEQ = 512
DEPTH = 2

HEAD_DIM = 64
FOX_HEADS = (3 * D_MODEL) // (8 * HEAD_DIM)
FOX_WIDTH = FOX_HEADS * HEAD_DIM
DIFF_QK_DIM = 32
DIFF_V_DIM = 2 * DIFF_QK_DIM
DIFF_HEADS = D_MODEL // (4 * DIFF_V_DIM)
DIFF_WIDTH = DIFF_HEADS * DIFF_V_DIM
SGU_HEAD_DIM = 64
SGU_WIDTH = D_MODEL - FOX_WIDTH - DIFF_WIDTH
SGU_HEADS = SGU_WIDTH // SGU_HEAD_DIM
CHUNK = 128
Q_BLOCK = 128
IN_COLS = 3 * FOX_WIDTH + FOX_HEADS + 3 * DIFF_WIDTH + 2 * SGU_WIDTH
D_FF = 2816
ALPHA = (2 * DEPTH) ** 0.25
BETA = (8 * DEPTH) ** -0.25
LN_EPS = 1e-5
NEG_INF = -1e30

kernel_name = 'hybrid_fox_diff_sgu_macaron_deepnorm'

def _layer_norm(x, g, b):
    xf = x.astype(jnp.float32)
    mu = jnp.mean(xf, axis=-1, keepdims=True)
    var = jnp.mean(jnp.square(xf - mu), axis=-1, keepdims=True)
    return ((xf - mu) * lax.rsqrt(var + LN_EPS)).astype(x.dtype) * g + b

def _swiglu(x, w_gate, w_up, w_down):
    return (jax.nn.silu(x @ w_gate) * (x @ w_up)) @ w_down

def _to_blocks(a):
    b, s = a.shape[0], a.shape[1]
    a = a.reshape((b, s // Q_BLOCK, Q_BLOCK) + a.shape[2:])
    return jnp.moveaxis(a, 1, 0)

def _from_blocks(a):
    a = jnp.moveaxis(a, 0, 1)
    return a.reshape((a.shape[0], a.shape[1] * a.shape[2]) + a.shape[3:])

def _forgetting_attention(q, k, v, log_f):
    seq = q.shape[1]
    scale = HEAD_DIM ** -0.5
    c = jnp.cumsum(log_f, axis=1)
    c_k = jnp.transpose(c, (0, 2, 1))
    k_pos = jnp.arange(seq)

    def block(args):
        q_blk, c_blk, i = args
        q_pos = i * Q_BLOCK + jnp.arange(Q_BLOCK)
        s = jnp.einsum('bqhd,bkhd->bhqk', q_blk, k, preferred_element_type=jnp.float32) * scale
        s = s + jnp.transpose(c_blk, (0, 2, 1))[..., None] - c_k[:, :, None, :]
        s = jnp.where(k_pos[None, :] <= q_pos[:, None], s, NEG_INF)
        p = jax.nn.softmax(s, axis=-1).astype(v.dtype)
        return jnp.einsum('bhqk,bkhd->bqhd', p, v)

    nb = seq // Q_BLOCK
    out = lax.map(block, (_to_blocks(q), _to_blocks(c), jnp.arange(nb)))
    return _from_blocks(out)

def _diff_attention(q, k, v, lam, lam_init, norm_g):
    seq = q.shape[1]
    scale = DIFF_QK_DIM ** -0.5
    slopes = 2.0 ** (-8.0 * jnp.arange(1, DIFF_HEADS + 1, dtype=jnp.float32) / DIFF_HEADS)
    k_pos = jnp.arange(seq)

    def block(args):
        q_blk, i = args
        q_pos = i * Q_BLOCK + jnp.arange(Q_BLOCK)
        dist = (q_pos[:, None] - k_pos[None, :]).astype(jnp.float32)
        s = jnp.einsum('bqhmd,bkhmd->bhmqk', q_blk, k, preferred_element_type=jnp.float32) * scale
        s = s - slopes[None, :, None, None, None] * dist[None, None, None]
        s = jnp.where(dist >= 0, s, NEG_INF)
        p = jax.nn.softmax(s, axis=-1)
        a = (p[:, :, 0] - lam * p[:, :, 1]).astype(v.dtype)
        return jnp.einsum('bhqk,bkhe->bqhe', a, v)

    nb = seq // Q_BLOCK
    o = _from_blocks(lax.map(block, (_to_blocks(q), jnp.arange(nb))))
    of = o.astype(jnp.float32)
    o = (of * lax.rsqrt(jnp.mean(jnp.square(of), axis=-1, keepdims=True) + LN_EPS)).astype(v.dtype)
    o = o * norm_g.reshape(DIFF_HEADS, DIFF_V_DIM)
    return o * (1.0 - lam_init)

def _chunked_spatial_gating(z, ln_g, ln_b, w_s, b_s):
    u, g = jnp.split(z, 2, axis=-1)
    g = _layer_norm(g, ln_g, ln_b)
    b, s, _ = g.shape
    g = g.reshape(b, s // CHUNK, CHUNK, SGU_HEADS, SGU_HEAD_DIM)
    w = jnp.tril(w_s)
    mixed = jnp.einsum('hts,bcshd->bcthd', w, g) + jnp.transpose(b_s)[None, None, :, :, None]
    return u * mixed.reshape(b, s, SGU_WIDTH)

def _hybrid_mixer(x, w_in, f_bias, lq1, lk1, lq2, lk2, lam_init, diff_norm_g,
                  sgu_ln_g, sgu_ln_b, sgu_w_s, sgu_b_s, w_out):
    b, s, _ = x.shape
    proj = x @ w_in
    i1 = 3 * FOX_WIDTH
    i2 = i1 + FOX_HEADS
    i3 = i2 + 3 * DIFF_WIDTH
    fox_qkv, fox_f, diff_qkv, sgu_z = jnp.split(proj, [i1, i2, i3], axis=-1)
    fq, fk, fv = [t.reshape(b, s, FOX_HEADS, HEAD_DIM) for t in jnp.split(fox_qkv, 3, axis=-1)]
    log_f = jax.nn.log_sigmoid(fox_f.astype(jnp.float32) + f_bias.astype(jnp.float32))
    y_fox = _forgetting_attention(fq, fk, fv, log_f).reshape(b, s, FOX_WIDTH)
    dq, dk, dv = jnp.split(diff_qkv, 3, axis=-1)
    dq = dq.reshape(b, s, DIFF_HEADS, 2, DIFF_QK_DIM)
    dk = dk.reshape(b, s, DIFF_HEADS, 2, DIFF_QK_DIM)
    dv = dv.reshape(b, s, DIFF_HEADS, DIFF_V_DIM)
    lam = (jnp.exp(jnp.sum(lq1.astype(jnp.float32) * lk1.astype(jnp.float32)))
           - jnp.exp(jnp.sum(lq2.astype(jnp.float32) * lk2.astype(jnp.float32))) + lam_init)
    y_diff = _diff_attention(dq, dk, dv, lam, lam_init, diff_norm_g).reshape(b, s, DIFF_WIDTH)
    y_sgu = _chunked_spatial_gating(jax.nn.gelu(sgu_z), sgu_ln_g, sgu_ln_b, sgu_w_s, sgu_b_s)
    return jnp.concatenate([y_fox, y_diff, y_sgu], axis=-1) @ w_out

def setup_inputs(seed: int = 0) -> dict:
    key = jax.random.key(seed)
    ks = jax.random.split(key, 32)
    L, D, F = DEPTH, D_MODEL, D_FF

    def nrm(k, shape, scale):
        return jax.random.normal(k, shape, jnp.float32) * scale

    def gain(k, shape):
        return 1.0 + nrm(k, shape, 0.02)

    return {
        'x': nrm(ks[0], (BATCH, SEQ, D), 1.0),
        'ffn_a_w_gate': nrm(ks[1], (L, D, F), D ** -0.5),
        'ffn_a_w_up': nrm(ks[2], (L, D, F), D ** -0.5),
        'ffn_a_w_down': nrm(ks[3], (L, F, D), BETA * F ** -0.5),
        'norm_a_g': gain(ks[4], (L, D)),
        'norm_a_b': nrm(ks[5], (L, D), 0.02),
        'w_in': nrm(ks[6], (L, D, IN_COLS), D ** -0.5),
        'fox_f_bias': jax.random.uniform(ks[7], (L, FOX_HEADS), jnp.float32, 1.0, 4.0),
        'diff_lambda_q1': nrm(ks[8], (L, DIFF_QK_DIM), 0.1),
        'diff_lambda_k1': nrm(ks[9], (L, DIFF_QK_DIM), 0.1),
        'diff_lambda_q2': nrm(ks[10], (L, DIFF_QK_DIM), 0.1),
        'diff_lambda_k2': nrm(ks[11], (L, DIFF_QK_DIM), 0.1),
        'diff_norm_g': gain(ks[12], (L, DIFF_WIDTH)),
        'sgu_norm_g': gain(ks[13], (L, SGU_WIDTH)),
        'sgu_norm_b': nrm(ks[14], (L, SGU_WIDTH), 0.02),
        'sgu_w_s': nrm(ks[15], (L, SGU_HEADS, CHUNK, CHUNK), CHUNK ** -0.5),
        'sgu_b_s': 1.0 + nrm(ks[16], (L, SGU_HEADS, CHUNK), 0.1),
        'w_out': nrm(ks[17], (L, D, D), BETA * D ** -0.5),
        'norm_m_g': gain(ks[18], (L, D)),
        'norm_m_b': nrm(ks[19], (L, D), 0.02),
        'ffn_b_w_gate': nrm(ks[20], (L, D, F), D ** -0.5),
        'ffn_b_w_up': nrm(ks[21], (L, D, F), D ** -0.5),
        'ffn_b_w_down': nrm(ks[22], (L, F, D), BETA * F ** -0.5),
        'norm_b_g': gain(ks[23], (L, D)),
        'norm_b_b': nrm(ks[24], (L, D), 0.02),
    }

def reference(x, ffn_a_w_gate, ffn_a_w_up, ffn_a_w_down, norm_a_g, norm_a_b,
              w_in, fox_f_bias, diff_lambda_q1, diff_lambda_k1, diff_lambda_q2, diff_lambda_k2,
              diff_norm_g, sgu_norm_g, sgu_norm_b, sgu_w_s, sgu_b_s, w_out, norm_m_g, norm_m_b,
              ffn_b_w_gate, ffn_b_w_up, ffn_b_w_down, norm_b_g, norm_b_b):
    h = x
    for l in range(DEPTH):
        lam_init = 0.8 - 0.6 * math.exp(-0.3 * l)
        h = _layer_norm(ALPHA * h + 0.5 * _swiglu(h, ffn_a_w_gate[l], ffn_a_w_up[l], ffn_a_w_down[l]),
                        norm_a_g[l], norm_a_b[l])
        m = _hybrid_mixer(h, w_in[l], fox_f_bias[l], diff_lambda_q1[l], diff_lambda_k1[l],
                          diff_lambda_q2[l], diff_lambda_k2[l], lam_init, diff_norm_g[l],
                          sgu_norm_g[l], sgu_norm_b[l], sgu_w_s[l], sgu_b_s[l], w_out[l])
        h = _layer_norm(ALPHA * h + m, norm_m_g[l], norm_m_b[l])
        h = _layer_norm(ALPHA * h + 0.5 * _swiglu(h, ffn_b_w_gate[l], ffn_b_w_up[l], ffn_b_w_down[l]),
                        norm_b_g[l], norm_b_b[l])
    return h


_drawn_inputs = setup_inputs


def setup_inputs(seed=0):
    import zlib

    import numpy as np

    out = dict(_drawn_inputs(seed))
    spreads = {}
    factors = {'diff_lambda_q1': 2.923,
     'diff_lambda_k1': 7.174,
     'diff_lambda_q2': 3.924,
     'diff_lambda_k2': 3.282,
     'diff_norm_g': 22.378,
     'sgu_norm_g': 32.903,
     'sgu_norm_b': 33.629,
     'sgu_b_s': 2.892}
    for name, (base, spread) in spreads.items():
        noise = np.random.default_rng([zlib.crc32(name.encode()), seed]).standard_normal(out[name].shape)
        drawn = base * np.exp(spread * noise) if base else spread * noise
        out[name] = __import__('jax').numpy.asarray(drawn.astype(out[name].dtype))
    for name, factor in factors.items():
        out[name] = (out[name] * factor).astype(out[name].dtype)
    return out
```

```python
from contextlib import ExitStack
import math

import numpy as np
import concourse.bass as bass
from concourse import mybir

ALU = mybir.AluOpType
ACT = mybir.ActivationFunctionType
F32 = mybir.dt.float32
F32R = mybir.dt.float32r
BF16 = mybir.dt.bfloat16
AX = mybir.AxisListType

P = 128
L = 2
D = 1024
S = 512
F = 2816
NT = S // P
NC = D // P
NPAIR = F // P // 2
HD = 64
FOX_H, DIFF_H, SGU_H = 6, 4, 6
FOX_W, DIFF_W, SGU_W = FOX_H * HD, DIFF_H * HD, SGU_H * HD
FOX_P, DIFF_P = FOX_H // 2, DIFF_H // 2
ALPHA = (2 * L) ** 0.25
EPS = 1e-5
NEG = -1e30
SLOPES = [2.0 ** (-8.0 * (h + 1) / DIFF_H) for h in range(DIFF_H)]
LAM_INIT = [0.8 - 0.6 * math.exp(-0.3 * l) for l in range(L)]

C_FQ, C_FK, C_FV, C_FF = 0, FOX_W, 2 * FOX_W, 3 * FOX_W
C_DQ = C_FF + FOX_H
C_DK, C_DV, C_Z = C_DQ + DIFF_W, C_DQ + 2 * DIFF_W, C_DQ + 3 * DIFF_W
NAT_COLS = [C_Z, C_Z + 256, C_Z + 512, C_FV, C_FV + 256, C_DV]
NPROJ = len(NAT_COLS) // 2
F_AT = C_FF - NAT_COLS[4]

SLOT = 2 * D

BODIES = FOX_P + DIFF_P
A_FFN, A_NAT, A_QK, A_WO, A_FFN2, A_ALL = (int(x) for x in np.cumsum([0, NPAIR, NPROJ, BODIES, 2, NPAIR]))
B_FFN, B_NAT, B_WO, B_FFN2, B_ALL = (int(x) for x in np.cumsum([0, NPAIR, NPROJ, 2, NPAIR]))
D_ALL = 2 * NPAIR
AU_FFN2, AU_ALL = A_WO, A_ALL - 2
BU_FFN2, BU_ALL = B_WO, B_ALL - 2
Y_WO, Y_FFN2, Y_ALL = NPAIR, NPAIR + 4, 2 * NPAIR + 4
STEPS = 2 * NT
FILL = 8


def build(nc, x_in, a_w, b_w, d_w, gb_row, gb_col, mix_row, mix_col, ws_in, lamv, out):
    ctx = ExitStack()
    with ctx:
        def sb(name, shape, dt=F32):
            return ctx.enter_context(nc.sbuf_tensor(name, shape, dt))

        def sem(name):
            return ctx.enter_context(nc.semaphore(name))

        bank = [ctx.enter_context(nc.psum_tensor(f"bank{i}", [P, 512], F32)) for i in range(8)]

        raw = {s: sb(f"raw{s}", [P, SLOT]) for s in "ABD"}
        whi = {s: sb(f"whi{s}", [P, SLOT], F32R) for s in "ABD"}
        wlo = {s: sb(f"wlo{s}", [P, SLOT], F32R) for s in "ABD"}
        xhi = sb("xhi", [P, NC, S], F32R)
        xlo = sb("xlo", [P, NC, S], F32R)
        res = sb("res", [P, NT, D])
        nat = sb("nat", [P, NT, D])
        s32 = sb("s32", [P, 4, 512])
        hl = sb("hl", [P, 9, 512], F32R)
        vhi = sb("vhi", [P, NT, FOX_W + DIFF_W], F32R)
        vlo = sb("vlo", [P, NT, FOX_W + DIFF_W], F32R)
        gbr = sb("gbr", [P, 2, D])
        gbc = sb("gbc", [P, 2, NC])
        mixr = sb("mixr", [P, DIFF_W + 2 * SGU_W + FOX_H])
        mixc = sb("mixc", [P, SGU_H])
        ident = sb("ident", [P, P])
        identb = sb("identb", [P, P], BF16)
        maskb = sb("maskb", [P, P], BF16)
        since = sb("since", [P, 7 * P])
        selall = sb("selall", [P, FOX_H + DIFF_H])
        alpha = sb("alpha", [P, 1])
        idle = sb("idle", [P, 8])
        free = sb("free", [P, 4])
        eps = sb("eps", [P, 1])
        qscale = sb("qscale", [P, BODIES])
        half = sb("half", [P, 4 * DIFF_H])
        brow = sb("brow", [P, S], F32R)
        sel = sb("sel", [P, 2, P], F32R)
        st = sb("st", [P, NT, 2, 6])
        mv = sb("mv", [P, NT, 2])
        ve = sb("ve", [P, NT])
        rstd = sb("rstd", [P, NT])
        nmr0 = sb("nmr0", [P, NT])
        mone = sb("mone", [P, 1])
        nmr = sb("nmr", [P, NT])
        gst = sb("gst", [P, NT, 6])
        gmv = sb("gmv", [P, NT, 2])
        gve = sb("gve", [P, NT])
        grs = sb("grs", [P, NT])
        flog = sb("flog", [P, NT, FOX_H])
        fneg = sb("fneg", [P, NT, FOX_H])
        fexp = sb("fexp", [P, NT, FOX_H])
        fln = sb("fln", [P, NT, FOX_H])
        lf = sb("lf", [P, NT, FOX_H])
        negm = sb("negm", [P, 4])
        rsum = sb("rsum", [P, 4])
        rinv = sb("rinv", [P, STEPS, 2])
        wlam = sb("wlam", [P, STEPS])
        lamp = sb("lamp", [P, L, 2, 2, 32])
        lams = sb("lams", [P, L, 2])
        lame = sb("lame", [P, L, 2])
        nlam = sb("nlam", [P, L])
        olam = sb("olam", [P, L])
        ilam = sb("ilam", [P, L])
        nlam1 = sb("nlam1", [P, 1])
        dms = sb("dms", [P, NT * DIFF_H])
        dve_ = sb("dve_", [P, NT * DIFF_H])
        drs = sb("drs", [P, NT * DIFF_H])

        landed = {s: sem(f"landed_{s}") for s in "ABD"}
        hi_ok = {s: sem(f"hi_ok_{s}") for s in "ABD"}
        lo_ok = {s: sem(f"lo_ok_{s}") for s in "ABD"}
        used = {s: sem(f"used_{s}") for s in "AB"}
        x_landed = sem("x_landed")
        gb_landed = sem("gb_landed")
        mix_landed = sem("mix_landed")
        ws_landed = sem("ws_landed")
        lam_landed = sem("lam_landed")
        const_ok = sem("const_ok")
        pos_ok = sem("pos_ok")
        za_ok = sem("za_ok")
        zd_ok = sem("zd_ok")
        ident_ok = sem("ident_ok")
        res_ok = sem("res_ok")
        rs_step = sem("rs_step")
        turned = sem("turned")
        x32_ok = sem("x32_ok")
        xhi_ok = sem("xhi_ok")
        x_ok = sem("x_ok")
        silu_ok = {s: sem(f"silu_ok_{s}") for s in "AB"}
        h32_ok = {s: sem(f"h32_ok_{s}") for s in "AB"}
        hhi_ok = {s: sem(f"hhi_ok_{s}") for s in "AB"}
        h_ok = {s: sem(f"h_ok_{s}") for s in "AB"}
        y_done = sem("y_done")
        y_free = sem("y_free")
        st_ok = sem("st_ok")
        mv_ok = sem("mv_ok")
        ve_ok = sem("ve_ok")
        rstd_ok = sem("rstd_ok")
        nmr_step = sem("nmr_step")
        nmr_ok = sem("nmr_ok")
        nat_done = {s: sem(f"nat_done_{s}") for s in "AB"}
        vhi_ok = sem("vhi_ok")
        nat_free = {s: sem(f"nat_free_{s}") for s in "AB"}
        f_ok = sem("f_ok")
        fneg_ok = sem("fneg_ok")
        fexp_ok = sem("fexp_ok")
        fln_ok = sem("fln_ok")
        lf_ok = sem("lf_ok")
        cum_done = sem("cum_done")
        chi_ok = sem("chi_ok")
        c_ok = sem("c_ok")
        ws_tri = sem("ws_tri")
        wshi_ok = sem("wshi_ok")
        wslo_ok = sem("wslo_ok")
        gst_ok = sem("gst_ok")
        gmv_ok = sem("gmv_ok")
        gve_ok = sem("gve_ok")
        grs_ok = sem("grs_ok")
        gn_ok = sem("gn_ok")
        gg_ok = sem("gg_ok")
        gb_ok = sem("gb_ok")
        ghi_ok = sem("ghi_ok")
        glo_ok = sem("glo_ok")
        sgu_done = sem("sgu_done")
        sgu_out = sem("sgu_out")
        q_done = sem("q_done")
        qhi_ok = sem("qhi_ok")
        khi_ok = sem("khi_ok")
        qk_ok = sem("qk_ok")
        s_done = [sem(f"s_done{m}") for m in range(2)]
        max_ok = [sem(f"max_ok{m}") for m in range(2)]
        exp_ok = [sem(f"exp_ok{m}") for m in range(2)]
        rinv_ok = sem("rinv_ok")
        wlam_ok = sem("wlam_ok")
        mixp_ok = sem("mixp_ok")
        pt_done = sem("pt_done")
        pthi_ok = sem("pthi_ok")
        pt_ok = sem("pt_ok")
        pv_done = sem("pv_done")
        o_ok = sem("o_ok")
        sq_ok = sem("sq_ok")
        dms_ok = sem("dms_ok")
        dve_ok = sem("dve_ok")
        drs_ok = sem("drs_ok")
        dn_ok = sem("dn_ok")
        dgs_ok = sem("dgs_ok")
        y_ok = sem("y_ok")
        lam_step = sem("lam_step")
        lame_ok = sem("lame_ok")
        ilam_ok = sem("ilam_ok")
        nlam1_ok = sem("nlam1_ok")
        fin_step = sem("fin_step")
        fin_ok = sem("fin_ok")
        out_done = sem("out_done")

        wsr = s32[:, 0:2, :].rearrange("p a n -> p (a n)")[:, 0:SGU_H * P]
        hlf = hl[:, :, :].rearrange("p a n -> p (a n)")
        ghi = hlf[:, 0:NT * SGU_W].rearrange("p (t n) -> p t n", t=NT)
        glo = hlf[:, NT * SGU_W:2 * NT * SGU_W].rearrange("p (t n) -> p t n", t=NT)
        wshi = hlf[:, 2 * NT * SGU_W:2 * NT * SGU_W + SGU_H * P]
        wslo = hlf[:, 2 * NT * SGU_W + SGU_H * P:2 * NT * SGU_W + 2 * SGU_H * P]
        silu = {"A": s32[:, 0, :], "B": s32[:, 1, :]}
        h32 = {"A": s32[:, 2, :], "B": s32[:, 3, :]}
        hhi = {"A": hl[:, 0, :], "B": hl[:, 2, :]}
        hlo = {"A": hl[:, 1, :], "B": hl[:, 3, :]}
        qhi, qlo, khi, klo = (hl[:, i, :] for i in range(4))
        pthi = [hl[:, 4, :], hl[:, 5, :]]
        ptlo = [hl[:, 6, :], hl[:, 7, :]]
        diff_g = mixr[:, 0:DIFF_W]
        sgu_g = mixr[:, DIFF_W:DIFF_W + SGU_W]
        sgu_b = mixr[:, DIFF_W + SGU_W:DIFF_W + 2 * SGU_W]
        f_bias = mixr[:, DIFF_W + 2 * SGU_W:]
        Y_DIFF, Y_SGU = FOX_W, FOX_W + DIFF_W
        sq = s32[:, 0:2, :].rearrange("p a n -> p (a n)").rearrange("p (t n) -> p t n", t=NT)

        def turn_bank(c, scaled):
            return 2 + c % 6 if scaled else c % 4

        block = ctx.enter_context(nc.Block())

        @block.sync
        def _(sp):
            w_in_dram = {"A": a_w, "B": b_w, "D": d_w}

            def fill(s, n):
                if isinstance(n, int) and n == 0:
                    sp.dma_start(raw[s][:, :], w_in_dram[s][0, :, :]).then_inc(landed[s], 16)
                    return
                sp.wait_ge(lo_ok[s], n)
                sp.dma_start(raw[s][:, :], w_in_dram[s][bass.ds(n, 1), :, :].rearrange("a p n -> (a p) n")).then_inc(landed[s], 16)

            def norm_params(q):
                sp.dma_start(gbr[:, :, :], gb_row[bass.ds(q, 1), :, :].broadcast_to([P, 2, D])).then_inc(gb_landed, 16)
                sp.dma_start(gbc[:, :, :], gb_col[bass.ds(q, 1), :, :, :].rearrange("a p g c -> (a p) g c")).then_inc(gb_landed, 16)

            def ffn(l, f):
                a0 = l * A_ALL + (A_FFN2 if f else A_FFN)
                b0 = l * B_ALL + (B_FFN2 if f else B_FFN)
                with sp.Fori(0, NPAIR - 1) as i:
                    fill("A", a0 + i + 1)
                    fill("B", b0 + i + 1)
                    fill("D", l * D_ALL + f * NPAIR + i + 1)
                fill("A", a0 + NPAIR)
                q = 3 * l + 2 * f
                sp.wait_ge(res_ok, q + 1)
                sp.wait_ge(x32_ok, (4 * l + 3 * f + 1) * NC)
                norm_params(q + 1)

            sp.dma_start(nat[:, :, :], x_in).then_inc(x_landed, 16)
            norm_params(0)
            fill("A", 0)
            sp.dma_start(lamp[:, :, :, :, :], lamv.broadcast_to([P, L, 2, 2, 32])).then_inc(lam_landed, 16)
            with sp.Fori(0, L) as l:
                fill("B", l * B_ALL)
                fill("D", l * D_ALL)
                sp.wait_ge(y_ok, l)
                sp.dma_start(mixr[:, :], mix_row[bass.ds(l, 1), :].broadcast_to([P, mix_row.shape[1]])).then_inc(mix_landed, 16)
                sp.dma_start(mixc[:, :], mix_col[bass.ds(l, 1), :, :].rearrange("a p n -> (a p) n")).then_inc(mix_landed, 16)
                ffn(l, 0)
                fill("B", l * B_ALL + B_NAT)
                fill("D", l * D_ALL + NPAIR)
                sp.wait_ge(x_ok, (4 * l + 2) * NC)
                sp.dma_start(wsr, ws_in[bass.ds(l, 1), :, :].rearrange("a p n -> (a p) n")).then_inc(ws_landed, 16)
                for j in range(NPROJ):
                    fill("A", l * A_ALL + A_NAT + j + 1)
                    fill("B", l * B_ALL + B_NAT + j + 1)
                sp.wait_ge(res_ok, 3 * l + 2)
                sp.wait_ge(x32_ok, (4 * l + 2) * NC)
                norm_params(3 * l + 2)
                for p in range(BODIES):
                    fill("A", l * A_ALL + A_QK + p + 1)
                for w in range(2):
                    fill("A", l * A_ALL + A_WO + w + 1)
                    fill("B", l * B_ALL + B_WO + w + 1)
                ffn(l, 1)
            for t in range(NT):
                sp.wait_ge(fin_ok, t + 1)
                sp.dma_start(out[:, t, :], nat[:, t, :]).then_inc(out_done, 16)
            sp.wait_ge(out_done, 16 * NT)

        @block.gpsimd
        def _(pool):
            g = nc.gpsimd
            n = 0

            def done(ins):
                nonlocal n
                n += 1
                ins.then_inc(const_ok, 1)

            g.memset(ident[:, :], 0.0).then_inc(ident_ok, 1)
            pool.wait_ge(ident_ok, 1)
            g.affine_select(out=ident[:, :], in_=ident[:, :], compare_op=ALU.not_equal, fill=1.0, base=0,
                            pattern=[[-1, P]], channel_multiplier=1).then_inc(ident_ok, 1)
            done(g.memset(identb[:, :], 0.0))
            done(g.memset(maskb[:, :], 0.0))
            done(g.memset(since[:, :], 1.0))
            done(g.memset(selall[:, :], 0.0))
            done(g.memset(half[:, :], -0.5))
            done(g.memset(alpha[:, :], ALPHA))
            done(g.memset(eps[:, :], EPS))
            done(g.memset(mone[:, :], -1.0))
            done(g.memset(brow[:, :].bitcast(F32), 0.0))
            for l in range(L):
                done(g.memset(olam[:, l:l + 1], 1.0 - LAM_INIT[l]))
                done(g.memset(ilam[:, l:l + 1], LAM_INIT[l]))
            for p in range(BODIES):
                done(g.memset(qscale[:, p:p + 1], HD ** -0.5 if p < FOX_P else (HD // 2) ** -0.5))
            pool.wait_ge(const_ok, n)
            done(g.affine_select(out=identb[:, :], in_=identb[:, :], compare_op=ALU.not_equal, fill=1.0, base=0,
                                 pattern=[[-1, P]], channel_multiplier=1))
            done(g.affine_select(out=maskb[:, :], in_=maskb[:, :], compare_op=ALU.is_ge, fill=NEG, base=0,
                                 pattern=[[-1, P]], channel_multiplier=1))
            done(g.affine_select(out=since[:, :], in_=since[:, :], compare_op=ALU.is_ge, fill=0.0, base=-3 * P,
                                 pattern=[[1, 7 * P]], channel_multiplier=-1))
            for r in (0, 32):
                pool.wait_ge(const_ok, n)
                v = selall[r:r + 32, 0:FOX_H]
                done(g.affine_select(out=v, in_=v, compare_op=ALU.not_equal, fill=-1.0, base=0,
                                     pattern=[[-1, FOX_H]], channel_multiplier=1))
            pool.wait_ge(const_ok, n)
            for h in range(DIFF_H):
                done(g.memset(selall[64:65, FOX_H + h:FOX_H + h + 1], SLOPES[h]))
            g.iota(s32[64:65, 0, :], pattern=[[1, S]], base=0, channel_multiplier=0,
                   allow_small_or_imprecise_dtypes=True).then_inc(pos_ok, 1)
            assert n == CONSTS
            pool.wait_ge(pos_ok, 1)

            def wait_here():
                g.tensor_tensor(idle[:, 1:2], eps[:, :], eps[:, :], ALU.add)

            def residual(l, j):
                q = 3 * l + j
                if j == 0:
                    pool.wait_ge(x_landed, 16)
                pool.wait_ge(gb_landed, 32 * q + 32)
                pool.wait_ge(za_ok, 3 * q)
                pool.wait_ge(zd_ok, q)
                s0 = q * 10
                for w in range(2):
                    g.tensor_tensor(gbr[:, w, :], gbr[:, w, :], alpha[:, :].broadcast_to([P, D]), ALU.mult).then_inc(rs_step, 1)
                pool.wait_ge(rs_step, s0 + 2)
                for t in range(NT):
                    g.tensor_tensor(res[:, t, :], nat[:, t, :], gbr[:, 0, :], ALU.mult).then_inc(rs_step, 1)
                for t in range(NT):
                    pool.wait_ge(rs_step, s0 + 3 + t)
                    ins = g.tensor_tensor(res[:, t, :], res[:, t, :], gbr[:, 1, :], ALU.add)
                    ins.then_inc(*((rs_step, 1) if t < NT - 1 else (res_ok, 1)))
                g.memset(idle[:, 2:3], 0.0).then_inc(rs_step, 1)

            def root(v, out_, in_, step, k, ready, n_):
                g.tensor_tensor(v, in_, eps[:, :].broadcast_to([P, n_]), ALU.add).then_inc(step, 1)
                pool.wait_ge(step, k)
                g.tensor_tensor(out_, v, half[:, 0:n_], ALU.pow).then_inc(ready, 1)

            def norm(l, j):
                q = 3 * l + j
                for h in range(2):
                    t = slice(2 * h, 2 * h + 2)
                    pool.wait_ge(mv_ok, NT * q + 2 * h + 2)
                    root(ve[:, t], rstd[:, t], mv[:, t, 1], ve_ok, 2 * q + h + 1, rstd_ok, 2)
                    pool.wait_ge(rstd_ok, 2 * q + h + 1)
                    g.tensor_tensor(nmr0[:, t], mv[:, t, 0], rstd[:, t], ALU.mult).then_inc(nmr_step, 1)
                    pool.wait_ge(nmr_step, 2 * q + h + 1)
                    g.tensor_tensor(nmr[:, t], nmr0[:, t], mone[:, :].broadcast_to([P, 2]), ALU.mult).then_inc(nmr_ok, 1)

            with pool.Fori(0, L) as l:
                residual(l, 0)
                norm(l, 0)
                residual(l, 1)
                pool.wait_ge(ws_landed, 16 * l + 16)
                wait_here()
                g.affine_select(out=wsr, in_=wsr, compare_op=ALU.is_ge, fill=0.0, base=0,
                                pattern=[[0, SGU_H], [1, P]], channel_multiplier=-1).then_inc(ws_tri, 1)
                pool.wait_ge(gmv_ok, NT * l + NT)
                root(gve[:, :], grs[:, :], gmv[:, :, 1], gve_ok, l + 1, grs_ok, NT)
                pool.wait_ge(dms_ok, l + 1)
                root(dve_[:, :], drs[:, :], dms[:, :], dve_ok, l + 1, drs_ok, NT * DIFF_H)
                norm(l, 1)
                residual(l, 2)
                norm(l, 2)

        @block.scalar
        def _(act):
            a = nc.scalar

            def split(s, n):
                act.wait_ge(landed[s], n * 16 + 16)
                a.activation(whi[s][:, :], raw[s][:, :], ACT.Copy).then_inc(hi_ok[s], 1)

            def turn(T, scaled):
                for c in range(NC):
                    act.wait_ge(turned, T * NC + c + 1)
                    if c >= 4:
                        act.wait_ge(x_ok, T * NC + c - 3)
                    if scaled:
                        ins = a.activation(s32[:, c % 4, :], bank[turn_bank(c, scaled)][:, :], ACT.Identity,
                                           bias=gbc[:, 1, c:c + 1], scale=gbc[:, 0, c:c + 1])
                    else:
                        ins = a.activation(s32[:, c % 4, :], bank[turn_bank(c, scaled)][:, :], ACT.Copy)
                    ins.then_inc(x32_ok, 1)

            def normalise(l, j):
                q = 3 * l + j
                for t in range(NT - 1):
                    act.wait_ge(nmr_ok, 2 * q + t // 2 + 1)
                    a.activation(nat[:, t, :], res[:, t, :], ACT.Identity, bias=nmr[:, t:t + 1],
                                 scale=rstd[:, t:t + 1]).then_inc(za_ok, 1)

            def ffn(l, f):
                act.wait_ge(gb_landed, 32 * (3 * l + 2 * f) + 32)
                turn(4 * l + 3 * f, True)
                with act.Fori(0, NPAIR) as i:
                    it = l * 2 * NPAIR + f * NPAIR + i
                    y = l * Y_ALL + f * Y_FFN2 + i
                    act.wait_ge(y_done, y * 8)
                    split("B", l * B_ALL + f * B_FFN2 + i)
                    split("D", it)
                    act.wait_ge(used["A"], l * AU_ALL + f * AU_FFN2 + i + 1)
                    a.activation(silu["A"], bank[0][:, :], ACT.Silu).then_inc(silu_ok["A"], 1)
                    split("A", l * A_ALL + f * A_FFN2 + i + 1)
                    act.wait_ge(h32_ok["A"], it + 1)
                    a.activation(hhi["A"], h32["A"], ACT.Copy).then_inc(hhi_ok["A"], 1)
                    act.wait_ge(used["B"], l * BU_ALL + f * BU_FFN2 + i + 1)
                    for h in range(2):
                        a.activation(silu["B"][:, h * 256:h * 256 + 256], bank[2][:, h * 256:h * 256 + 256],
                                     ACT.Silu).then_inc(silu_ok["B"], 1)
                    for h in range(2):
                        act.wait_ge(h32_ok["B"], it * 2 + h + 1)
                        a.activation(hhi["B"][:, h * 256:h * 256 + 256], h32["B"][:, h * 256:h * 256 + 256],
                                     ACT.Copy).then_inc(hhi_ok["B"], 1)
                normalise(l, 2 * f)

            split("A", 0)
            act.wait_ge(lam_landed, 16)
            act.wait_ge(lam_step, 2)
            a.activation(lame[:, :, :], lams[:, :, :], ACT.Exp).then_inc(lame_ok, 1)
            act.wait_ge(pos_ok, 2)
            with act.Fori(0, L) as l:
                ffn(l, 0)
                act.wait_ge(gb_landed, 32 * (3 * l + 1) + 32)
                turn(4 * l + 1, True)
                act.wait_ge(res_ok, 3 * l + 2)
                split("B", l * B_ALL + B_NAT)
                for j in range(NPROJ):
                    for s in "AB":
                        k = 2 * j + (s == "B")
                        for t in range(NT):
                            if t < NT - 1:
                                act.wait_ge(nat_done[s], l * 3 * NPROJ + 3 * j + t + 1)
                            elif s == "A":
                                act.wait_ge(used["A"], l * AU_ALL + A_NAT + j + 1)
                            else:
                                act.wait_ge(used["B"], l * BU_ALL + B_NAT + j + 1)
                            src = bank[t + (4 if s == "B" else 0)]
                            if k == 0:
                                a.activation(nat[:, t, Y_SGU:Y_SGU + 256], src[:, 0:256], ACT.Gelu_apprx_tanh).then_inc(nat_free[s], 1)
                            elif k == 1:
                                a.activation(nat[:, t, Y_SGU + 256:Y_SGU + SGU_W], src[:, 0:128], ACT.Gelu_apprx_tanh)
                                a.activation(nat[:, t, 0:128], src[:, 128:256], ACT.Gelu_apprx_tanh).then_inc(nat_free[s], 1)
                            elif k == 2:
                                a.activation(nat[:, t, 128:SGU_W], src[:, 0:256], ACT.Gelu_apprx_tanh).then_inc(nat_free[s], 1)
                            elif k == 3:
                                a.activation(vhi[:, t, 0:256], src[:, 0:256], ACT.Copy).then_inc(vhi_ok, 1)
                            elif k == 4:
                                a.activation(vhi[:, t, 256:FOX_W], src[:, 0:FOX_W - 256], ACT.Copy).then_inc(vhi_ok, 1)
                            else:
                                a.activation(vhi[:, t, FOX_W:FOX_W + DIFF_W], src[:, 0:256], ACT.Copy).then_inc(vhi_ok, 1)
                        if k == 2:
                            act.wait_ge(ws_tri, l + 1)
                            a.activation(wshi, wsr, ACT.Copy).then_inc(wshi_ok, 1)
                        if k == 4:
                            act.wait_ge(fneg_ok, l + 1)
                            a.activation(fexp[:, :, :], fneg[:, :, :], ACT.Exp).then_inc(fexp_ok, 1)
                            act.wait_ge(fexp_ok, l + 1)
                            a.activation(fln[:, :, :], fexp[:, :, :], ACT.Ln, bias=1.0).then_inc(fln_ok, 1)
                            act.wait_ge(gb_ok, NT * l + NT)
                            a.activation(ghi, nat[:, :, 0:SGU_W], ACT.Copy).then_inc(ghi_ok, 1)
                        if s == "A":
                            split(s, l * A_ALL + A_NAT + j + 1)
                        elif j < NPROJ - 1:
                            split(s, l * B_ALL + B_NAT + j + 1)
                act.wait_ge(cum_done, l + 1)
                a.activation(brow[0:FOX_H, :], bank[0][0:FOX_H, :], ACT.Copy).then_inc(chi_ok, 1)

                def project(body, b):
                    act.wait_ge(q_done, body + 1)
                    a.activation(qhi, bank[6][:, :], ACT.Copy, scale=qscale[:, bass.ds(b, 1)]).then_inc(qhi_ok, 1)
                    act.wait_ge(used["A"], l * AU_ALL + A_QK + b + 1)
                    a.activation(khi, bank[7][:, :], ACT.Copy).then_inc(khi_ok, 1)

                def heads(b, body_d, maps, more):
                    body = l * BODIES + b
                    K = body * STEPS
                    KD = body_d * STEPS
                    act.wait_ge(pv_done, K)
                    for k in range(STEPS + 1):
                        if k < STEPS:
                            for m in range(maps):
                                km = (K if m == 0 else KD) + k
                                act.wait_ge(max_ok[m], km + 1)
                                if k >= 2:
                                    act.wait_ge(pt_done, K + k - 1)
                                w = (k % NT + 1) * P
                                i = 2 * (k % 2) + m
                                a.activation(s32[:, i, 0:w], bank[i][:, 0:w], ACT.Exp, bias=negm[:, i:i + 1],
                                             accum_out=rsum[:, i:i + 1]).then_inc(exp_ok[m], 1)
                        if k >= 1:
                            j = k - 1
                            w = (j % NT + 1) * P
                            act.wait_ge(pt_done, K + j + 1)
                            if j >= 2:
                                act.wait_ge(pv_done, K + j - 1)
                            a.activation(pthi[j % 2][:, 0:w], bank[4 + j % 2][:, 0:w], ACT.Copy).then_inc(pthi_ok, 1)
                        if k == STEPS - 1:
                            if more:
                                project(body + 1, b + 1)
                        if k == STEPS - 2 and more:
                            act.wait_ge(used["A"], l * AU_ALL + A_QK + b + 2)
                            split("A", l * A_ALL + A_QK + b + 2)

                project(l * BODIES, 0)
                split("A", l * A_ALL + A_QK + 1)
                with act.Fori(0, FOX_P) as p:
                    heads(p, l, 1, True)
                for p in range(DIFF_P):
                    heads(FOX_P + p, l * DIFF_P + p, 2, p < DIFF_P - 1)
                split("B", l * B_ALL + B_WO)
                turn(4 * l + 2, False)
                for w in range(4):
                    act.wait_ge(y_done, (l * Y_ALL + Y_WO + w) * 8 + 8)
                    if w % 2 == 0:
                        split("A", l * A_ALL + A_WO + w // 2 + 1)
                    elif w == 1:
                        split("B", l * B_ALL + B_WO + 1)
                normalise(l, 1)
                ffn(l, 1)

        @block.tensor
        def _(pe):
            t_ = nc.tensor

            def product(out_, pairs, start=True, stop=True, check=False):
                n = 3 * len(pairs)
                k = 0
                for (shi, slo), (mhi, mlo) in pairs:
                    for a_, b_ in ((shi, mhi), (shi, mlo), (slo, mhi)):
                        k += 1
                        ins = t_.matmul(out_, a_, b_, start=(start and k == 1), stop=(stop and k == n), skip_group_check=check)
                return ins

            def w(s, lo, n):
                return whi[s][:, lo:lo + n], wlo[s][:, lo:lo + n]

            def x(c, lo=0, n=S):
                return xhi[:, c, lo:lo + n], xlo[:, c, lo:lo + n]

            def turn(T, scaled):
                for c in range(NC):
                    n = 6 if scaled else 4
                    if c >= n:
                        pe.wait_ge(x32_ok, T * NC + c - n + 1)
                    for t in range(NT):
                        ins = t_.transpose(bank[turn_bank(c, scaled)][:, t * P:t * P + P], nat[:, t, c * P:c * P + P], ident[:, :])
                    ins.then_inc(turned, 1)

            def outputs(y, parts):
                for r in range(2):
                    for n, (stat, slot, off, wait) in enumerate(parts):
                        wait(r)
                        for b in range(4):
                            t, hf = divmod(4 * r + b, 2)
                            if n == 0:
                                pe.wait_ge(y_free, y * 8 + 4 * r + b + 1)
                            ins = product(bank[4 + b][:, :], [(stat(t), w(slot, off + hf * 512, 512))],
                                          start=(n == 0), stop=(n == 1))
                            if n == 1:
                                ins.then_inc(y_done, 1)

            def ffn(l, f):
                T = 4 * l + 3 * f
                if f == 0:
                    pe.wait_ge(x_landed, 16)
                pe.wait_ge(za_ok, 3 * (3 * l + 2 * f))
                pe.wait_ge(zd_ok, 3 * l + 2 * f)
                turn(T, True)
                with pe.Fori(0, NPAIR) as i:
                    it = l * 2 * NPAIR + f * NPAIR + i
                    for s, n in (("A", l * A_ALL + f * A_FFN2 + i), ("B", l * B_ALL + f * B_FFN2 + i)):
                        b = 0 if s == "A" else 2
                        pe.wait_ge(lo_ok[s], n + 1)
                        pe.wait_ge(h32_ok[s], it if s == "A" else it * 2)
                        for c in range(NC):
                            if s == "A":
                                pe.wait_ge(x_ok, T * NC + c + 1)
                            for g in range(2):
                                ins = product(bank[b + g][:, :], [(w(s, (g * NC + c) * P, P), x(c))],
                                              start=(c == 0), stop=(c == NC - 1))
                        ins.then_inc(used[s], 1)
                    pe.wait_ge(lo_ok["D"], it + 1)
                    waits = {"A": lambda r: pe.wait_ge(h_ok["A"], it + 1) if r == 0 else None,
                             "B": lambda r: pe.wait_ge(h_ok["B"], it * 2 + r + 1)}
                    outputs(l * Y_ALL + f * Y_FFN2 + i,
                            [(lambda t, s=s: (hhi[s][:, t * P:t * P + P], hlo[s][:, t * P:t * P + P]), "D", k * D, waits[s])
                             for k, s in enumerate("AB")])

            def project(body, n):
                pe.wait_ge(lo_ok["A"], n + 1)
                for g in range(2):
                    k = 0
                    for c in range(NC):
                        (shi, slo), (mhi, mlo) = w("A", (g * NC + c) * P, P), x(c)
                        for a_, b_ in ((shi, mhi), (shi, mlo), (slo, mhi)):
                            k += 1
                            ins = t_.matmul(bank[6 + g][:, :], a_, b_, start=(k == 1), stop=(k == 3 * NC))
                            if k == 3 * NC:
                                ins.then_inc(*((used["A"], 1) if g else (q_done, 1)))
                            yield

            def heads(l, b, body_d, maps, v0, more):
                body = l * BODIES + b
                K = body * STEPS
                KD = body_d * STEPS
                pe.wait_ge(qk_ok, body * 3 + 3)
                ahead = None
                rows = HD // maps

                def scores(k):
                    hh, t = divmod(k, NT)
                    n_ = (t + 1) * P
                    for m in range(maps):
                        i = 2 * (k % 2) + m
                        km = (K if m == 0 else KD) + k
                        if k >= 2:
                            pe.wait_ge(exp_ok[m], km - 1)
                        r = hh * HD + m * rows
                        ins = product(bank[i][:, 0:n_], [((qhi[r:r + rows, t * P:t * P + P], qlo[r:r + rows, t * P:t * P + P]),
                                                          (khi[r:r + rows, 0:n_], klo[r:r + rows, 0:n_]))], stop=False)
                        t_.matmul(bank[i][:, 0:n_], sel[0:65, hh, :], brow[0:65, 0:n_], start=False, stop=False)
                        t_.matmul(bank[i][:, t * P:n_], identb[:, :], maskb[:, :], start=False, stop=True).then_inc(s_done[m], 1)

                def turn_p(k):
                    t = k % NT
                    if maps == 1:
                        pe.wait_ge(exp_ok[0], K + k + 1)
                    else:
                        pe.wait_ge(mixp_ok, KD + k + 1)
                    if k != 1:
                        pe.wait_ge(o_ok, K + max(k - 1, 0))
                    for b in range(t + 1):
                        ins = t_.transpose(bank[4 + k % 2][:, b * P:b * P + P], s32[:, 2 * (k % 2), b * P:b * P + P], ident[:, :])
                    ins.then_inc(pt_done, 1)

                def values(k):
                    hh, t = divmod(k, NT)
                    pe.wait_ge(pt_ok, K + k + 1)
                    vc = v0 + hh * HD
                    pairs = []
                    for b in range(t + 1):
                        pairs.append(((pthi[k % 2][:, b * P:b * P + P], ptlo[k % 2][:, b * P:b * P + P]),
                                      (vhi[:, b, bass.ds(vc, HD)], vlo[:, b, bass.ds(vc, HD)])))
                    product(bank[4 + k % 2][:, 0:HD], pairs).then_inc(pv_done, 1)

                for k in range(STEPS + 2):
                    if k < STEPS:
                        scores(k)
                    if more:
                        if ahead is None:
                            ahead = project(body + 1, l * A_ALL + A_QK + b + 1)
                        for _ in range(FILL // 2):
                            next(ahead, None)
                    if 1 <= k <= STEPS:
                        turn_p(k - 1)
                    if more:
                        for _ in range(FILL // 2):
                            next(ahead, None)
                    if k >= 2:
                        values(k - 2)

            pe.wait_ge(ident_ok, 2)
            with pe.Fori(0, L) as l:
                ffn(l, 0)
                pe.wait_ge(za_ok, 3 * (3 * l + 1))
                pe.wait_ge(zd_ok, 3 * l + 1)
                T = 4 * l + 1
                turn(T, True)
                with pe.Fori(0, NPROJ) as j:
                    for s, n in (("A", l * A_ALL + A_NAT + j), ("B", l * B_ALL + B_NAT + j)):
                        pe.wait_ge(lo_ok[s], n + 1)
                        pe.wait_ge(nat_free[s], l * NT * NPROJ + j * NT)
                        for t in range(NT):
                            if s == "A" and t == 0:
                                pe.wait_ge(x_ok, T * NC + NC)
                            ins = product(bank[t + (4 if s == "B" else 0)][:, 0:256],
                                          [(x(c, t * P, P), w(s, c * 256, 256)) for c in range(NC)])
                            ins.then_inc(*((nat_done[s], 1) if t < NT - 1 else (used[s], 1)))
                pe.wait_ge(nat_free["A"], l * NT * NPROJ + NT * NPROJ)
                pe.wait_ge(lf_ok, l + 1)
                for b in range(NT):
                    ins = t_.matmul(bank[0][0:FOX_H, :], lf[:, b, :], since[:, (3 - b) * P:(3 - b) * P + S],
                                    start=(b == 0), stop=(b == NT - 1))
                ins.then_inc(cum_done, 1)
                pe.wait_ge(wslo_ok, l + 1)
                pe.wait_ge(glo_ok, l + 1)
                for h in range(SGU_H):
                    o = bank[1 + h // 2][:, (h % 2) * 256:(h % 2) * 256 + 256].rearrange("p (c n) -> p c n", c=NT)
                    ins = product(o, [((wshi[:, h * P:h * P + P], wslo[:, h * P:h * P + P]),
                                       (ghi[:, :, h * HD:h * HD + HD], glo[:, :, h * HD:h * HD + HD]))])
                    if h % 2:
                        ins.then_inc(sgu_done, 1)
                pe.wait_ge(nat_free["B"], l * NT * NPROJ + NT * NPROJ)
                for _ in project(l * BODIES, l * A_ALL + A_QK):
                    pass
                pe.wait_ge(const_ok, CONSTS)
                with pe.Fori(0, FOX_P) as p:
                    pe.wait_ge(sgu_out, l * SGU_H + SGU_H)
                    pe.wait_ge(c_ok, l + 1)
                    heads(l, p, l, 1, p * 2 * HD, True)
                for p in range(DIFF_P):
                    heads(l, FOX_P + p, l * DIFF_P + p, 2, p * 2 * HD + FOX_W, p < DIFF_P - 1)
                pe.wait_ge(y_ok, l + 1)
                T = 4 * l + 2
                turn(T, False)
                for wv in range(4):
                    s = "AB"[wv % 2]
                    n = l * (A_ALL if s == "A" else B_ALL) + (A_WO if s == "A" else B_WO) + wv // 2
                    pe.wait_ge(lo_ok[s], n + 1)
                    outputs(l * Y_ALL + Y_WO + wv,
                            [(lambda t, c=2 * wv + k: x(c, t * P, P), s, k * D,
                              lambda r, c=2 * wv + k: pe.wait_ge(x_ok, T * NC + c + 1) if r == 0 else None) for k in range(2)])
                ffn(l, 1)

        @block.vector
        def _(dve):
            v = nc.vector

            def f32(ap):
                return ap.bitcast(F32)

            def split(s, n):
                dve.wait_ge(hi_ok[s], n + 1)
                v.tensor_tensor(wlo[s][:, :], raw[s][:, :], f32(whi[s][:, :]), ALU.subtract).then_inc(lo_ok[s], 1)

            def turn(T):
                for c in range(NC + 1):
                    if c < NC:
                        dve.wait_ge(x32_ok, T * NC + c + 1)
                        v.tensor_copy(xhi[:, c, :], s32[:, c % 4, :]).then_inc(xhi_ok, 1)
                    if c >= 1:
                        dve.wait_ge(xhi_ok, T * NC + c)
                        v.tensor_tensor(xlo[:, c - 1, :], s32[:, (c - 1) % 4, :], f32(xhi[:, c - 1, :]),
                                        ALU.subtract).then_inc(x_ok, 1)

            def add(y, o, scale):
                t, hf = divmod(o, 2)
                dve.wait_ge(y_done, y * 8 + o + 1)
                r = res[:, t, hf * 512:hf * 512 + 512]
                v.scalar_tensor_tensor(out=r, in0=bank[4 + o % 4][:, :], scalar=scale, in1=r,
                                       op0=ALU.mult, op1=ALU.add).then_inc(y_free, 1)

            def add_outputs(y, scale):
                dve.wait_ge(y_free, y * 8 + 4)
                for o in range(8):
                    add(y, o, scale)

            def last_outputs(l, j, y, scale):
                q = 3 * l + j
                dve.wait_ge(y_free, y * 8 + 4)
                for h in range(2):
                    for o in range(4 * h, 4 * h + 4):
                        add(y, o, scale)
                    for t in (2 * h, 2 * h + 1):
                        dve.wait_ge(y_free, y * 8 + 4 + 2 * t + 2)
                        for hf in range(2):
                            v.bn_stats(st[:, t, hf, :], res[:, t, hf * 512:hf * 512 + 512]).then_inc(st_ok, 1)
                    dve.wait_ge(st_ok, q * 8 + 4 * h + 4)
                    wait_here(6 + h)
                    for t in (2 * h, 2 * h + 1):
                        v.bn_aggr(mv[:, t, :], st[:, t, :, :].rearrange("p a n -> p (a n)")).then_inc(mv_ok, 1)
                t = NT - 1
                dve.wait_ge(rstd_ok, 2 * q + 2)
                v.tensor_scalar(nat[:, t, :], res[:, t, :], mv[:, t, 0:1], rstd[:, t:t + 1], ALU.subtract,
                                ALU.mult).then_inc(zd_ok, 1)

            def ffn(l, f):
                turn(4 * l + 3 * f)

                def pair(i):
                    it = l * 2 * NPAIR + f * NPAIR + i
                    split("B", l * B_ALL + f * B_FFN2 + i)
                    split("D", it)
                    dve.wait_ge(silu_ok["A"], it + 1)
                    dve.wait_ge(hhi_ok["A"], it)
                    v.tensor_tensor(h32["A"], silu["A"], bank[1][:, :], ALU.mult).then_inc(h32_ok["A"], 1)
                    split("A", l * A_ALL + f * A_FFN2 + i + 1)
                    dve.wait_ge(hhi_ok["A"], it + 1)
                    v.tensor_tensor(hlo["A"], h32["A"], f32(hhi["A"]), ALU.subtract).then_inc(h_ok["A"], 1)
                    for h in range(2):
                        t = slice(h * 256, h * 256 + 256)
                        dve.wait_ge(silu_ok["B"], it * 2 + h + 1)
                        v.tensor_tensor(h32["B"][:, t], silu["B"][:, t], bank[3][:, t], ALU.mult).then_inc(h32_ok["B"], 1)
                    for h in range(2):
                        t = slice(h * 256, h * 256 + 256)
                        dve.wait_ge(hhi_ok["B"], it * 2 + h + 1)
                        v.tensor_tensor(hlo["B"][:, t], h32["B"][:, t], f32(hhi["B"][:, t]), ALU.subtract).then_inc(h_ok["B"], 1)

                with dve.Fori(0, NPAIR - 1) as i:
                    pair(i)
                    dve.wait_ge(res_ok, 3 * l + 2 * f + 1)
                    add_outputs(l * Y_ALL + f * Y_FFN2 + i, 0.5)
                pair(NPAIR - 1)
                last_outputs(l, 2 * f, l * Y_ALL + f * Y_FFN2 + NPAIR - 1, 0.5)

            def wait_here(i):
                v.memset(idle[0:1, i:i + 1], 0.0)

            split("A", 0)
            for b in range(4):
                v.memset(free[0:1, b:b + 1], 0.0).then_inc(y_free, 1)
            dve.wait_ge(lam_landed, 16)
            v.tensor_tensor(lamp[:, :, :, 0, :], lamp[:, :, :, 0, :], lamp[:, :, :, 1, :], ALU.mult).then_inc(lam_step, 1)
            dve.wait_ge(lam_step, 1)
            v.tensor_reduce(lams[:, :, :], lamp[:, :, :, 0, :], AX.X, ALU.add).then_inc(lam_step, 1)
            dve.wait_ge(lame_ok, 1)
            v.tensor_tensor(nlam[:, :], lame[:, :, 1], lame[:, :, 0], ALU.subtract).then_inc(lam_step, 1)
            dve.wait_ge(lam_step, 3)
            dve.wait_ge(const_ok, CONSTS)
            v.tensor_tensor(nlam[:, :], nlam[:, :], ilam[:, :], ALU.subtract).then_inc(lam_step, 1)
            dve.wait_ge(pos_ok, 1)
            v.tensor_copy(brow[64:65, :], s32[64:65, 0, :]).then_inc(pos_ok, 1)
            dve.wait_ge(lam_step, 4)
            with dve.Fori(0, L) as l:
                ffn(l, 0)
                turn(4 * l + 1)
                dve.wait_ge(mix_landed, l * 32 + 32)
                v.tensor_copy(nlam1[:, :], nlam[:, bass.ds(l, 1)]).then_inc(nlam1_ok, 1)
                v.tensor_scalar(diff_g, diff_g, olam[:, bass.ds(l, 1)], None, ALU.mult).then_inc(dgs_ok, 1)
                split("B", l * B_ALL + B_NAT)
                split("A", l * A_ALL + A_NAT + 1)
                split("B", l * B_ALL + B_NAT + 1)
                split("A", l * A_ALL + A_NAT + 2)
                dve.wait_ge(nat_free["B"], l * NT * NPROJ + NT)
                dve.wait_ge(nat_free["A"], l * NT * NPROJ + 2 * NT)
                for t in range(NT):
                    v.bn_stats(gst[:, t, :], nat[:, t, 0:SGU_W]).then_inc(gst_ok, 1)
                dve.wait_ge(gst_ok, l * NT + NT)
                wait_here(4)
                for t in range(NT):
                    v.bn_aggr(gmv[:, t, :], gst[:, t, :]).then_inc(gmv_ok, 1)
                dve.wait_ge(wshi_ok, l + 1)
                v.tensor_tensor(wslo, wsr, f32(wshi), ALU.subtract).then_inc(wslo_ok, 1)

                def values(k):
                    s = "AB"[k % 2]
                    lo, n = ((0, 256), (256, FOX_W - 256), (FOX_W, DIFF_W))[k - 3]
                    for t in range(NT):
                        src = bank[t + (4 if s == "B" else 0)]
                        dve.wait_ge(vhi_ok, l * 3 * NT + (k - 3) * NT + t + 1)
                        if k == 4:
                            v.tensor_tensor(flog[:, t, :], src[:, F_AT:F_AT + FOX_H], f_bias, ALU.add).then_inc(f_ok, 1)
                        v.tensor_tensor(vlo[:, t, lo:lo + n], src[:, 0:n], f32(vhi[:, t, lo:lo + n]),
                                        ALU.subtract).then_inc(nat_free[s], 1)

                values(3)
                split("B", l * B_ALL + B_NAT + 2)
                dve.wait_ge(grs_ok, l + 1)
                for t in range(NT):
                    v.tensor_scalar(nat[:, t, 0:SGU_W], nat[:, t, 0:SGU_W], gmv[:, t, 0:1], grs[:, t:t + 1],
                                    ALU.subtract, ALU.mult).then_inc(gn_ok, 1)
                for t in range(NT):
                    dve.wait_ge(gn_ok, l * NT + t + 1)
                    v.tensor_tensor(nat[:, t, 0:SGU_W], nat[:, t, 0:SGU_W], sgu_g, ALU.mult).then_inc(gg_ok, 1)
                for t in range(NT):
                    dve.wait_ge(gg_ok, l * NT + t + 1)
                    v.tensor_tensor(nat[:, t, 0:SGU_W], nat[:, t, 0:SGU_W], sgu_b, ALU.add).then_inc(gb_ok, 1)
                values(4)
                dve.wait_ge(f_ok, l * NT + NT)
                v.scalar_tensor_tensor(out=fneg[:, :, :], in0=flog[:, :, :], scalar=-1.0, in1=flog[:, :, :],
                                       op0=ALU.mult, op1=ALU.min).then_inc(fneg_ok, 1)
                dve.wait_ge(fln_ok, l + 1)
                v.scalar_tensor_tensor(out=lf[:, :, :], in0=flog[:, :, :], scalar=0.0, in1=fln[:, :, :],
                                       op0=ALU.min, op1=ALU.subtract).then_inc(lf_ok, 1)
                dve.wait_ge(ghi_ok, l + 1)
                v.tensor_tensor(glo, nat[:, :, 0:SGU_W], f32(ghi), ALU.subtract).then_inc(glo_ok, 1)
                split("A", l * A_ALL + A_QK)
                values(5)
                dve.wait_ge(chi_ok, l + 1)
                v.tensor_tensor(brow[32:32 + FOX_H, :], bank[0][0:FOX_H, :], f32(brow[0:FOX_H, :]),
                                ALU.subtract).then_inc(c_ok, 1)
                for h in range(SGU_H):
                    if h % 2 == 0:
                        dve.wait_ge(sgu_done, l * (SGU_H // 2) + h // 2 + 1)
                    o = bank[1 + h // 2][:, (h % 2) * 256:(h % 2) * 256 + 256].rearrange("p (c n) -> p c n", c=NT)
                    u = nat[:, :, Y_SGU + h * HD:Y_SGU + h * HD + HD]
                    v.scalar_tensor_tensor(out=u, in0=o, scalar=mixc[:, h:h + 1], in1=u, op0=ALU.add,
                                           op1=ALU.mult).then_inc(sgu_out, 1)

                def project(body, b):
                    v.tensor_copy(sel[0:65, :, :], selall[0:65, bass.ds(b * 2, 2)].broadcast_to([65, 2, P])).then_inc(qk_ok, 1)
                    dve.wait_ge(qhi_ok, body + 1)
                    v.scalar_tensor_tensor(out=qlo, in0=bank[6][:, :], scalar=qscale[:, bass.ds(b, 1)], in1=f32(qhi),
                                           op0=ALU.mult, op1=ALU.subtract).then_inc(qk_ok, 1)
                    dve.wait_ge(khi_ok, body + 1)
                    v.tensor_tensor(klo, bank[7][:, :], f32(khi), ALU.subtract).then_inc(qk_ok, 1)

                def heads(b, body_d, maps, y0, more):
                    body = l * BODIES + b
                    K = body * STEPS
                    KD = body_d * STEPS
                    for k in range(STEPS + 2):
                        if k < STEPS:
                            w_ = (k % NT + 1) * P
                            for m in range(maps):
                                i = 2 * (k % 2) + m
                                dve.wait_ge(s_done[m], (K if m == 0 else KD) + k + 1)
                                v.tensor_reduce(negm[:, i:i + 1], bank[i][:, 0:w_], AX.X, ALU.max,
                                                negate=True).then_inc(max_ok[m], 1)
                        if 1 <= k <= STEPS:
                            j = k - 1
                            w_ = (j % NT + 1) * P
                            if maps == 1:
                                dve.wait_ge(exp_ok[0], K + j + 1)
                                i = 2 * (j % 2)
                                v.reciprocal(rinv[:, j, 0:1], rsum[:, i:i + 1]).then_inc(rinv_ok, 1)
                        if maps == 2 and k < STEPS:
                            i = 2 * (k % 2)
                            dve.wait_ge(exp_ok[0], K + k + 1)
                            dve.wait_ge(exp_ok[1], KD + k + 1)
                            v.reciprocal(rinv[:, k, :], rsum[:, i:i + 2]).then_inc(rinv_ok, 1)
                            dve.wait_ge(rinv_ok, K + k + 1)
                            v.scalar_tensor_tensor(out=wlam[:, k:k + 1], in0=rinv[:, k, 1:2], scalar=rsum[:, i:i + 1],
                                                   in1=nlam1[:, :], op0=ALU.mult, op1=ALU.mult).then_inc(wlam_ok, 1)
                            dve.wait_ge(wlam_ok, KD + k + 1)
                            w_ = (k % NT + 1) * P
                            v.scalar_tensor_tensor(out=s32[:, i, 0:w_], in0=s32[:, i + 1, 0:w_], scalar=wlam[:, k:k + 1],
                                                   in1=s32[:, i, 0:w_], op0=ALU.mult, op1=ALU.add).then_inc(mixp_ok, 1)
                        if 1 <= k <= STEPS:
                            j = k - 1
                            w_ = (j % NT + 1) * P
                            dve.wait_ge(pthi_ok, K + j + 1)
                            v.tensor_tensor(ptlo[j % 2][:, 0:w_], bank[4 + j % 2][:, 0:w_], f32(pthi[j % 2][:, 0:w_]),
                                            ALU.subtract).then_inc(pt_ok, 1)
                        if k >= 2:
                            j = k - 2
                            hh, t = divmod(j, NT)
                            dve.wait_ge(pv_done, K + j + 1)
                            o = nat[:, t, bass.ds(y0 + hh * HD, HD)]
                            dve.wait_ge(rinv_ok, K + j + 1)
                            v.tensor_scalar(o, bank[4 + j % 2][:, 0:HD], rinv[:, j, 0:1], None, ALU.mult).then_inc(o_ok, 1)
                        if k == STEPS - 1 and more:
                            project(body + 1, b + 1)
                        if k == STEPS and more:
                            split("A", l * A_ALL + A_QK + b + 2)

                project(l * BODIES, 0)
                split("A", l * A_ALL + A_QK + 1)
                dve.wait_ge(nlam1_ok, l + 1)
                wait_here(5)
                with dve.Fori(0, FOX_P) as p:
                    heads(p, l, 1, p * 2 * HD, True)
                for p in range(DIFF_P):
                    heads(FOX_P + p, l * DIFF_P + p, 2, p * 2 * HD + Y_DIFF, p < DIFF_P - 1)
                split("B", l * B_ALL + B_WO)
                yd = nat[:, :, Y_DIFF:Y_DIFF + DIFF_W]
                dve.wait_ge(o_ok, (l * BODIES + BODIES) * STEPS)
                for t in range(NT):
                    v.scalar_tensor_tensor(out=sq[:, t, :], in0=yd[:, t, :], scalar=1.0 / HD, in1=yd[:, t, :],
                                           op0=ALU.mult, op1=ALU.mult).then_inc(sq_ok, 1)
                dve.wait_ge(sq_ok, l * NT + NT)
                v.tensor_reduce(dms[:, :], sq.rearrange("p t (h n) -> p (t h) n", n=HD), AX.X, ALU.add).then_inc(dms_ok, 1)
                dve.wait_ge(drs_ok, l + 1)
                for t in range(NT):
                    yt = yd[:, t, :].rearrange("p (h n) -> p h n", n=HD)
                    v.tensor_tensor(yt, yt, drs[:, t * DIFF_H:t * DIFF_H + DIFF_H].broadcast_to([P, DIFF_H, HD]),
                                    ALU.mult).then_inc(dn_ok, 1)
                dve.wait_ge(dgs_ok, l + 1)
                for t in range(NT):
                    dve.wait_ge(dn_ok, l * NT + t + 1)
                    ins = v.tensor_tensor(yd[:, t, :], yd[:, t, :], diff_g, ALU.mult)
                    if t == NT - 1:
                        ins.then_inc(y_ok, 1)
                turn(4 * l + 2)
                dve.wait_ge(res_ok, 3 * l + 2)
                for w_ in range(4):
                    y = l * Y_ALL + Y_WO + w_
                    if w_ < 3:
                        add_outputs(y, 1.0)
                    if w_ % 2 == 0:
                        split("A", l * A_ALL + A_WO + w_ // 2 + 1)
                    elif w_ == 1:
                        split("B", l * B_ALL + B_WO + 1)
                    else:
                        last_outputs(l, 1, y, 1.0)
                ffn(l, 1)
            dve.wait_ge(gb_landed, 32 * 3 * L + 32)
            dve.wait_ge(za_ok, 3 * 3 * L)
            dve.wait_ge(zd_ok, 3 * L)
            for t in range(NT):
                v.tensor_tensor(nat[:, t, :], nat[:, t, :], gbr[:, 0, :], ALU.mult).then_inc(fin_step, 1)
            for t in range(NT):
                dve.wait_ge(fin_step, t + 1)
                v.tensor_tensor(nat[:, t, :], nat[:, t, :], gbr[:, 1, :], ALU.add).then_inc(fin_ok, 1)


CONSTS = 9 + 2 * L + BODIES + 1 + 2 + 2 + DIFF_H


def lay_out(i):
    def cols(w, n, width):
        return w.reshape(NC, P, n, width).transpose(2, 1, 0, 3)

    def ffn(l, k):
        g, u = (cols(i[f"ffn_{k}_w_{x}"][l], 2 * NPAIR, P) for x in ("gate", "up"))
        gu = np.stack([g, u], 2).reshape(NPAIR, 2, P, SLOT)
        d = i[f"ffn_{k}_w_down"][l].reshape(NPAIR, 2, P, D).transpose(0, 2, 1, 3).reshape(NPAIR, P, SLOT)
        return gu[:, 0], gu[:, 1], d

    A, B, Dn = [], [], []
    for l in range(L):
        w = i["w_in"][l]
        a, b, d = ffn(l, "a")
        natp = np.stack([w[:, c:c + 256].reshape(NC, P, 256).transpose(1, 0, 2).reshape(P, SLOT) for c in NAT_COLS])

        def qk(q, k, n):
            return np.stack([cols(w[:, q:q + n * P], n, P), cols(w[:, k:k + n * P], n, P)], 2).reshape(n, P, SLOT)

        wo = i["w_out"][l].reshape(4, 2, P, D).transpose(0, 2, 1, 3).reshape(4, P, SLOT)
        a2, b2, d2 = ffn(l, "b")
        A += [a, natp[0::2], qk(C_FQ, C_FK, FOX_P), qk(C_DQ, C_DK, DIFF_P), wo[0::2], a2]
        B += [b, natp[1::2], wo[1::2], b2]
        Dn += [d, d2]
    A, B, Dn = np.concatenate(A + [A[0][0:1]]), np.concatenate(B), np.concatenate(Dn)
    one, zero = np.ones((1, D), np.float32), np.zeros((1, D), np.float32)
    g = np.stack([i["norm_a_g"], i["norm_m_g"], i["norm_b_g"]], 1).reshape(3 * L, D)
    b = np.stack([i["norm_a_b"], i["norm_m_b"], i["norm_b_b"]], 1).reshape(3 * L, D)
    gb = np.stack([np.concatenate([one, g]), np.concatenate([zero, b])], 1)
    return {
        "x": i["x"].reshape(NT, P, D).transpose(1, 0, 2),
        "a_w": A, "b_w": B, "d_w": Dn,
        "gb_row": gb,
        "gb_col": gb.reshape(-1, 2, NC, P).transpose(0, 3, 1, 2),
        "mix_row": np.concatenate([i["diff_norm_g"], i["sgu_norm_g"], i["sgu_norm_b"], i["fox_f_bias"]], 1),
        "mix_col": i["sgu_b_s"].transpose(0, 2, 1),
        "ws": i["sgu_w_s"].transpose(0, 3, 1, 2).reshape(L, P, SGU_H * P),
        "lamv": np.stack([np.stack([i["diff_lambda_q1"], i["diff_lambda_k1"]], 1),
                          np.stack([i["diff_lambda_q2"], i["diff_lambda_k2"]], 1)], 1)[None],
    }


def kernel(**inputs):
    import concourse.bacc as bacc
    from concourse.bass_utils import run_bass_kernel_spmd

    nc = bacc.Bacc("TRN2", target_bir_lowering=False, num_devices=1)
    arrays, args = {}, []
    for name, a in lay_out({k: np.asarray(v) for k, v in inputs.items()}).items():
        a = np.ascontiguousarray(a)
        arrays[f"in_{name}"] = a
        args.append(nc.dram_tensor(f"in_{name}", a.shape, mybir.dt.from_np(a.dtype), kind="ExternalInput").ap())
    args.append(nc.dram_tensor("out", (P, NT, D), F32, kind="ExternalOutput").ap())
    build(nc, *args)
    r = run_bass_kernel_spmd(nc, [arrays], core_ids=[0])
    y = r.results[0]["out"]
    return np.ascontiguousarray(y.reshape(P, NT, D).transpose(1, 0, 2)).reshape(1, S, D)
```

```python
from contextlib import ExitStack
import math

import numpy as np
import concourse.bass as bass
from concourse import mybir

ALU = mybir.AluOpType
ACT = mybir.ActivationFunctionType
F32 = mybir.dt.float32
F32R = mybir.dt.float32r
BF16 = mybir.dt.bfloat16
AX = mybir.AxisListType

P = 128
L = 2
D = 1024
S = 512
F = 2816
NT = S // P
NC = D // P
NPAIR = F // P // 2
HD = 64
FOX_H, DIFF_H, SGU_H = 6, 4, 6
FOX_W, DIFF_W, SGU_W = FOX_H * HD, DIFF_H * HD, SGU_H * HD
FOX_P, DIFF_P = FOX_H // 2, DIFF_H // 2
ALPHA = (2 * L) ** 0.25
EPS = 1e-5
NEG = -1e30
SLOPES = [2.0 ** (-8.0 * (h + 1) / DIFF_H) for h in range(DIFF_H)]
LAM_INIT = [0.8 - 0.6 * math.exp(-0.3 * l) for l in range(L)]

C_FQ, C_FK, C_FV, C_FF = 0, FOX_W, 2 * FOX_W, 3 * FOX_W
C_DQ = C_FF + FOX_H
C_DK, C_DV, C_Z = C_DQ + DIFF_W, C_DQ + 2 * DIFF_W, C_DQ + 3 * DIFF_W
NAT_COLS = [C_Z, C_Z + 256, C_Z + 512, C_FV, C_FV + 256, C_DV]
NPROJ = len(NAT_COLS) // 2
F_AT = C_FF - NAT_COLS[4]

SLOT = 2 * D

BODIES = FOX_P + DIFF_P
A_FFN, A_NAT, A_QK, A_WO, A_FFN2, A_ALL = (int(x) for x in np.cumsum([0, NPAIR, NPROJ, BODIES, 2, NPAIR]))
B_FFN, B_NAT, B_WO, B_FFN2, B_ALL = (int(x) for x in np.cumsum([0, NPAIR, NPROJ, 1, NPAIR]))
D_FFN, D_WO, D_FFN2, D_ALL = (int(x) for x in np.cumsum([0, NPAIR, 1, NPAIR]))
AU_FFN2, AU_ALL = A_WO, A_ALL - 2
BU_FFN2, BU_ALL = B_WO, B_ALL - 1
Y_WO, Y_FFN2, Y_ALL = NPAIR, NPAIR + 1, 2 * NPAIR + 1
STEPS = 2 * NT
FILL = (4, 3)
EARLY = [(0, "A", 0), (1, "A", D), (2, "B", 0), (5, "B", D), (6, "D", 0), (7, "D", D)]
LATE = [3, 4]
AMONG = 5


def build(nc, x_in, a_w, b_w, d_w, gb_row, gb_col, mix_row, mix_col, ws_in, lamv, out):
    ctx = ExitStack()
    with ctx:
        def sb(name, shape, dt=F32):
            return ctx.enter_context(nc.sbuf_tensor(name, shape, dt))

        def sem(name):
            return ctx.enter_context(nc.semaphore(name))

        bank = [ctx.enter_context(nc.psum_tensor(f"bank{i}", [P, 512], F32)) for i in range(8)]

        raw = {s: sb(f"raw{s}", [P, SLOT]) for s in "ABD"}
        whi = {s: sb(f"whi{s}", [P, SLOT], F32R) for s in "ABD"}
        wlo = {s: sb(f"wlo{s}", [P, SLOT], F32R) for s in "ABD"}
        xhi = sb("xhi", [P, NC, S], F32R)
        xlo = sb("xlo", [P, NC, S], F32R)
        res = sb("res", [P, NT, D])
        nat = sb("nat", [P, NT, D])
        s32 = sb("s32", [P, 4, 512])
        hl = sb("hl", [P, 9, 512], F32R)
        vhi = sb("vhi", [P, NT, FOX_W + DIFF_W], F32R)
        vlo = sb("vlo", [P, NT, FOX_W + DIFF_W], F32R)
        gbr = sb("gbr", [P, 2, D])
        gbc = sb("gbc", [P, 2, NC])
        mixr = sb("mixr", [P, DIFF_W + 2 * SGU_W + FOX_H])
        mixc = sb("mixc", [P, SGU_H])
        ident = sb("ident", [P, P])
        identb = sb("identb", [P, P], BF16)
        maskb = sb("maskb", [P, P], BF16)
        since = sb("since", [P, 7 * P])
        selall = sb("selall", [P, FOX_H + DIFF_H])
        alpha = sb("alpha", [P, 1])
        idle = sb("idle", [P, 8])
        free = sb("free", [P, 8])
        eps = sb("eps", [P, 1])
        qscale = sb("qscale", [P, BODIES])
        half = sb("half", [P, 4 * DIFF_H])
        brow = sb("brow", [P, S], F32R)
        sel = sb("sel", [P, 2, P], F32R)
        st = sb("st", [P, NT, 2, 6])
        mv = sb("mv", [P, NT, 2])
        ve = sb("ve", [P, NT])
        rstd = sb("rstd", [P, NT])
        nmr0 = sb("nmr0", [P, NT])
        mone = sb("mone", [P, 1])
        nmr = sb("nmr", [P, NT])
        gst = sb("gst", [P, NT, 6])
        gmv = sb("gmv", [P, NT, 2])
        gve = sb("gve", [P, NT])
        grs = sb("grs", [P, NT])
        flog = sb("flog", [P, NT, FOX_H])
        fneg = sb("fneg", [P, NT, FOX_H])
        fexp = sb("fexp", [P, NT, FOX_H])
        fln = sb("fln", [P, NT, FOX_H])
        lf = sb("lf", [P, NT, FOX_H])
        negm = sb("negm", [P, 4])
        rsum = sb("rsum", [P, 4])
        rinv = sb("rinv", [P, STEPS, 2])
        wlam = sb("wlam", [P, STEPS])
        lamp = sb("lamp", [P, L, 2, 2, 32])
        lams = sb("lams", [P, L, 2])
        lame = sb("lame", [P, L, 2])
        nlam = sb("nlam", [P, L])
        olam = sb("olam", [P, L])
        ilam = sb("ilam", [P, L])
        nlam1 = sb("nlam1", [P, 1])
        sq = sb("sq", [P, NT, 2 * HD])
        dms = sb("dms", [P, NT * DIFF_H])
        dve_ = sb("dve_", [P, NT * DIFF_H])
        drs = sb("drs", [P, NT * DIFF_H])

        landed = {s: sem(f"landed_{s}") for s in "ABD"}
        hi_ok = {s: sem(f"hi_ok_{s}") for s in "ABD"}
        lo_ok = {s: sem(f"lo_ok_{s}") for s in "ABD"}
        used = {s: sem(f"used_{s}") for s in "AB"}
        x_landed = sem("x_landed")
        gbr_landed = sem("gbr_landed")
        gbc_landed = sem("gbc_landed")
        mix_landed = sem("mix_landed")
        ws_landed = sem("ws_landed")
        lam_landed = sem("lam_landed")
        const_ok = sem("const_ok")
        pos_ok = sem("pos_ok")
        za_ok = sem("za_ok")
        zd_ok = sem("zd_ok")
        ident_ok = sem("ident_ok")
        res_ok = sem("res_ok")
        rs_step = sem("rs_step")
        turned = sem("turned")
        x32_ok = sem("x32_ok")
        xhi_ok = sem("xhi_ok")
        x_ok = sem("x_ok")
        silu_ok = {s: sem(f"silu_ok_{s}") for s in "AB"}
        h32_ok = {s: sem(f"h32_ok_{s}") for s in "AB"}
        hhi_ok = {s: sem(f"hhi_ok_{s}") for s in "AB"}
        h_ok = {s: sem(f"h_ok_{s}") for s in "AB"}
        y_done = sem("y_done")
        y_free = sem("y_free")
        st_ok = sem("st_ok")
        mv_ok = sem("mv_ok")
        ve_ok = sem("ve_ok")
        rstd_ok = sem("rstd_ok")
        nmr_step = sem("nmr_step")
        nmr_ok = sem("nmr_ok")
        vhi_ok = sem("vhi_ok")
        nat_free = {s: sem(f"nat_free_{s}") for s in "AB"}
        f_ok = sem("f_ok")
        fneg_ok = sem("fneg_ok")
        fexp_ok = sem("fexp_ok")
        fln_ok = sem("fln_ok")
        lf_ok = sem("lf_ok")
        cum_done = sem("cum_done")
        chi_ok = sem("chi_ok")
        c_ok = sem("c_ok")
        ws_tri = sem("ws_tri")
        wshi_ok = sem("wshi_ok")
        wslo_ok = sem("wslo_ok")
        gst_ok = sem("gst_ok")
        gmv_ok = sem("gmv_ok")
        gve_ok = sem("gve_ok")
        grs_ok = sem("grs_ok")
        gn_ok = sem("gn_ok")
        gg_ok = sem("gg_ok")
        gb_ok = sem("gb_ok")
        ghi_ok = sem("ghi_ok")
        glo_ok = sem("glo_ok")
        sgu_done = sem("sgu_done")
        sgu_out = sem("sgu_out")
        q_done = sem("q_done")
        qhi_ok = sem("qhi_ok")
        khi_ok = sem("khi_ok")
        qk_ok = sem("qk_ok")
        qw_hi_ok = sem("qw_hi_ok")
        qw_ok = sem("qw_ok")
        yt_done = sem("yt_done")
        ythi_ok = sem("ythi_ok")
        yt_ok = sem("yt_ok")
        wo_done = sem("wo_done")
        wo_free = sem("wo_free")
        wo_a_done = sem("wo_a_done")
        s_done = [sem(f"s_done{m}") for m in range(2)]
        max_ok = [sem(f"max_ok{m}") for m in range(2)]
        exp_ok = [sem(f"exp_ok{m}") for m in range(2)]
        rinv_ok = sem("rinv_ok")
        wlam_ok = sem("wlam_ok")
        mixp_ok = sem("mixp_ok")
        pt_done = sem("pt_done")
        pthi_ok = sem("pthi_ok")
        pt_ok = sem("pt_ok")
        pv_done = sem("pv_done")
        o_ok = sem("o_ok")
        sq_ok = sem("sq_ok")
        dms_ok = sem("dms_ok")
        dve_ok = sem("dve_ok")
        drs_ok = sem("drs_ok")
        dn_ok = sem("dn_ok")
        dgs_ok = sem("dgs_ok")
        y_ok = sem("y_ok")
        lam_step = sem("lam_step")
        lame_ok = sem("lame_ok")
        ilam_ok = sem("ilam_ok")
        nlam1_ok = sem("nlam1_ok")
        fin_step = sem("fin_step")
        fin_ok = sem("fin_ok")
        out_done = sem("out_done")

        wsr = s32[:, 0:2, :].rearrange("p a n -> p (a n)")[:, 0:SGU_H * P]
        hlf = hl[:, :, :].rearrange("p a n -> p (a n)")
        ghi = hlf[:, 0:NT * SGU_W].rearrange("p (t n) -> p t n", t=NT)
        glo = hlf[:, NT * SGU_W:2 * NT * SGU_W].rearrange("p (t n) -> p t n", t=NT)
        wshi = hlf[:, 2 * NT * SGU_W:2 * NT * SGU_W + SGU_H * P]
        wslo = hlf[:, 2 * NT * SGU_W + SGU_H * P:2 * NT * SGU_W + 2 * SGU_H * P]
        silu = {"A": s32[:, 0, :], "B": s32[:, 1, :]}
        h32 = {"A": s32[:, 2, :], "B": s32[:, 3, :]}
        hhi = {"A": hl[:, 0, :], "B": hl[:, 2, :]}
        hlo = {"A": hl[:, 1, :], "B": hl[:, 3, :]}
        qhi, qlo, khi, klo = (hl[:, i, :] for i in range(4))
        pthi = [hl[:, 4, :], hl[:, 5, :]]
        ptlo = [hl[:, 6, :], hl[:, 7, :]]
        diff_g = mixr[:, 0:DIFF_W]
        sgu_g = mixr[:, DIFF_W:DIFF_W + SGU_W]
        sgu_b = mixr[:, DIFF_W + SGU_W:DIFF_W + 2 * SGU_W]
        f_bias = mixr[:, DIFF_W + 2 * SGU_W:]
        Y_DIFF, Y_SGU = FOX_W, FOX_W + DIFF_W
        block = ctx.enter_context(nc.Block())

        @block.sync
        def _(sp):
            w_in_dram = {"A": a_w, "B": b_w, "D": d_w}

            def fill(s, n):
                if isinstance(n, int) and n == 0:
                    sp.dma_start(raw[s][:, :], w_in_dram[s][0, :, :]).then_inc(landed[s], 16)
                    return
                sp.wait_ge(lo_ok[s], n)
                sp.dma_start(raw[s][:, :], w_in_dram[s][bass.ds(n, 1), :, :].rearrange("a p n -> (a p) n")).then_inc(landed[s], 16)

            def norm_params(q):
                sp.dma_start(gbc[:, :, :], gb_col[bass.ds(q, 1), :, :, :].rearrange("a p g c -> (a p) g c")).then_inc(gbc_landed, 16)
                sp.dma_start(gbr[:, :, :], gb_row[bass.ds(q, 1), :, :].broadcast_to([P, 2, D])).then_inc(gbr_landed, 16)

            def ffn(l, f):
                a0 = l * A_ALL + (A_FFN2 if f else A_FFN)
                b0 = l * B_ALL + (B_FFN2 if f else B_FFN)
                with sp.Fori(0, NPAIR - 1) as i:
                    fill("A", a0 + i + 1)
                    fill("B", b0 + i + 1)
                    fill("D", l * D_ALL + f * D_FFN2 + i + 1)
                fill("A", a0 + NPAIR)
                q = 3 * l + 2 * f
                sp.wait_ge(x32_ok, (q + 1) * NC)
                sp.wait_ge(res_ok, q + 1)
                norm_params(q + 1)

            sp.dma_start(lamp[:, :, :, :, :], lamv.broadcast_to([P, L, 2, 2, 32])).then_inc(lam_landed, 16)
            fill("A", 0)
            sp.dma_start(nat[:, :, :], x_in).then_inc(x_landed, 16)
            norm_params(0)
            with sp.Fori(0, L) as l:
                fill("B", l * B_ALL)
                fill("D", l * D_ALL)
                sp.wait_ge(y_ok, l)
                sp.dma_start(mixr[:, :], mix_row[bass.ds(l, 1), :].broadcast_to([P, mix_row.shape[1]])).then_inc(mix_landed, 16)
                sp.dma_start(mixc[:, :], mix_col[bass.ds(l, 1), :, :].rearrange("a p n -> (a p) n")).then_inc(mix_landed, 16)
                ffn(l, 0)
                fill("B", l * B_ALL + B_NAT)
                fill("D", l * D_ALL + D_WO)
                sp.wait_ge(x_ok, (3 * l + 2) * NC)
                sp.dma_start(wsr, ws_in[bass.ds(l, 1), :, :].rearrange("a p n -> (a p) n")).then_inc(ws_landed, 16)
                for j in range(NPROJ):
                    fill("A", l * A_ALL + A_NAT + j + 1)
                    fill("B", l * B_ALL + B_NAT + j + 1)
                sp.wait_ge(res_ok, 3 * l + 2)
                sp.wait_ge(x32_ok, (3 * l + 2) * NC)
                norm_params(3 * l + 2)
                fill("B", l * B_ALL + B_FFN2)
                fill("D", l * D_ALL + D_FFN2)
                for p in range(BODIES):
                    fill("A", l * A_ALL + A_QK + p + 1)
                fill("A", l * A_ALL + A_WO + 1)
                fill("A", l * A_ALL + A_FFN2)
                ffn(l, 1)
            for t in range(NT):
                sp.wait_ge(fin_ok, t + 1)
                sp.dma_start(out[:, t, :], nat[:, t, :]).then_inc(out_done, 16)
            sp.wait_ge(out_done, 16 * NT)

        @block.gpsimd
        def _(pool):
            g = nc.gpsimd
            n = 0

            def done(ins):
                nonlocal n
                n += 1
                ins.then_inc(const_ok, 1)

            g.memset(ident[:, :], 0.0).then_inc(ident_ok, 1)
            pool.wait_ge(ident_ok, 1)
            g.affine_select(out=ident[:, :], in_=ident[:, :], compare_op=ALU.not_equal, fill=1.0, base=0,
                            pattern=[[-1, P]], channel_multiplier=1).then_inc(ident_ok, 1)
            done(g.memset(identb[:, :], 0.0))
            done(g.memset(maskb[:, :], 0.0))
            done(g.memset(since[:, :], 1.0))
            done(g.memset(selall[:, :], 0.0))
            done(g.memset(half[:, :], -0.5))
            done(g.memset(alpha[:, :], ALPHA))
            done(g.memset(eps[:, :], EPS))
            done(g.memset(mone[:, :], -1.0))
            done(g.memset(brow[:, :].bitcast(F32), 0.0))
            for l in range(L):
                done(g.memset(olam[:, l:l + 1], 1.0 - LAM_INIT[l]))
                done(g.memset(ilam[:, l:l + 1], LAM_INIT[l]))
            for p in range(BODIES):
                done(g.memset(qscale[:, p:p + 1], HD ** -0.5 if p < FOX_P else (HD // 2) ** -0.5))
            pool.wait_ge(const_ok, n)
            done(g.affine_select(out=identb[:, :], in_=identb[:, :], compare_op=ALU.not_equal, fill=1.0, base=0,
                                 pattern=[[-1, P]], channel_multiplier=1))
            done(g.affine_select(out=maskb[:, :], in_=maskb[:, :], compare_op=ALU.is_ge, fill=NEG, base=0,
                                 pattern=[[-1, P]], channel_multiplier=1))
            done(g.affine_select(out=since[:, :], in_=since[:, :], compare_op=ALU.is_ge, fill=0.0, base=-3 * P,
                                 pattern=[[1, 7 * P]], channel_multiplier=-1))
            for r in (0, 32):
                pool.wait_ge(const_ok, n)
                v = selall[r:r + 32, 0:FOX_H]
                done(g.affine_select(out=v, in_=v, compare_op=ALU.not_equal, fill=-1.0, base=0,
                                     pattern=[[-1, FOX_H]], channel_multiplier=1))
            pool.wait_ge(const_ok, n)
            for h in range(DIFF_H):
                done(g.memset(selall[64:65, FOX_H + h:FOX_H + h + 1], SLOPES[h]))
            g.iota(s32[64:65, 0, :], pattern=[[1, S]], base=0, channel_multiplier=0,
                   allow_small_or_imprecise_dtypes=True).then_inc(pos_ok, 1)
            assert n == CONSTS
            pool.wait_ge(pos_ok, 1)

            def wait_here():
                g.tensor_tensor(idle[:, 1:2], eps[:, :], eps[:, :], ALU.add)

            def residual(l, j):
                q = 3 * l + j
                pool.wait_ge(gbr_landed, 16 * q + 16)
                s0 = q * 10
                for w in range(2):
                    g.tensor_tensor(gbr[:, w, :], gbr[:, w, :], alpha[:, :].broadcast_to([P, D]), ALU.mult).then_inc(rs_step, 1)
                pool.wait_ge(rs_step, s0 + 2)
                pool.wait_ge(za_ok, 3 * q + 3)
                pool.wait_ge(zd_ok, q + 1)
                for t in range(NT):
                    g.tensor_tensor(res[:, t, :], nat[:, t, :], gbr[:, 0, :], ALU.mult).then_inc(rs_step, 1)
                for t in range(NT):
                    pool.wait_ge(rs_step, s0 + 3 + t)
                    ins = g.tensor_tensor(res[:, t, :], res[:, t, :], gbr[:, 1, :], ALU.add)
                    ins.then_inc(*((rs_step, 1) if t < NT - 1 else (res_ok, 1)))
                g.memset(idle[:, 2:3], 0.0).then_inc(rs_step, 1)

            def root(v, out_, in_, step, k, ready, n_):
                g.tensor_tensor(v, in_, eps[:, :].broadcast_to([P, n_]), ALU.add).then_inc(step, 1)
                pool.wait_ge(step, k)
                g.tensor_tensor(out_, v, half[:, 0:n_], ALU.pow).then_inc(ready, 1)

            def norm(l, j):
                q = 3 * l + j
                for h in range(2):
                    t = slice(2 * h, 2 * h + 2)
                    pool.wait_ge(mv_ok, NT * q + 2 * h + 2)
                    root(ve[:, t], rstd[:, t], mv[:, t, 1], ve_ok, 2 * q + h + 1, rstd_ok, 2)
                    pool.wait_ge(rstd_ok, 2 * q + h + 1)
                    g.tensor_tensor(nmr0[:, t], mv[:, t, 0], rstd[:, t], ALU.mult).then_inc(nmr_step, 1)
                    pool.wait_ge(nmr_step, 2 * q + h + 1)
                    g.tensor_tensor(nmr[:, t], nmr0[:, t], mone[:, :].broadcast_to([P, 2]), ALU.mult).then_inc(nmr_ok, 1)

            pool.wait_ge(x_landed, 16)
            wait_here()
            with pool.Fori(0, L) as l:
                residual(l, 0)
                norm(l, 0)
                residual(l, 1)
                pool.wait_ge(ws_landed, 16 * l + 16)
                wait_here()
                g.affine_select(out=wsr, in_=wsr, compare_op=ALU.is_ge, fill=0.0, base=0,
                                pattern=[[0, SGU_H], [1, P]], channel_multiplier=-1).then_inc(ws_tri, 1)
                pool.wait_ge(gmv_ok, NT * l + NT)
                root(gve[:, :], grs[:, :], gmv[:, :, 1], gve_ok, l + 1, grs_ok, NT)
                for p in range(DIFF_P):
                    c = slice(p * STEPS, p * STEPS + STEPS)
                    pool.wait_ge(dms_ok, l * DIFF_P + p + 1)
                    root(dve_[:, c], drs[:, c], dms[:, c], dve_ok, l * DIFF_P + p + 1, drs_ok, STEPS)
                norm(l, 1)
                residual(l, 2)
                norm(l, 2)

        @block.scalar
        def _(act):
            a = nc.scalar

            def split(s, n):
                act.wait_ge(landed[s], n * 16 + 16)
                a.activation(whi[s][:, :], raw[s][:, :], ACT.Copy).then_inc(hi_ok[s], 1)

            def split_half(n, h, step):
                if h == 0:
                    act.wait_ge(landed["A"], n * 16 + 16)
                t = slice(h * D, h * D + D)
                a.activation(whi["A"][:, t], raw["A"][:, t], ACT.Copy).then_inc(step, 1)

            def turn_z(q):
                act.wait_ge(gbc_landed, 16 * q + 16)
                for c in range(NC):
                    act.wait_ge(turned, q * NC + c + 1)
                    if c >= 4:
                        act.wait_ge(x_ok, q * NC + c - 3)
                    a.activation(s32[:, c % 4, :], bank[c][:, :], ACT.Identity, bias=gbc[:, 1, c:c + 1],
                                 scale=gbc[:, 0, c:c + 1]).then_inc(x32_ok, 1)

            def normalise(q, tiles):
                for t in tiles:
                    act.wait_ge(nmr_ok, 2 * q + t // 2 + 1)
                    a.activation(nat[:, t, :], res[:, t, :], ACT.Identity, bias=nmr[:, t:t + 1],
                                 scale=rstd[:, t:t + 1]).then_inc(za_ok, 1)

            def ffn(l, f):
                turn_z(3 * l + 2 * f)
                with act.Fori(0, NPAIR) as i:
                    it = l * 2 * NPAIR + f * NPAIR + i
                    y = l * Y_ALL + f * Y_FFN2 + i
                    act.wait_ge(y_done, y * 8)
                    split("B", l * B_ALL + f * B_FFN2 + i)
                    split("D", l * D_ALL + f * D_FFN2 + i)
                    act.wait_ge(used["A"], l * AU_ALL + f * AU_FFN2 + i + 1)
                    a.activation(silu["A"], bank[0][:, :], ACT.Silu).then_inc(silu_ok["A"], 1)
                    split("A", l * A_ALL + f * A_FFN2 + i + 1)
                    act.wait_ge(h32_ok["A"], it + 1)
                    a.activation(hhi["A"], h32["A"], ACT.Copy).then_inc(hhi_ok["A"], 1)
                    act.wait_ge(used["B"], l * BU_ALL + f * BU_FFN2 + i + 1)
                    for h in range(2):
                        a.activation(silu["B"][:, h * 256:h * 256 + 256], bank[2][:, h * 256:h * 256 + 256],
                                     ACT.Silu).then_inc(silu_ok["B"], 1)
                    for h in range(2):
                        act.wait_ge(h32_ok["B"], it * 2 + h + 1)
                        a.activation(hhi["B"][:, h * 256:h * 256 + 256], h32["B"][:, h * 256:h * 256 + 256],
                                     ACT.Copy).then_inc(hhi_ok["B"], 1)
                normalise(3 * l + 2 * f, (0, 1, 2))

            split("A", 0)
            act.wait_ge(lam_landed, 16)
            act.wait_ge(lam_step, 2)
            a.activation(lame[:, :, :], lams[:, :, :], ACT.Exp).then_inc(lame_ok, 1)
            act.wait_ge(pos_ok, 2)
            with act.Fori(0, L) as l:
                ffn(l, 0)
                turn_z(3 * l + 1)
                split("B", l * B_ALL + B_NAT)
                act.wait_ge(res_ok, 3 * l + 2)
                for j in range(NPROJ):
                    for s in "AB":
                        k = 2 * j + (s == "B")
                        if s == "A":
                            act.wait_ge(used["A"], l * AU_ALL + A_NAT + j + 1)
                        else:
                            act.wait_ge(used["B"], l * BU_ALL + B_NAT + j + 1)
                        for t in range(NT):
                            src = bank[t + (4 if s == "B" else 0)]
                            if k == 0:
                                a.activation(nat[:, t, Y_SGU:Y_SGU + 256], src[:, 0:256], ACT.Gelu_apprx_tanh).then_inc(nat_free[s], 1)
                            elif k == 1:
                                a.activation(nat[:, t, Y_SGU + 256:Y_SGU + SGU_W], src[:, 0:128], ACT.Gelu_apprx_tanh)
                                a.activation(nat[:, t, 0:128], src[:, 128:256], ACT.Gelu_apprx_tanh).then_inc(nat_free[s], 1)
                            elif k == 2:
                                a.activation(nat[:, t, 128:SGU_W], src[:, 0:256], ACT.Gelu_apprx_tanh).then_inc(nat_free[s], 1)
                            elif k == 3:
                                a.activation(vhi[:, t, 0:256], src[:, 0:256], ACT.Copy).then_inc(vhi_ok, 1)
                            elif k == 4:
                                a.activation(vhi[:, t, 256:FOX_W], src[:, 0:FOX_W - 256], ACT.Copy).then_inc(vhi_ok, 1)
                            else:
                                a.activation(vhi[:, t, FOX_W:FOX_W + DIFF_W], src[:, 0:256], ACT.Copy).then_inc(vhi_ok, 1)
                        if k == 2:
                            act.wait_ge(ws_tri, l + 1)
                            a.activation(wshi, wsr, ACT.Copy).then_inc(wshi_ok, 1)
                        if k == 4:
                            act.wait_ge(fneg_ok, l + 1)
                            a.activation(fexp[:, :, :], fneg[:, :, :], ACT.Exp).then_inc(fexp_ok, 1)
                            act.wait_ge(fexp_ok, l + 1)
                            a.activation(fln[:, :, :], fexp[:, :, :], ACT.Ln, bias=1.0).then_inc(fln_ok, 1)
                            act.wait_ge(gb_ok, NT * l + NT)
                            a.activation(ghi, nat[:, :, 0:SGU_W], ACT.Copy).then_inc(ghi_ok, 1)
                        if s == "A":
                            split(s, l * A_ALL + A_NAT + j + 1)
                        elif j < NPROJ - 1:
                            split(s, l * B_ALL + B_NAT + j + 1)
                act.wait_ge(cum_done, l + 1)
                a.activation(brow[0:FOX_H, :], bank[0][0:FOX_H, :], ACT.Copy).then_inc(chi_ok, 1)

                split("B", l * B_ALL + B_WO)
                act.wait_ge(y_done, (l * Y_ALL + Y_WO) * 8)
                split("D", l * D_ALL + D_WO)

                def query(body, b):
                    act.wait_ge(q_done, body + 1)
                    a.activation(qhi, bank[6][:, :], ACT.Copy, scale=qscale[:, bass.ds(b, 1)]).then_inc(qhi_ok, 1)

                def key(b):
                    act.wait_ge(used["A"], l * AU_ALL + A_QK + b + 1)
                    a.activation(khi, bank[7][:, :], ACT.Copy).then_inc(khi_ok, 1)

                def heads(b, d, carry, last):
                    body = l * BODIES + b
                    K = body * STEPS
                    maps = 1 if d is None else 2
                    KD = None if d is None else (l * DIFF_P + d) * STEPS

                    def exp(k):
                        for m in range(maps):
                            act.wait_ge(max_ok[m], (K if m == 0 else KD) + k + 1)
                            if k >= 2 or carry:
                                act.wait_ge(pt_done, K + k - 1)
                            w = (k % NT + 1) * P
                            i = 2 * (k % 2) + m
                            a.activation(s32[:, i, 0:w], bank[i][:, 0:w], ACT.Exp, bias=negm[:, i:i + 1],
                                         accum_out=rsum[:, i:i + 1]).then_inc(exp_ok[m], 1)

                    def p_hi(k):
                        w = (k % NT + 1) * P
                        act.wait_ge(pt_done, K + k + 1)
                        if k >= 2 or carry:
                            act.wait_ge(pv_done, K + k - 1)
                        a.activation(pthi[k % 2][:, 0:w], bank[4 + k % 2][:, 0:w], ACT.Copy).then_inc(pthi_ok, 1)

                    if not carry:
                        act.wait_ge(pv_done, K)
                    for k in range(STEPS):
                        if k == STEPS - 1 and not last:
                            act.wait_ge(s_done[maps - 1], (K if maps == 1 else KD) + k + 1)
                            query(body + 1, b + 1)
                            p_hi(k - 1)
                            key(b + 1)
                            exp(k)
                            continue
                        if k == 0 and carry:
                            p_hi(-1)
                        exp(k)
                        if last and k < len(EARLY) // 2:
                            y_hi(2 * k)
                        if k >= 1:
                            p_hi(k - 1)
                        if last and k < len(EARLY) // 2:
                            y_hi(2 * k + 1)
                        if k == 0:
                            split_half(l * A_ALL + A_QK + b + 1, 1, hi_ok["A"])
                        if k == 4 and not last:
                            act.wait_ge(q_done, body + 2)
                            split_half(l * A_ALL + A_QK + b + 2, 0, qw_hi_ok)
                    if last:
                        p_hi(STEPS - 1)

                def y_hi(i):
                    act.wait_ge(yt_done, l * NC + i + 1)
                    c = ([e[0] for e in EARLY] + LATE)[i]
                    b = 6 + i % 2 if i < len(EARLY) else i - len(EARLY)
                    a.activation(xhi[:, c, :], bank[b][:, :], ACT.Copy).then_inc(ythi_ok, 1)

                query(l * BODIES, 0)
                key(0)
                split_half(l * A_ALL + A_QK + 1, 0, qw_hi_ok)
                heads(0, None, False, False)
                with act.Fori(0, FOX_P - 1) as p:
                    heads(p + 1, None, True, False)
                for d in range(DIFF_P):
                    heads(FOX_P + d, d, True, d == DIFF_P - 1)
                act.wait_ge(wo_a_done, l + 1)
                for h in range(2):
                    split_half(l * A_ALL + A_WO + 1, h, (qw_hi_ok, hi_ok["A"])[h])
                for i in range(len(LATE)):
                    y_hi(len(EARLY) + i)
                normalise(3 * l + 1, (0, 1))
                act.wait_ge(y_done, (l * Y_ALL + Y_FFN2) * 8)
                split("A", l * A_ALL + A_FFN2)
                normalise(3 * l + 1, (2,))
                ffn(l, 1)

        @block.tensor
        def _(pe):
            t_ = nc.tensor

            def product(out_, pairs, start=True, stop=True, check=False):
                n = 3 * len(pairs)
                k = 0
                for (shi, slo), (mhi, mlo) in pairs:
                    for a_, b_ in ((shi, mhi), (shi, mlo), (slo, mhi)):
                        k += 1
                        ins = t_.matmul(out_, a_, b_, start=(start and k == 1), stop=(stop and k == n), skip_group_check=check)
                return ins

            def w(s, lo, n):
                return whi[s][:, lo:lo + n], wlo[s][:, lo:lo + n]

            def x(c, lo=0, n=S):
                return xhi[:, c, lo:lo + n], xlo[:, c, lo:lo + n]

            def turn_z(q, y):
                for tiles in ((0, 1), (2,), (3,)):
                    if tiles == (3,):
                        pe.wait_ge(zd_ok, q + 1)
                    else:
                        pe.wait_ge(za_ok, 3 * q + tiles[-1] + 1)
                    for c in range(NC):
                        if tiles[0] == 0 and c == 4:
                            pe.wait_ge(y_free, y * 8 + 4)
                        for t in tiles:
                            ins = t_.transpose(bank[c][:, t * P:t * P + P], nat[:, t, c * P:c * P + P], ident[:, :])
                        if tiles == (3,):
                            ins.then_inc(turned, 1)

            def outputs(y, parts):
                def part(o, n):
                    stat, slot, off, _ = parts[n]
                    t, hf = divmod(o, 2)
                    if n == 0:
                        pe.wait_ge(y_free, y * 8 + o + 1)
                    ins = product(bank[4 + o % 4][:, :], [(stat(t), w(slot, off + hf * 512, 512))],
                                  start=(n == 0), stop=(n == 1))
                    if n == 1:
                        ins.then_inc(y_done, 1)

                for n in range(2):
                    parts[n][3](0)
                    for o in range(4):
                        part(o, n)
                for n in range(2):
                    parts[n][3](1)
                for o in range(4, 8):
                    part(o, 0)
                    part(o, 1)

            def ffn(l, f):
                T = 3 * l + 2 * f
                turn_z(T, l * Y_ALL + f * Y_FFN2)
                with pe.Fori(0, NPAIR) as i:
                    it = l * 2 * NPAIR + f * NPAIR + i
                    for s, n in (("A", l * A_ALL + f * A_FFN2 + i), ("B", l * B_ALL + f * B_FFN2 + i)):
                        b = 0 if s == "A" else 2
                        pe.wait_ge(lo_ok[s], n + 1)
                        pe.wait_ge(h32_ok[s], it if s == "A" else it * 2)
                        for c in range(NC):
                            if s == "A":
                                pe.wait_ge(x_ok, T * NC + c + 1)
                                if c == 0:
                                    pe.wait_ge(x32_ok, T * NC + 2)
                            for g in range(2):
                                ins = product(bank[b + g][:, :], [(w(s, (g * NC + c) * P, P), x(c))],
                                              start=(c == 0), stop=(c == NC - 1))
                        ins.then_inc(used[s], 1)
                    pe.wait_ge(lo_ok["D"], l * D_ALL + f * D_FFN2 + i + 1)
                    waits = {"A": lambda r: pe.wait_ge(h_ok["A"], it + 1) if r == 0 else None,
                             "B": lambda r: pe.wait_ge(h_ok["B"], it * 2 + r + 1)}
                    outputs(l * Y_ALL + f * Y_FFN2 + i,
                            [(lambda t, s=s: (hhi[s][:, t * P:t * P + P], hlo[s][:, t * P:t * P + P]), "D", k * D, waits[s])
                             for k, s in enumerate("AB")])

            def project(l, b):
                n = l * A_ALL + A_QK + b
                for g in range(2):
                    if g == 0 and not (isinstance(b, int) and b == 0):
                        pe.wait_ge(qw_ok, l * (BODIES + 1) + b)
                    else:
                        pe.wait_ge(lo_ok["A"], n + 1)
                    k = 0
                    for c in range(NC):
                        (shi, slo), (mhi, mlo) = w("A", (g * NC + c) * P, P), x(c)
                        for a_, b_ in ((shi, mhi), (shi, mlo), (slo, mhi)):
                            k += 1
                            ins = t_.matmul(bank[6 + g][:, :], a_, b_, start=(k == 1), stop=(k == 3 * NC))
                            if k == 3 * NC:
                                ins.then_inc(*((used["A"], 1) if g else (q_done, 1)))
                            yield

            def turn_y(l, i):
                early = i < len(EARLY)
                c = EARLY[i][0] if early else LATE[i - len(EARLY)]
                if early and i >= 2:
                    pe.wait_ge(yt_ok, l * NC + i - 1)
                b = 6 + i % 2 if early else i - len(EARLY)
                for t in range(NT):
                    ins = t_.transpose(bank[b][:, t * P:t * P + P], nat[:, t, c * P:c * P + P], ident[:, :])
                ins.then_inc(yt_done, 1)

            def early_output(l, u, parts):
                t, hf = divmod(u, 2)
                for n in parts:
                    c, s, off = EARLY[n]
                    if n == 0 and u >= 2:
                        pe.wait_ge(wo_free, l * 8 + u - 1)
                    ins = product(bank[6 + u % 2][:, :], [(x(c, t * P, P), w(s, off + hf * 512, 512))],
                                  start=(n == 0), stop=(n == len(EARLY) - 1))
                if n == len(EARLY) - 1:
                    ins.then_inc(wo_done, 1)

            def early(l):
                for i in range(len(EARLY)):
                    turn_y(l, i)
                    yield
                pe.wait_ge(yt_ok, l * NC + len(EARLY))
                pe.wait_ge(lo_ok["A"], l * A_ALL + A_WO + 1)
                pe.wait_ge(lo_ok["B"], l * B_ALL + B_WO + 1)
                pe.wait_ge(lo_ok["D"], l * D_ALL + D_WO + 1)
                for u in range(AMONG):
                    for h in range(2):
                        early_output(l, u, range(3 * h, 3 * h + 3))
                        yield

            def heads(l, b, d, carry, last):
                body = l * BODIES + b
                K = body * STEPS
                maps = 1 if d is None else 2
                KD = None if d is None else (l * DIFF_P + d) * STEPS
                rows = HD // maps

                def scores(k):
                    hh, t = divmod(k, NT)
                    n_ = (t + 1) * P
                    for m in range(maps):
                        i = 2 * (k % 2) + m
                        if k >= 2 or (carry and (m == 0 or d > 0)):
                            pe.wait_ge(exp_ok[m], (K if m == 0 else KD) + k - 1)
                        r = hh * HD + m * rows
                        product(bank[i][:, 0:n_], [((qhi[r:r + rows, t * P:t * P + P], qlo[r:r + rows, t * P:t * P + P]),
                                                    (khi[r:r + rows, 0:n_], klo[r:r + rows, 0:n_]))], stop=False)
                        t_.matmul(bank[i][:, 0:n_], sel[0:65, hh, :], brow[0:65, 0:n_], start=False, stop=False)
                        t_.matmul(bank[i][:, t * P:n_], identb[:, :], maskb[:, :], start=False, stop=True).then_inc(s_done[m], 1)

                def turn_p(k):
                    t = k % NT
                    if maps == 1 or (k < 0 and d == 0):
                        pe.wait_ge(exp_ok[0], K + k + 1)
                    else:
                        pe.wait_ge(mixp_ok, KD + k + 1)
                    if k >= 2 or carry:
                        pe.wait_ge(o_ok, K + k - 1)
                    elif k == 0:
                        pe.wait_ge(o_ok, K)
                    for e in range(t + 1):
                        ins = t_.transpose(bank[4 + k % 2][:, e * P:e * P + P], s32[:, 2 * (k % 2), e * P:e * P + P], ident[:, :])
                    ins.then_inc(pt_done, 1)

                def values(k):
                    hh, t = divmod(k % STEPS, NT)
                    pe.wait_ge(pt_ok, K + k + 1)
                    vc = (b - 1 if k < 0 else b) * 2 * HD + hh * HD
                    pairs = []
                    for e in range(t + 1):
                        pairs.append(((pthi[k % 2][:, e * P:e * P + P], ptlo[k % 2][:, e * P:e * P + P]),
                                      (vhi[:, e, bass.ds(vc, HD)], vlo[:, e, bass.ds(vc, HD)])))
                    product(bank[4 + k % 2][:, 0:HD], pairs).then_inc(pv_done, 1)

                between = early(l) if last else project(l, b + 1)

                def fill(i):
                    for _ in range(1 if last else FILL[i]):
                        next(between, None)

                for k in range(STEPS):
                    if k == 0:
                        if carry:
                            values(-2)
                            turn_p(-1)
                        pe.wait_ge(qk_ok, body * 3 + 3)
                        scores(0)
                        fill(0)
                        fill(1)
                        continue
                    scores(k)
                    fill(0)
                    turn_p(k - 1)
                    fill(1)
                    if k >= 2 or carry:
                        values(k - 2)
                if last:
                    values(STEPS - 2)
                    turn_p(STEPS - 1)
                    early_output(l, AMONG, range(len(EARLY)))
                    values(STEPS - 1)

            pe.wait_ge(ident_ok, 2)
            pe.wait_ge(x_landed, 16)
            t_.transpose(bank[0][:, 0:P], ident[:, :], ident[:, :])
            with pe.Fori(0, L) as l:
                ffn(l, 0)
                T = 3 * l + 1
                turn_z(T, l * Y_ALL + NPAIR)
                with pe.Fori(0, NPROJ) as j:
                    for s, n in (("A", l * A_ALL + A_NAT + j), ("B", l * B_ALL + B_NAT + j)):
                        pe.wait_ge(lo_ok[s], n + 1)
                        pe.wait_ge(nat_free[s], l * NT * NPROJ + j * NT)
                        for c in range(NC):
                            if s == "A":
                                pe.wait_ge(x_ok, T * NC + c + 1)
                                if c == 0:
                                    pe.wait_ge(x32_ok, T * NC + 4)
                            for t in range(NT):
                                ins = product(bank[t + (4 if s == "B" else 0)][:, 0:256], [(x(c, t * P, P), w(s, c * 256, 256))],
                                              start=(c == 0), stop=(c == NC - 1))
                        ins.then_inc(used[s], 1)
                pe.wait_ge(nat_free["A"], l * NT * NPROJ + NT * NPROJ)
                pe.wait_ge(lf_ok, l + 1)
                for b in range(NT):
                    ins = t_.matmul(bank[0][0:FOX_H, :], lf[:, b, :], since[:, (3 - b) * P:(3 - b) * P + S],
                                    start=(b == 0), stop=(b == NT - 1))
                ins.then_inc(cum_done, 1)
                pe.wait_ge(wslo_ok, l + 1)
                pe.wait_ge(glo_ok, l + 1)
                for h in range(SGU_H):
                    o = bank[1 + h // 2][:, (h % 2) * 256:(h % 2) * 256 + 256].rearrange("p (c n) -> p c n", c=NT)
                    ins = product(o, [((wshi[:, h * P:h * P + P], wslo[:, h * P:h * P + P]),
                                       (ghi[:, :, h * HD:h * HD + HD], glo[:, :, h * HD:h * HD + HD]))])
                    if h % 2:
                        ins.then_inc(sgu_done, 1)
                pe.wait_ge(nat_free["B"], l * NT * NPROJ + NT * NPROJ)
                for _ in project(l, 0):
                    pass
                pe.wait_ge(const_ok, CONSTS)
                pe.wait_ge(sgu_out, l * SGU_H + SGU_H)
                pe.wait_ge(c_ok, l + 1)
                heads(l, 0, None, False, False)
                with pe.Fori(0, FOX_P - 1) as p:
                    heads(l, p + 1, None, True, False)
                for d in range(DIFF_P):
                    heads(l, FOX_P + d, d, True, d == DIFF_P - 1)
                for u in (6, 7):
                    early_output(l, u, range(2))
                t_.transpose(bank[2][:, 0:P], ident[:, :], ident[:, :]).then_inc(wo_a_done, 1)
                early_output(l, 6, range(2, len(EARLY)))
                pe.wait_ge(y_ok, l + 1)
                for i in range(len(LATE)):
                    turn_y(l, len(EARLY) + i)
                early_output(l, 7, range(2, len(EARLY)))
                pe.wait_ge(lo_ok["A"], l * A_ALL + A_WO + 2)
                pe.wait_ge(o_ok, (l + 1) * BODIES * STEPS)
                pe.wait_ge(wo_free, l * 8 + 8)
                outputs(l * Y_ALL + Y_WO,
                        [(lambda t, c=c: x(c, t * P, P), "A", k * D,
                          lambda r, k=k: pe.wait_ge(yt_ok, l * NC + len(EARLY) + k + 1) if r == 0 else None)
                         for k, c in enumerate(LATE)])
                ffn(l, 1)

        @block.vector
        def _(dve):
            v = nc.vector

            def f32(ap):
                return ap.bitcast(F32)

            def split(s, n):
                dve.wait_ge(hi_ok[s], n + 1)
                v.tensor_tensor(wlo[s][:, :], raw[s][:, :], f32(whi[s][:, :]), ALU.subtract).then_inc(lo_ok[s], 1)

            def split_half(n, h, ready, step):
                dve.wait_ge(*ready)
                t = slice(h * D, h * D + D)
                v.tensor_tensor(wlo["A"][:, t], raw["A"][:, t], f32(whi["A"][:, t]), ALU.subtract).then_inc(step, 1)

            def turn(T):
                for c in range(NC + 1):
                    if c < NC:
                        dve.wait_ge(x32_ok, T * NC + c + 1)
                        v.tensor_copy(xhi[:, c, :], s32[:, c % 4, :]).then_inc(xhi_ok, 1)
                    if c >= 1:
                        dve.wait_ge(xhi_ok, T * NC + c)
                        v.tensor_tensor(xlo[:, c - 1, :], s32[:, (c - 1) % 4, :], f32(xhi[:, c - 1, :]),
                                        ALU.subtract).then_inc(x_ok, 1)

            def accumulate(o, b, scale, step):
                t, hf = divmod(o, 2)
                r = res[:, t, hf * 512:hf * 512 + 512]
                v.scalar_tensor_tensor(out=r, in0=bank[b][:, :], scalar=scale, in1=r,
                                       op0=ALU.mult, op1=ALU.add).then_inc(step, 1)

            def add(y, o, scale):
                dve.wait_ge(y_done, y * 8 + o + 1)
                accumulate(o, 4 + o % 4, scale, y_free)

            def add_outputs(y, scale):
                dve.wait_ge(y_free, y * 8 + 4)
                for o in range(8):
                    add(y, o, scale)

            def last_outputs(l, j, y, scale):
                q = 3 * l + j
                dve.wait_ge(y_free, y * 8 + 4)
                for o in range(9):
                    if o < 8:
                        add(y, o, scale)
                    if o >= 1:
                        t, hf = divmod(o - 1, 2)
                        dve.wait_ge(y_free, y * 8 + 4 + o)
                        v.bn_stats(st[:, t, hf, :], res[:, t, hf * 512:hf * 512 + 512]).then_inc(st_ok, 1)
                    if o in (4, 8):
                        dve.wait_ge(st_ok, q * 8 + o)
                        wait_here(5 + o // 4)
                        for t in (o // 2 - 2, o // 2 - 1):
                            v.bn_aggr(mv[:, t, :], st[:, t, :, :].rearrange("p a n -> p (a n)")).then_inc(mv_ok, 1)
                t = NT - 1
                dve.wait_ge(rstd_ok, 2 * q + 2)
                v.tensor_scalar(nat[:, t, :], res[:, t, :], mv[:, t, 0:1], rstd[:, t:t + 1], ALU.subtract,
                                ALU.mult).then_inc(zd_ok, 1)

            def ffn(l, f):
                turn(3 * l + 2 * f)

                def pair(i):
                    it = l * 2 * NPAIR + f * NPAIR + i
                    split("B", l * B_ALL + f * B_FFN2 + i)
                    split("D", l * D_ALL + f * D_FFN2 + i)
                    dve.wait_ge(silu_ok["A"], it + 1)
                    dve.wait_ge(hhi_ok["A"], it)
                    v.tensor_tensor(h32["A"], silu["A"], bank[1][:, :], ALU.mult).then_inc(h32_ok["A"], 1)
                    split("A", l * A_ALL + f * A_FFN2 + i + 1)
                    dve.wait_ge(hhi_ok["A"], it + 1)
                    v.tensor_tensor(hlo["A"], h32["A"], f32(hhi["A"]), ALU.subtract).then_inc(h_ok["A"], 1)
                    for h in range(2):
                        t = slice(h * 256, h * 256 + 256)
                        dve.wait_ge(silu_ok["B"], it * 2 + h + 1)
                        v.tensor_tensor(h32["B"][:, t], silu["B"][:, t], bank[3][:, t], ALU.mult).then_inc(h32_ok["B"], 1)
                    for h in range(2):
                        t = slice(h * 256, h * 256 + 256)
                        dve.wait_ge(hhi_ok["B"], it * 2 + h + 1)
                        v.tensor_tensor(hlo["B"][:, t], h32["B"][:, t], f32(hhi["B"][:, t]), ALU.subtract).then_inc(h_ok["B"], 1)

                with dve.Fori(0, NPAIR - 1) as i:
                    pair(i)
                    dve.wait_ge(res_ok, 3 * l + 2 * f + 1)
                    add_outputs(l * Y_ALL + f * Y_FFN2 + i, 0.5)
                pair(NPAIR - 1)
                last_outputs(l, 2 * f, l * Y_ALL + f * Y_FFN2 + NPAIR - 1, 0.5)

            def wait_here(i):
                v.memset(idle[0:1, i:i + 1], 0.0)

            for b in range(4):
                v.memset(free[0:1, b:b + 1], 0.0).then_inc(y_free, 1)
            for b in range(NT):
                v.memset(free[0:1, 4 + b:5 + b], 0.0).then_inc(*((za_ok, 1) if b < NT - 1 else (zd_ok, 1)))
            split("A", 0)
            dve.wait_ge(lam_landed, 16)
            v.tensor_tensor(lamp[:, :, :, 0, :], lamp[:, :, :, 0, :], lamp[:, :, :, 1, :], ALU.mult).then_inc(lam_step, 1)
            dve.wait_ge(lam_step, 1)
            v.tensor_reduce(lams[:, :, :], lamp[:, :, :, 0, :], AX.X, ALU.add).then_inc(lam_step, 1)
            dve.wait_ge(lame_ok, 1)
            v.tensor_tensor(nlam[:, :], lame[:, :, 1], lame[:, :, 0], ALU.subtract).then_inc(lam_step, 1)
            dve.wait_ge(lam_step, 3)
            dve.wait_ge(const_ok, CONSTS)
            v.tensor_tensor(nlam[:, :], nlam[:, :], ilam[:, :], ALU.subtract).then_inc(lam_step, 1)
            dve.wait_ge(pos_ok, 1)
            v.tensor_copy(brow[64:65, :], s32[64:65, 0, :]).then_inc(pos_ok, 1)
            dve.wait_ge(lam_step, 4)
            with dve.Fori(0, L) as l:
                ffn(l, 0)
                turn(3 * l + 1)
                dve.wait_ge(mix_landed, l * 32 + 32)
                v.tensor_copy(nlam1[:, :], nlam[:, bass.ds(l, 1)]).then_inc(nlam1_ok, 1)
                v.tensor_scalar(diff_g, diff_g, olam[:, bass.ds(l, 1)], None, ALU.mult).then_inc(dgs_ok, 1)
                split("B", l * B_ALL + B_NAT)
                split("A", l * A_ALL + A_NAT + 1)
                split("B", l * B_ALL + B_NAT + 1)
                split("A", l * A_ALL + A_NAT + 2)
                dve.wait_ge(nat_free["B"], l * NT * NPROJ + NT)
                dve.wait_ge(nat_free["A"], l * NT * NPROJ + 2 * NT)
                for t in range(NT):
                    v.bn_stats(gst[:, t, :], nat[:, t, 0:SGU_W]).then_inc(gst_ok, 1)
                dve.wait_ge(gst_ok, l * NT + NT)
                wait_here(4)
                for t in range(NT):
                    v.bn_aggr(gmv[:, t, :], gst[:, t, :]).then_inc(gmv_ok, 1)
                dve.wait_ge(wshi_ok, l + 1)
                v.tensor_tensor(wslo, wsr, f32(wshi), ALU.subtract).then_inc(wslo_ok, 1)

                def values(k):
                    s = "AB"[k % 2]
                    lo, n = ((0, 256), (256, FOX_W - 256), (FOX_W, DIFF_W))[k - 3]
                    for t in range(NT):
                        src = bank[t + (4 if s == "B" else 0)]
                        dve.wait_ge(vhi_ok, l * 3 * NT + (k - 3) * NT + t + 1)
                        if k == 4:
                            v.tensor_tensor(flog[:, t, :], src[:, F_AT:F_AT + FOX_H], f_bias, ALU.add).then_inc(f_ok, 1)
                        v.tensor_tensor(vlo[:, t, lo:lo + n], src[:, 0:n], f32(vhi[:, t, lo:lo + n]),
                                        ALU.subtract).then_inc(nat_free[s], 1)

                values(3)
                split("B", l * B_ALL + B_NAT + 2)
                dve.wait_ge(grs_ok, l + 1)
                for t in range(NT):
                    v.tensor_scalar(nat[:, t, 0:SGU_W], nat[:, t, 0:SGU_W], gmv[:, t, 0:1], grs[:, t:t + 1],
                                    ALU.subtract, ALU.mult).then_inc(gn_ok, 1)
                for t in range(NT):
                    dve.wait_ge(gn_ok, l * NT + t + 1)
                    v.tensor_tensor(nat[:, t, 0:SGU_W], nat[:, t, 0:SGU_W], sgu_g, ALU.mult).then_inc(gg_ok, 1)
                for t in range(NT):
                    dve.wait_ge(gg_ok, l * NT + t + 1)
                    v.tensor_tensor(nat[:, t, 0:SGU_W], nat[:, t, 0:SGU_W], sgu_b, ALU.add).then_inc(gb_ok, 1)
                values(4)
                dve.wait_ge(f_ok, l * NT + NT)
                v.scalar_tensor_tensor(out=fneg[:, :, :], in0=flog[:, :, :], scalar=-1.0, in1=flog[:, :, :],
                                       op0=ALU.mult, op1=ALU.min).then_inc(fneg_ok, 1)
                dve.wait_ge(fln_ok, l + 1)
                v.scalar_tensor_tensor(out=lf[:, :, :], in0=flog[:, :, :], scalar=0.0, in1=fln[:, :, :],
                                       op0=ALU.min, op1=ALU.subtract).then_inc(lf_ok, 1)
                dve.wait_ge(ghi_ok, l + 1)
                v.tensor_tensor(glo, nat[:, :, 0:SGU_W], f32(ghi), ALU.subtract).then_inc(glo_ok, 1)
                split("A", l * A_ALL + A_QK)
                values(5)
                dve.wait_ge(chi_ok, l + 1)
                v.tensor_tensor(brow[32:32 + FOX_H, :], bank[0][0:FOX_H, :], f32(brow[0:FOX_H, :]),
                                ALU.subtract).then_inc(c_ok, 1)
                for h in range(SGU_H):
                    if h % 2 == 0:
                        dve.wait_ge(sgu_done, l * (SGU_H // 2) + h // 2 + 1)
                    o = bank[1 + h // 2][:, (h % 2) * 256:(h % 2) * 256 + 256].rearrange("p (c n) -> p c n", c=NT)
                    u = nat[:, :, Y_SGU + h * HD:Y_SGU + h * HD + HD]
                    v.scalar_tensor_tensor(out=u, in0=o, scalar=mixc[:, h:h + 1], in1=u, op0=ALU.add,
                                           op1=ALU.mult).then_inc(sgu_out, 1)

                split("B", l * B_ALL + B_WO)
                split("D", l * D_ALL + D_WO)

                def query(body, b):
                    v.tensor_copy(sel[0:65, :, :], selall[0:65, bass.ds(b * 2, 2)].broadcast_to([65, 2, P])).then_inc(qk_ok, 1)
                    dve.wait_ge(qhi_ok, body + 1)
                    v.scalar_tensor_tensor(out=qlo, in0=bank[6][:, :], scalar=qscale[:, bass.ds(b, 1)], in1=f32(qhi),
                                           op0=ALU.mult, op1=ALU.subtract).then_inc(qk_ok, 1)

                def key(body):
                    dve.wait_ge(khi_ok, body + 1)
                    v.tensor_tensor(klo, bank[7][:, :], f32(khi), ALU.subtract).then_inc(qk_ok, 1)

                def y_lo(i):
                    dve.wait_ge(ythi_ok, l * NC + i + 1)
                    c = ([e[0] for e in EARLY] + LATE)[i]
                    b = 6 + i % 2 if i < len(EARLY) else i - len(EARLY)
                    v.tensor_tensor(xlo[:, c, :], bank[b][:, :], f32(xhi[:, c, :]), ALU.subtract).then_inc(yt_ok, 1)

                def early_add(u):
                    dve.wait_ge(wo_done, l * 8 + u + 1)
                    accumulate(u, 6 + u % 2, 1.0, wo_free)

                def rms(p, stage):
                    pair = l * DIFF_P + p
                    lo = Y_DIFF + p * 2 * HD
                    yd = nat[:, :, lo:lo + 2 * HD]
                    if stage == 0:
                        dve.wait_ge(o_ok, (l * BODIES + FOX_P + p + 1) * STEPS)
                        v.scalar_tensor_tensor(out=sq[:, :, :], in0=yd, scalar=1.0 / HD, in1=yd, op0=ALU.mult,
                                               op1=ALU.mult).then_inc(sq_ok, 1)
                    elif stage == 1:
                        dve.wait_ge(sq_ok, pair + 1)
                        v.tensor_reduce(dms[:, p * STEPS:p * STEPS + STEPS], sq[:, :, :].rearrange("p t (h n) -> p (t h) n", n=HD),
                                        AX.X, ALU.add).then_inc(dms_ok, 1)
                    elif stage == 2:
                        dve.wait_ge(drs_ok, pair + 1)
                        for t in range(NT):
                            yt = yd[:, t, :].rearrange("p (h n) -> p h n", n=HD)
                            i = p * STEPS + 2 * t
                            v.tensor_tensor(yt, yt, drs[:, i:i + 2].broadcast_to([P, 2, HD]), ALU.mult).then_inc(dn_ok, 1)
                    else:
                        dve.wait_ge(dgs_ok, l + 1)
                        for t in range(NT):
                            dve.wait_ge(dn_ok, pair * NT + t + 1)
                            ins = v.tensor_tensor(yd[:, t, :], yd[:, t, :], diff_g[:, p * 2 * HD:(p + 1) * 2 * HD], ALU.mult)
                        if p == DIFF_P - 1:
                            ins.then_inc(y_ok, 1)

                def heads(b, d, carry, last):
                    body = l * BODIES + b
                    K = body * STEPS
                    maps = 1 if d is None else 2
                    KD = None if d is None else (l * DIFF_P + d) * STEPS

                    def row_max(k):
                        w_ = (k % NT + 1) * P
                        for m in range(maps):
                            i = 2 * (k % 2) + m
                            dve.wait_ge(s_done[m], (K if m == 0 else KD) + k + 1)
                            v.tensor_reduce(negm[:, i:i + 1], bank[i][:, 0:w_], AX.X, ALU.max,
                                            negate=True).then_inc(max_ok[m], 1)

                    def inverse(k):
                        dve.wait_ge(exp_ok[0], K + k + 1)
                        i = 2 * (k % 2)
                        j = k % STEPS
                        v.reciprocal(rinv[:, j, 0:1], rsum[:, i:i + 1]).then_inc(rinv_ok, 1)

                    def mix(k):
                        i = 2 * (k % 2)
                        dve.wait_ge(exp_ok[0], K + k + 1)
                        dve.wait_ge(exp_ok[1], KD + k + 1)
                        v.reciprocal(rinv[:, k, :], rsum[:, i:i + 2]).then_inc(rinv_ok, 1)
                        dve.wait_ge(rinv_ok, K + k + 1)
                        v.scalar_tensor_tensor(out=wlam[:, k:k + 1], in0=rinv[:, k, 1:2], scalar=rsum[:, i:i + 1],
                                               in1=nlam1[:, :], op0=ALU.mult, op1=ALU.mult).then_inc(wlam_ok, 1)
                        dve.wait_ge(wlam_ok, KD + k + 1)
                        w_ = (k % NT + 1) * P
                        v.scalar_tensor_tensor(out=s32[:, i, 0:w_], in0=s32[:, i + 1, 0:w_], scalar=wlam[:, k:k + 1],
                                               in1=s32[:, i, 0:w_], op0=ALU.mult, op1=ALU.add).then_inc(mixp_ok, 1)

                    def p_lo(k):
                        w_ = (k % NT + 1) * P
                        dve.wait_ge(pthi_ok, K + k + 1)
                        v.tensor_tensor(ptlo[k % 2][:, 0:w_], bank[4 + k % 2][:, 0:w_], f32(pthi[k % 2][:, 0:w_]),
                                        ALU.subtract).then_inc(pt_ok, 1)

                    def output(k):
                        j = k % STEPS
                        hh, t = divmod(j, NT)
                        dve.wait_ge(pv_done, K + k + 1)
                        o = nat[:, t, bass.ds((b - 1 if k < 0 else b) * 2 * HD + hh * HD, HD)]
                        dve.wait_ge(rinv_ok, K + k + 1)
                        v.tensor_scalar(o, bank[4 + k % 2][:, 0:HD], rinv[:, j, 0:1], None, ALU.mult).then_inc(o_ok, 1)

                    for k in range(STEPS):
                        if k == 0 and carry:
                            output(-2)
                            if maps == 1 or d == 0:
                                inverse(-1)
                            p_lo(-1)
                        row_max(k)
                        if k == STEPS - 1 and not last:
                            query(body + 1, b + 1)
                            p_lo(k - 1)
                            key(body + 1)
                            output(k - 2)
                            if maps == 1:
                                inverse(k - 1)
                            else:
                                mix(k)
                            continue
                        if last and k < len(EARLY) // 2:
                            y_lo(2 * k)
                        if maps == 2:
                            mix(k)
                        elif k >= 1:
                            inverse(k - 1)
                        if k >= 1:
                            p_lo(k - 1)
                        if last and k < len(EARLY) // 2:
                            y_lo(2 * k + 1)
                        if k >= 2 or (carry and k == 1):
                            output(k - 2)
                        if k == 1:
                            split_half(l * A_ALL + A_QK + b + 1, 1, (hi_ok["A"], l * A_ALL + A_QK + b + 2), lo_ok["A"])
                        if k == 5 and not last:
                            split_half(l * A_ALL + A_QK + b + 2, 0, (qw_hi_ok, l * (BODIES + 1) + b + 2), qw_ok)
                        if last and 2 <= k <= 5:
                            rms(0, k - 2)
                        if last and k == 3:
                            dve.wait_ge(res_ok, 3 * l + 2)
                        if last and k >= 4:
                            early_add(k - 4)
                    if last:
                        output(STEPS - 2)
                        p_lo(STEPS - 1)
                        early_add(4)
                        output(STEPS - 1)

                query(l * BODIES, 0)
                key(l * BODIES)
                split_half(l * A_ALL + A_QK + 1, 0, (qw_hi_ok, l * (BODIES + 1) + 1), qw_ok)
                dve.wait_ge(nlam1_ok, l + 1)
                wait_here(5)
                heads(0, None, False, False)
                with dve.Fori(0, FOX_P - 1) as p:
                    heads(p + 1, None, True, False)
                for d in range(DIFF_P):
                    heads(FOX_P + d, d, True, d == DIFF_P - 1)
                rms(DIFF_P - 1, 0)
                rms(DIFF_P - 1, 1)
                early_add(AMONG)
                rms(DIFF_P - 1, 2)
                rms(DIFF_P - 1, 3)
                for h in range(2):
                    split_half(l * A_ALL + A_WO + 1, h,
                               ((qw_hi_ok, (l + 1) * (BODIES + 1)), (hi_ok["A"], l * A_ALL + A_WO + 2))[h],
                               (qw_ok, lo_ok["A"])[h])
                for i in range(len(LATE)):
                    y_lo(len(EARLY) + i)
                early_add(6)
                early_add(7)
                dve.wait_ge(wo_free, l * 8 + 8)
                last_outputs(l, 1, l * Y_ALL + Y_WO, 1.0)
                split("A", l * A_ALL + A_FFN2)
                ffn(l, 1)
            dve.wait_ge(gbr_landed, 16 * 3 * L + 16)
            dve.wait_ge(za_ok, 3 * 3 * L + 3)
            dve.wait_ge(zd_ok, 3 * L + 1)
            for t in range(NT):
                v.tensor_tensor(nat[:, t, :], nat[:, t, :], gbr[:, 0, :], ALU.mult).then_inc(fin_step, 1)
            for t in range(NT):
                dve.wait_ge(fin_step, t + 1)
                v.tensor_tensor(nat[:, t, :], nat[:, t, :], gbr[:, 1, :], ALU.add).then_inc(fin_ok, 1)


CONSTS = 9 + 2 * L + BODIES + 1 + 2 + 2 + DIFF_H


def lay_out(i):
    def cols(w, n, width):
        return w.reshape(NC, P, n, width).transpose(2, 1, 0, 3)

    def ffn(l, k):
        g, u = (cols(i[f"ffn_{k}_w_{x}"][l], 2 * NPAIR, P) for x in ("gate", "up"))
        gu = np.stack([g, u], 2).reshape(NPAIR, 2, P, SLOT)
        d = i[f"ffn_{k}_w_down"][l].reshape(NPAIR, 2, P, D).transpose(0, 2, 1, 3).reshape(NPAIR, P, SLOT)
        return gu[:, 0], gu[:, 1], d

    A, B, Dn = [], [], []
    for l in range(L):
        w = i["w_in"][l]
        a, b, d = ffn(l, "a")
        natp = np.stack([w[:, c:c + 256].reshape(NC, P, 256).transpose(1, 0, 2).reshape(P, SLOT) for c in NAT_COLS])

        def qk(q, k, n):
            return np.stack([cols(w[:, q:q + n * P], n, P), cols(w[:, k:k + n * P], n, P)], 2).reshape(n, P, SLOT)

        def wo(c, e):
            return i["w_out"][l].reshape(NC, P, D)[[c, e]].transpose(1, 0, 2).reshape(1, P, SLOT)

        a2, b2, d2 = ffn(l, "b")
        early = {s: wo(*[c for c, slot, _ in EARLY if slot == s]) for s in "ABD"}
        A += [a, natp[0::2], qk(C_FQ, C_FK, FOX_P), qk(C_DQ, C_DK, DIFF_P), early["A"], wo(*LATE), a2]
        B += [b, natp[1::2], early["B"], b2]
        Dn += [d, early["D"], d2]
    A, B, Dn = np.concatenate(A + [A[0][0:1]]), np.concatenate(B), np.concatenate(Dn)
    one, zero = np.ones((1, D), np.float32), np.zeros((1, D), np.float32)
    g = np.stack([i["norm_a_g"], i["norm_m_g"], i["norm_b_g"]], 1).reshape(3 * L, D)
    b = np.stack([i["norm_a_b"], i["norm_m_b"], i["norm_b_b"]], 1).reshape(3 * L, D)
    gb = np.stack([np.concatenate([one, g]), np.concatenate([zero, b])], 1)
    return {
        "x": i["x"].reshape(NT, P, D).transpose(1, 0, 2),
        "a_w": A, "b_w": B, "d_w": Dn,
        "gb_row": gb,
        "gb_col": gb.reshape(-1, 2, NC, P).transpose(0, 3, 1, 2),
        "mix_row": np.concatenate([i["diff_norm_g"], i["sgu_norm_g"], i["sgu_norm_b"], i["fox_f_bias"]], 1),
        "mix_col": i["sgu_b_s"].transpose(0, 2, 1),
        "ws": i["sgu_w_s"].transpose(0, 3, 1, 2).reshape(L, P, SGU_H * P),
        "lamv": np.stack([np.stack([i["diff_lambda_q1"], i["diff_lambda_k1"]], 1),
                          np.stack([i["diff_lambda_q2"], i["diff_lambda_k2"]], 1)], 1)[None],
    }


def kernel(**inputs):
    import concourse.bacc as bacc
    from concourse.bass_utils import run_bass_kernel_spmd

    nc = bacc.Bacc("TRN2", target_bir_lowering=False, num_devices=1)
    arrays, args = {}, []
    for name, a in lay_out({k: np.asarray(v) for k, v in inputs.items()}).items():
        a = np.ascontiguousarray(a)
        arrays[f"in_{name}"] = a
        args.append(nc.dram_tensor(f"in_{name}", a.shape, mybir.dt.from_np(a.dtype), kind="ExternalInput").ap())
    args.append(nc.dram_tensor("out", (P, NT, D), F32, kind="ExternalOutput").ap())
    build(nc, *args)
    r = run_bass_kernel_spmd(nc, [arrays], core_ids=[0])
    y = r.results[0]["out"]
    return np.ascontiguousarray(y.reshape(P, NT, D).transpose(1, 0, 2)).reshape(1, S, D)
```

```python
from contextlib import ExitStack
import math

import numpy as np
import concourse.bass as bass
from concourse import mybir

ALU = mybir.AluOpType
ACT = mybir.ActivationFunctionType
F32 = mybir.dt.float32
F32R = mybir.dt.float32r
BF16 = mybir.dt.bfloat16
AX = mybir.AxisListType

P = 128
L = 2
D = 1024
S = 512
F = 2816
NT = S // P
NC = D // P
NPAIR = F // P // 2
HD = 64
FOX_H, DIFF_H, SGU_H = 6, 4, 6
FOX_W, DIFF_W, SGU_W = FOX_H * HD, DIFF_H * HD, SGU_H * HD
FOX_P, DIFF_P = FOX_H // 2, DIFF_H // 2
ALPHA = (2 * L) ** 0.25
EPS = 1e-5
NEG = -1e30
SLOPES = [2.0 ** (-8.0 * (h + 1) / DIFF_H) for h in range(DIFF_H)]
LAM_INIT = [0.8 - 0.6 * math.exp(-0.3 * l) for l in range(L)]

C_FQ, C_FK, C_FV, C_FF = 0, FOX_W, 2 * FOX_W, 3 * FOX_W
C_DQ = C_FF + FOX_H
C_DK, C_DV, C_Z = C_DQ + DIFF_W, C_DQ + 2 * DIFF_W, C_DQ + 3 * DIFF_W
NAT_COLS = [C_Z, C_Z + 256, C_Z + 512, C_FV, C_FV + 256, C_DV]
NPROJ = len(NAT_COLS) // 2
F_AT = C_FF - NAT_COLS[4]

SLOT = 2 * D

BODIES = FOX_P + DIFF_P
A_FFN, A_NAT, A_QK, A_WO, A_FFN2, A_ALL = (int(x) for x in np.cumsum([0, NPAIR, NPROJ, BODIES, 1, NPAIR]))
B_FFN, B_NAT, B_WO, B_FFN2, B_ALL = (int(x) for x in np.cumsum([0, NPAIR, NPROJ, 2, NPAIR]))
D_FFN, D_WO, D_FFN2, D_ALL = (int(x) for x in np.cumsum([0, NPAIR, 1, NPAIR]))
AU_FFN2, AU_ALL = A_WO, A_ALL - 1
BU_FFN2, BU_ALL = B_WO, B_ALL - 2
Y_WO, Y_FFN2, Y_ALL = NPAIR, NPAIR + 1, 2 * NPAIR + 1
STEPS = 2 * NT
FILL = (3, 3)
EARLY = [(0, "B", 0), (1, "B", D), (2, "A", 0), (5, "A", D), (6, "D", 0), (7, "D", D)]
LATE = [3, 4]
AMONG = 5
HALF = S // 2
HALF_BANKS = [(2, 3, 4, 5), (6, 7, 4, 5)]


def build(nc, x_in, a_w, b_w, d_w, gb_row, gb_col, mix_row, mix_col, ws_in, lamv, out):
    ctx = ExitStack()
    with ctx:
        def sb(name, shape, dt=F32):
            return ctx.enter_context(nc.sbuf_tensor(name, shape, dt))

        def sem(name):
            return ctx.enter_context(nc.semaphore(name))

        bank = [ctx.enter_context(nc.psum_tensor(f"bank{i}", [P, 512], F32)) for i in range(8)]

        raw = {s: sb(f"raw{s}", [P, SLOT]) for s in "ABD"}
        whi = {s: sb(f"whi{s}", [P, SLOT], F32R) for s in "ABD"}
        wlo = {s: sb(f"wlo{s}", [P, SLOT], F32R) for s in "ABD"}
        xhi = sb("xhi", [P, NC, S], F32R)
        xlo = sb("xlo", [P, NC, S], F32R)
        res = sb("res", [P, NT, D])
        nat = sb("nat", [P, NT, D])
        s32 = sb("s32", [P, 4, 512])
        hl = sb("hl", [P, 9, 512], F32R)
        vals = sb("vals", [P, NT, 2, FOX_W + DIFF_W], F32R)
        gbr = sb("gbr", [P, 2, D])
        gbc = sb("gbc", [P, 2, NC])
        mixr = sb("mixr", [P, DIFF_W + 2 * SGU_W + FOX_H])
        mixc = sb("mixc", [P, SGU_H])
        ident = sb("ident", [P, P])
        identb = sb("identb", [P, P], BF16)
        maskb = sb("maskb", [P, P], BF16)
        since = sb("since", [P, 7 * P])
        selall = sb("selall", [P, FOX_H + DIFF_H])
        alpha = sb("alpha", [P, 1])
        idle = sb("idle", [P, 10])
        free = sb("free", [P, 8])
        eps = sb("eps", [P, 1])
        qscale = sb("qscale", [P, BODIES])
        half = sb("half", [P, 4 * DIFF_H])
        brow = sb("brow", [P, S], F32R)
        sel = sb("sel", [P, 2, P], F32R)
        st = sb("st", [P, NT, 2, 6])
        mv = sb("mv", [P, NT, 2])
        ve = sb("ve", [P, NT])
        rstd = sb("rstd", [P, NT])
        nmr0 = sb("nmr0", [P, NT])
        mone = sb("mone", [P, 1])
        nmr = sb("nmr", [P, NT])
        gst = sb("gst", [P, NT, 6])
        gmv = sb("gmv", [P, NT, 2])
        gve = sb("gve", [P, NT])
        grs = sb("grs", [P, NT])
        flog = sb("flog", [P, NT, FOX_H])
        fneg = sb("fneg", [P, NT, FOX_H])
        fexp = sb("fexp", [P, NT, FOX_H])
        fln = sb("fln", [P, NT, FOX_H])
        lf = sb("lf", [P, NT, FOX_H])
        negm = sb("negm", [P, 4])
        olo = sb("olo", [P, 2, HD])
        rsum = sb("rsum", [P, 4])
        rinv = sb("rinv", [P, STEPS, 2])
        wlam = sb("wlam", [P, STEPS])
        lamp = sb("lamp", [P, L, 2, 2, 32])
        lams = sb("lams", [P, L, 2])
        lame = sb("lame", [P, L, 2])
        nlam = sb("nlam", [P, L])
        olam = sb("olam", [P, L])
        ilam = sb("ilam", [P, L])
        nlam1 = sb("nlam1", [P, 1])
        sq = sb("sq", [P, NT, 2 * HD])
        dms = sb("dms", [P, NT * DIFF_H])
        dve_ = sb("dve_", [P, NT * DIFF_H])
        drs = sb("drs", [P, NT * DIFF_H])

        landed = {s: sem(f"landed_{s}") for s in "ABD"}
        hi_ok = {s: sem(f"hi_ok_{s}") for s in "ABD"}
        lo_ok = {s: sem(f"lo_ok_{s}") for s in "ABD"}
        used = {s: sem(f"used_{s}") for s in "AB"}
        x_landed = sem("x_landed")
        x2_landed = sem("x2_landed")
        gbr_landed = sem("gbr_landed")
        gbc_landed = sem("gbc_landed")
        mix_landed = sem("mix_landed")
        ws_landed = sem("ws_landed")
        lam_landed = sem("lam_landed")
        const_ok = sem("const_ok")
        pos_ok = sem("pos_ok")
        za_ok = sem("za_ok")
        zd_ok = sem("zd_ok")
        ident_ok = sem("ident_ok")
        res_ok = sem("res_ok")
        rs_step = sem("rs_step")
        turned = sem("turned")
        x32_ok = sem("x32_ok")
        xhi_ok = sem("xhi_ok")
        x_ok = sem("x_ok")
        silu_ok = {s: sem(f"silu_ok_{s}") for s in "AB"}
        h32_ok = {s: sem(f"h32_ok_{s}") for s in "AB"}
        hhi_ok = {s: sem(f"hhi_ok_{s}") for s in "AB"}
        h_ok = {s: sem(f"h_ok_{s}") for s in "AB"}
        y_done = sem("y_done")
        y_free = sem("y_free")
        st_ok = sem("st_ok")
        mv_ok = sem("mv_ok")
        ve_ok = sem("ve_ok")
        rstd_ok = sem("rstd_ok")
        nmr_step = sem("nmr_step")
        nmr_ok = sem("nmr_ok")
        vhi_ok = sem("vhi_ok")
        nat_free = {s: sem(f"nat_free_{s}") for s in "AB"}
        f_ok = sem("f_ok")
        fneg_ok = sem("fneg_ok")
        fexp_ok = sem("fexp_ok")
        fln_ok = sem("fln_ok")
        lf_ok = sem("lf_ok")
        cum_done = sem("cum_done")
        chi_ok = sem("chi_ok")
        c_ok = sem("c_ok")
        ws_tri = sem("ws_tri")
        wshi_ok = sem("wshi_ok")
        wslo_ok = sem("wslo_ok")
        gst_ok = sem("gst_ok")
        gmv_ok = sem("gmv_ok")
        gve_ok = sem("gve_ok")
        grs_ok = sem("grs_ok")
        gn_ok = sem("gn_ok")
        gg_ok = sem("gg_ok")
        gb_ok = sem("gb_ok")
        ghi_ok = sem("ghi_ok")
        glo_ok = sem("glo_ok")
        sgu_done = sem("sgu_done")
        sgu_out = sem("sgu_out")
        q_done = sem("q_done")
        qhi_ok = sem("qhi_ok")
        khi_ok = sem("khi_ok")
        qk_ok = sem("qk_ok")
        qw_hi_ok = sem("qw_hi_ok")
        qw_ok = sem("qw_ok")
        yt_done = sem("yt_done")
        ythi_ok = sem("ythi_ok")
        yt_ok = sem("yt_ok")
        wo_done = sem("wo_done")
        wo_free = sem("wo_free")
        wo_b_done = sem("wo_b_done")
        s_done = [sem(f"s_done{m}") for m in range(2)]
        max_ok = [sem(f"max_ok{m}") for m in range(2)]
        exp_ok = [sem(f"exp_ok{m}") for m in range(2)]
        rinv_ok = sem("rinv_ok")
        wlam_ok = sem("wlam_ok")
        mixp_ok = sem("mixp_ok")
        pt_done = sem("pt_done")
        pthi_ok = sem("pthi_ok")
        pt_ok = sem("pt_ok")
        pv_done = sem("pv_done")
        olo_ok = sem("olo_ok")
        o_ok = sem("o_ok")
        sq_ok = sem("sq_ok")
        dms_ok = sem("dms_ok")
        dve_ok = sem("dve_ok")
        drs_ok = sem("drs_ok")
        dn_ok = sem("dn_ok")
        dgs_ok = sem("dgs_ok")
        y_ok = sem("y_ok")
        lam_step = sem("lam_step")
        lame_ok = sem("lame_ok")
        ilam_ok = sem("ilam_ok")
        nlam1_ok = sem("nlam1_ok")
        fin_step = sem("fin_step")
        fin_ok = sem("fin_ok")
        fin_pool = sem("fin_pool")
        out_done = sem("out_done")

        wsr = s32[:, 0:2, :].rearrange("p a n -> p (a n)")[:, 0:SGU_H * P]
        hlf = hl[:, :, :].rearrange("p a n -> p (a n)")
        ghi = hlf[:, 0:NT * SGU_W].rearrange("p (t n) -> p t n", t=NT)
        glo = hlf[:, NT * SGU_W:2 * NT * SGU_W].rearrange("p (t n) -> p t n", t=NT)
        wshi = hlf[:, 2 * NT * SGU_W:2 * NT * SGU_W + SGU_H * P]
        wslo = hlf[:, 2 * NT * SGU_W + SGU_H * P:2 * NT * SGU_W + 2 * SGU_H * P]
        x32 = [s32[:, c // 2, (c % 2) * HALF:(c % 2) * HALF + HALF] for c in range(NC)]
        vhi, vlo = vals[:, :, 0, :], vals[:, :, 1, :]
        silu = {"A": s32[:, 0, :], "B": s32[:, 1, :]}
        h32 = {"A": s32[:, 2, :], "B": s32[:, 3, :]}
        hhi = {"A": hl[:, 0, :], "B": hl[:, 2, :]}
        hlo = {"A": hl[:, 1, :], "B": hl[:, 3, :]}
        qhi, qlo, khi, klo = (hl[:, i, :] for i in range(4))
        pthi = [hl[:, 4, :], hl[:, 5, :]]
        ptlo = [hl[:, 6, :], hl[:, 7, :]]
        diff_g = mixr[:, 0:DIFF_W]
        sgu_g = mixr[:, DIFF_W:DIFF_W + SGU_W]
        sgu_b = mixr[:, DIFF_W + SGU_W:DIFF_W + 2 * SGU_W]
        f_bias = mixr[:, DIFF_W + 2 * SGU_W:]
        Y_DIFF, Y_SGU = FOX_W, FOX_W + DIFF_W
        block = ctx.enter_context(nc.Block())

        @block.sync
        def _(sp):
            w_in_dram = {"A": a_w, "B": b_w, "D": d_w}

            def fill(s, n):
                if isinstance(n, int) and n == 0:
                    sp.dma_start(raw[s][:, :], w_in_dram[s][0, :, :]).then_inc(landed[s], 16)
                    return
                sp.wait_ge(lo_ok[s], n)
                sp.dma_start(raw[s][:, :], w_in_dram[s][bass.ds(n, 1), :, :].rearrange("a p n -> (a p) n")).then_inc(landed[s], 16)

            def norm_columns(q):
                sp.dma_start(gbc[:, :, :], gb_col[bass.ds(q, 1), :, :, :].rearrange("a p g c -> (a p) g c")).then_inc(gbc_landed, 16)

            def norm_rows(q):
                sp.dma_start(gbr[:, :, :], gb_row[bass.ds(q, 1), :, :].broadcast_to([P, 2, D])).then_inc(gbr_landed, 16)

            def norm_params(q):
                norm_columns(q)
                norm_rows(q)

            def ffn(l, f):
                a0 = l * A_ALL + (A_FFN2 if f else A_FFN)
                b0 = l * B_ALL + (B_FFN2 if f else B_FFN)
                with sp.Fori(0, NPAIR - 1) as i:
                    fill("A", a0 + i + 1)
                    fill("B", b0 + i + 1)
                    fill("D", l * D_ALL + f * D_FFN2 + i + 1)
                fill("A", a0 + NPAIR)
                q = 3 * l + 2 * f
                sp.wait_ge(x32_ok, (q + 1) * 2 * NC)
                sp.wait_ge(res_ok, q + 1)
                norm_params(q + 1)

            sp.dma_start(lamp[:, :, :, :, :], lamv.broadcast_to([P, L, 2, 2, 32])).then_inc(lam_landed, 16)
            sp.dma_start(nat[:, 0:2, :], x_in[:, 0:2, :]).then_inc(x_landed, 16)
            fill("A", 0)
            norm_columns(0)
            sp.dma_start(res[:, 2:4, :], x_in[:, 2:4, :]).then_inc(x2_landed, 16)
            norm_rows(0)
            with sp.Fori(0, L) as l:
                fill("B", l * B_ALL)
                fill("D", l * D_ALL)
                sp.wait_ge(y_ok, l)
                sp.dma_start(mixr[:, :], mix_row[bass.ds(l, 1), :].broadcast_to([P, mix_row.shape[1]])).then_inc(mix_landed, 16)
                sp.dma_start(mixc[:, :], mix_col[bass.ds(l, 1), :, :].rearrange("a p n -> (a p) n")).then_inc(mix_landed, 16)
                ffn(l, 0)
                fill("B", l * B_ALL + B_NAT)
                fill("D", l * D_ALL + D_WO)
                sp.wait_ge(x_ok, (3 * l + 2) * 2 * NC)
                sp.dma_start(wsr, ws_in[bass.ds(l, 1), :, :].rearrange("a p n -> (a p) n")).then_inc(ws_landed, 16)
                for j in range(NPROJ):
                    fill("A", l * A_ALL + A_NAT + j + 1)
                    fill("B", l * B_ALL + B_NAT + j + 1)
                sp.wait_ge(res_ok, 3 * l + 2)
                sp.wait_ge(x32_ok, (3 * l + 2) * 2 * NC)
                norm_params(3 * l + 2)
                fill("A", l * A_ALL + A_QK + 1)
                fill("B", l * B_ALL + B_WO + 1)
                fill("D", l * D_ALL + D_FFN2)
                for p in range(1, BODIES):
                    fill("A", l * A_ALL + A_QK + p + 1)
                fill("A", l * A_ALL + A_FFN2)
                fill("B", l * B_ALL + B_FFN2)
                ffn(l, 1)
            for n, t in enumerate((1, 2, 3, 0)):
                if t == 0:
                    sp.wait_ge(fin_pool, 2)
                else:
                    sp.wait_ge(fin_ok, n + 1)
                sp.dma_start(out[:, t, :], nat[:, t, :]).then_inc(out_done, 16)
            sp.wait_ge(out_done, 16 * NT)

        @block.gpsimd
        def _(pool):
            g = nc.gpsimd
            n = 0

            def done(ins):
                nonlocal n
                n += 1
                ins.then_inc(const_ok, 1)

            g.memset(ident[:, :], 0.0).then_inc(ident_ok, 1)
            pool.wait_ge(ident_ok, 1)
            g.affine_select(out=ident[:, :], in_=ident[:, :], compare_op=ALU.not_equal, fill=1.0, base=0,
                            pattern=[[-1, P]], channel_multiplier=1).then_inc(ident_ok, 1)
            done(g.memset(identb[:, :], 0.0))
            done(g.memset(maskb[:, :], 0.0))
            done(g.memset(since[:, :], 1.0))
            done(g.memset(selall[:, :], 0.0))
            done(g.memset(half[:, :], -0.5))
            done(g.memset(alpha[:, :], ALPHA))
            done(g.memset(eps[:, :], EPS))
            done(g.memset(mone[:, :], -1.0))
            done(g.memset(brow[:, :].bitcast(F32), 0.0))
            done(g.memset(mv[:, :, :], 0.0))
            g.memset(rstd[:, :], 1.0).then_inc(rstd_ok, NT)
            g.memset(nmr[:, :], 0.0).then_inc(nmr_ok, NT)
            for l in range(L):
                done(g.memset(olam[:, l:l + 1], 1.0 - LAM_INIT[l]))
                done(g.memset(ilam[:, l:l + 1], LAM_INIT[l]))
            for p in range(BODIES):
                done(g.memset(qscale[:, p:p + 1], HD ** -0.5 if p < FOX_P else (HD // 2) ** -0.5))
            pool.wait_ge(const_ok, n)
            done(g.affine_select(out=identb[:, :], in_=identb[:, :], compare_op=ALU.not_equal, fill=1.0, base=0,
                                 pattern=[[-1, P]], channel_multiplier=1))
            done(g.affine_select(out=maskb[:, :], in_=maskb[:, :], compare_op=ALU.is_ge, fill=NEG, base=0,
                                 pattern=[[-1, P]], channel_multiplier=1))
            done(g.affine_select(out=since[:, :], in_=since[:, :], compare_op=ALU.is_ge, fill=0.0, base=-3 * P,
                                 pattern=[[1, 7 * P]], channel_multiplier=-1))
            for r in (0, 32):
                pool.wait_ge(const_ok, n)
                v = selall[r:r + 32, 0:FOX_H]
                done(g.affine_select(out=v, in_=v, compare_op=ALU.not_equal, fill=-1.0, base=0,
                                     pattern=[[-1, FOX_H]], channel_multiplier=1))
            pool.wait_ge(const_ok, n)
            for h in range(DIFF_H):
                done(g.memset(selall[64:65, FOX_H + h:FOX_H + h + 1], SLOPES[h]))
            g.iota(s32[64:65, 0, :], pattern=[[1, S]], base=0, channel_multiplier=0,
                   allow_small_or_imprecise_dtypes=True).then_inc(pos_ok, 1)
            assert n == CONSTS
            pool.wait_ge(pos_ok, 1)

            def wait_here():
                g.tensor_tensor(idle[:, 1:2], eps[:, :], eps[:, :], ALU.add)

            def scale_gain(q):
                pool.wait_ge(gbr_landed, 16 * q + 16)
                for w in range(2):
                    g.tensor_tensor(gbr[:, w, :], gbr[:, w, :], alpha[:, :].broadcast_to([P, D]), ALU.mult).then_inc(rs_step, 1)

            def residual(l, j):
                q = 3 * l + j
                s0 = q * 10
                pool.wait_ge(rs_step, s0 + 2)
                pool.wait_ge(za_ok, 3 * q + 3)
                pool.wait_ge(zd_ok, q + 1)
                for t in range(NT):
                    g.tensor_tensor(res[:, t, :], nat[:, t, :], gbr[:, 0, :], ALU.mult).then_inc(rs_step, 1)
                for t in range(NT):
                    pool.wait_ge(rs_step, s0 + 3 + t)
                    ins = g.tensor_tensor(res[:, t, :], res[:, t, :], gbr[:, 1, :], ALU.add)
                    ins.then_inc(*((rs_step, 1) if t < NT - 1 else (res_ok, 1)))
                g.memset(idle[:, 2:3], 0.0).then_inc(rs_step, 1)

            def root(v, out_, in_, step, k, ready, n_):
                g.tensor_tensor(v, in_, eps[:, :].broadcast_to([P, n_]), ALU.add).then_inc(step, 1)
                pool.wait_ge(step, k)
                g.tensor_tensor(out_, v, half[:, 0:n_], ALU.pow).then_inc(ready, 1)

            def norm(l, j):
                q = 3 * l + j
                for h in range(NT):
                    t = slice(h, h + 1)
                    pool.wait_ge(mv_ok, NT * q + h + 1)
                    root(ve[:, t], rstd[:, t], mv[:, t, 1], ve_ok, NT * q + h + 1, rstd_ok, 1)
                    pool.wait_ge(rstd_ok, NT * q + h + 5)
                    g.tensor_tensor(nmr0[:, t], mv[:, t, 0], rstd[:, t], ALU.mult).then_inc(nmr_step, 1)
                    pool.wait_ge(nmr_step, NT * q + h + 1)
                    g.tensor_tensor(nmr[:, t], nmr0[:, t], mone[:, :], ALU.mult).then_inc(nmr_ok, 1)

            pool.wait_ge(x_landed, 16)
            wait_here()
            with pool.Fori(0, L) as l:
                scale_gain(3 * l)
                residual(l, 0)
                scale_gain(3 * l + 1)
                norm(l, 0)
                residual(l, 1)
                pool.wait_ge(ws_landed, 16 * l + 16)
                wait_here()
                g.affine_select(out=wsr, in_=wsr, compare_op=ALU.is_ge, fill=0.0, base=0,
                                pattern=[[0, SGU_H], [1, P]], channel_multiplier=-1).then_inc(ws_tri, 1)
                pool.wait_ge(gmv_ok, NT * l + NT)
                root(gve[:, :], grs[:, :], gmv[:, :, 1], gve_ok, l + 1, grs_ok, NT)
                with pool.Fori(0, BODIES) as b:
                    for h, (ready, done_) in enumerate(((qw_hi_ok, qw_ok), (hi_ok["A"], lo_ok["A"]))):
                        pool.wait_ge(ready, (l * BODIES if h == 0 else l * A_ALL + A_QK + 1) + b + 1)
                        c = slice(h * D, h * D + D)
                        g.tensor_tensor(wlo["A"][:, c], raw["A"][:, c], whi["A"][:, c].bitcast(F32),
                                        ALU.subtract).then_inc(done_, 1)
                for p in range(DIFF_P):
                    c = slice(p * STEPS, p * STEPS + STEPS)
                    pool.wait_ge(dms_ok, l * DIFF_P + p + 1)
                    root(dve_[:, c], drs[:, c], dms[:, c], dve_ok, l * DIFF_P + p + 1, drs_ok, STEPS)
                scale_gain(3 * l + 2)
                pool.wait_ge(hi_ok["A"], l * A_ALL + A_FFN2 + 1)
                g.tensor_tensor(wlo["A"][:, :], raw["A"][:, :], whi["A"][:, :].bitcast(F32),
                                ALU.subtract).then_inc(lo_ok["A"], 1)
                norm(l, 1)
                residual(l, 2)
                norm(l, 2)
            pool.wait_ge(gbr_landed, 16 * 3 * L + 16)
            pool.wait_ge(za_ok, 3 * 3 * L + 1)
            g.tensor_tensor(nat[:, 0, :], nat[:, 0, :], gbr[:, 0, :], ALU.mult).then_inc(fin_pool, 1)
            pool.wait_ge(fin_pool, 1)
            g.tensor_tensor(nat[:, 0, :], nat[:, 0, :], gbr[:, 1, :], ALU.add).then_inc(fin_pool, 1)

        @block.scalar
        def _(act):
            a = nc.scalar

            def split(s, n):
                act.wait_ge(landed[s], n * 16 + 16)
                a.activation(whi[s][:, :], raw[s][:, :], ACT.Copy).then_inc(hi_ok[s], 1)

            def split_half(n, h, step):
                if h == 0:
                    act.wait_ge(landed["A"], n * 16 + 16)
                t = slice(h * D, h * D + D)
                a.activation(whi["A"][:, t], raw["A"][:, t], ACT.Copy).then_inc(step, 1)

            def turn_z(q, b_fill):
                act.wait_ge(gbc_landed, 16 * q + 16)
                for h in range(2):
                    for c in range(NC):
                        act.wait_ge(turned, q * NC + h * NT + c // 2 + 1)
                        if h == 1:
                            act.wait_ge(x_ok, q * 2 * NC + c + 1)
                        b = bank[HALF_BANKS[h][c // 2]]
                        a.activation(x32[c], b[:, (c % 2) * HALF:(c % 2) * HALF + HALF], ACT.Identity, bias=gbc[:, 1, c:c + 1],
                                     scale=gbc[:, 0, c:c + 1]).then_inc(x32_ok, 1)
                    if h == 0:
                        act.wait_ge(x2_landed, 16)
                        normalise(q, (2,))
                        split("B", b_fill)

            def normalise(q, tiles):
                for t in tiles:
                    act.wait_ge(nmr_ok, NT * q + t + 1)
                    a.activation(nat[:, t, :], res[:, t, :], ACT.Identity, bias=nmr[:, t:t + 1],
                                 scale=rstd[:, t:t + 1]).then_inc(za_ok, 1)

            def ffn(l, f):
                turn_z(3 * l + 2 * f, l * B_ALL + f * B_FFN2)

                def pair(i, last):
                    it = l * 2 * NPAIR + f * NPAIR + i
                    y = l * Y_ALL + f * Y_FFN2 + i
                    act.wait_ge(y_done, y * 8)
                    split("D", l * D_ALL + f * D_FFN2 + i)
                    act.wait_ge(used["A"], l * AU_ALL + f * AU_FFN2 + i + 1)
                    a.activation(silu["A"], bank[0][:, :], ACT.Silu).then_inc(silu_ok["A"], 1)
                    split("A", l * A_ALL + f * A_FFN2 + i + 1)
                    act.wait_ge(h32_ok["A"], it + 1)
                    a.activation(hhi["A"], h32["A"], ACT.Copy).then_inc(hhi_ok["A"], 1)
                    act.wait_ge(used["B"], l * BU_ALL + f * BU_FFN2 + i + 1)
                    for h in range(2):
                        a.activation(silu["B"][:, h * 256:h * 256 + 256], bank[2][:, h * 256:h * 256 + 256],
                                     ACT.Silu).then_inc(silu_ok["B"], 1)
                    for h in range(2):
                        act.wait_ge(h32_ok["B"], it * 2 + h + 1)
                        a.activation(hhi["B"][:, h * 256:h * 256 + 256], h32["B"][:, h * 256:h * 256 + 256],
                                     ACT.Copy).then_inc(hhi_ok["B"], 1)
                    if not last:
                        split("B", l * B_ALL + f * B_FFN2 + i + 1)

                with act.Fori(0, NPAIR - 1) as i:
                    pair(i, False)
                pair(NPAIR - 1, True)
                normalise(3 * l + 2 * f + 1, (0, 1))

            act.wait_ge(lam_step, 2)
            a.activation(lame[:, :, :], lams[:, :, :], ACT.Exp).then_inc(lame_ok, 1)
            act.wait_ge(pos_ok, 2)
            split("A", 0)
            with act.Fori(0, L) as l:
                ffn(l, 0)
                turn_z(3 * l + 1, l * B_ALL + B_NAT)
                for j in range(NPROJ):
                    for s in "AB":
                        k = 2 * j + (s == "B")
                        if s == "A":
                            act.wait_ge(used["A"], l * AU_ALL + A_NAT + j + 1)
                        else:
                            act.wait_ge(used["B"], l * BU_ALL + B_NAT + j + 1)
                        if s == "A":
                            split(s, l * A_ALL + A_NAT + j + 1)
                        elif j < NPROJ - 1:
                            split(s, l * B_ALL + B_NAT + j + 1)
                        if k == 0:
                            act.wait_ge(res_ok, 3 * l + 2)
                        for t in range(NT):
                            src = bank[t + (4 if s == "B" else 0)]
                            if k == 0:
                                a.activation(nat[:, t, Y_SGU:Y_SGU + 256], src[:, 0:256], ACT.Gelu_apprx_tanh).then_inc(nat_free[s], 1)
                            elif k == 1:
                                a.activation(nat[:, t, Y_SGU + 256:Y_SGU + SGU_W], src[:, 0:128], ACT.Gelu_apprx_tanh)
                                a.activation(nat[:, t, 0:128], src[:, 128:256], ACT.Gelu_apprx_tanh).then_inc(nat_free[s], 1)
                            elif k == 2:
                                a.activation(nat[:, t, 128:SGU_W], src[:, 0:256], ACT.Gelu_apprx_tanh).then_inc(nat_free[s], 1)
                            elif k == 3:
                                a.activation(vhi[:, t, 0:256], src[:, 0:256], ACT.Copy).then_inc(vhi_ok, 1)
                            elif k == 4:
                                a.activation(vhi[:, t, 256:FOX_W], src[:, 0:FOX_W - 256], ACT.Copy).then_inc(vhi_ok, 1)
                            else:
                                a.activation(vhi[:, t, FOX_W:FOX_W + DIFF_W], src[:, 0:256], ACT.Copy).then_inc(vhi_ok, 1)
                        if k == 2:
                            act.wait_ge(ws_tri, l + 1)
                            a.activation(wshi, wsr, ACT.Copy).then_inc(wshi_ok, 1)
                        if k == 4:
                            act.wait_ge(fneg_ok, l + 1)
                            a.activation(fexp[:, :, :], fneg[:, :, :], ACT.Exp).then_inc(fexp_ok, 1)
                            act.wait_ge(fexp_ok, l + 1)
                            a.activation(fln[:, :, :], fexp[:, :, :], ACT.Ln, bias=1.0).then_inc(fln_ok, 1)
                            act.wait_ge(gb_ok, NT * l + NT)
                            a.activation(ghi, nat[:, :, 0:SGU_W], ACT.Copy).then_inc(ghi_ok, 1)
                act.wait_ge(cum_done, l + 1)
                a.activation(brow[0:FOX_H, :], bank[0][0:FOX_H, :], ACT.Copy).then_inc(chi_ok, 1)

                split("B", l * B_ALL + B_WO)
                act.wait_ge(y_done, (l * Y_ALL + Y_WO) * 8)
                split("D", l * D_ALL + D_WO)

                def query(body, b):
                    act.wait_ge(q_done, body + 1)
                    a.activation(qhi, bank[6][:, :], ACT.Copy, scale=qscale[:, bass.ds(b, 1)]).then_inc(qhi_ok, 1)

                def key(b):
                    act.wait_ge(used["A"], l * AU_ALL + A_QK + b + 1)
                    a.activation(khi, bank[7][:, :], ACT.Copy).then_inc(khi_ok, 1)

                def heads(b, d, carry, last):
                    body = l * BODIES + b
                    K = body * STEPS
                    maps = 1 if d is None else 2
                    KD = None if d is None else (l * DIFF_P + d) * STEPS

                    def exp(k):
                        for m in range(maps):
                            act.wait_ge(max_ok[m], (K if m == 0 else KD) + k + 1)
                            if k >= 2 or carry:
                                act.wait_ge(pt_done, K + k - 1)
                            w = (k % NT + 1) * P
                            i = 2 * (k % 2) + m
                            a.activation(s32[:, i, 0:w], bank[i][:, 0:w], ACT.Exp, bias=negm[:, i:i + 1],
                                         accum_out=rsum[:, i:i + 1]).then_inc(exp_ok[m], 1)

                    def p_hi(k):
                        w = (k % NT + 1) * P
                        act.wait_ge(pt_done, K + k + 1)
                        if k >= 2 or carry:
                            act.wait_ge(pv_done, K + k - 1)
                        a.activation(pthi[k % 2][:, 0:w], bank[4 + k % 2][:, 0:w], ACT.Copy).then_inc(pthi_ok, 1)

                    if not carry:
                        act.wait_ge(pv_done, K)
                    for k in range(STEPS):
                        if k == STEPS - 1 and not last:
                            act.wait_ge(s_done[maps - 1], (K if maps == 1 else KD) + k + 1)
                            query(body + 1, b + 1)
                            p_hi(k - 1)
                            exp(k)
                            key(b + 1)
                            continue
                        if k == 0 and carry:
                            p_hi(-1)
                        exp(k)
                        if last and k < len(EARLY) // 2:
                            y_hi(2 * k)
                        if k >= 1:
                            p_hi(k - 1)
                        if last and k < len(EARLY) // 2:
                            y_hi(2 * k + 1)
                        if k == 0:
                            split_half(l * A_ALL + A_QK + b + 1, 1, hi_ok["A"])
                        if k == 4 and not last:
                            act.wait_ge(q_done, body + 2)
                            split_half(l * A_ALL + A_QK + b + 2, 0, qw_hi_ok)
                    if last:
                        p_hi(STEPS - 1)

                def y_hi(i):
                    act.wait_ge(yt_done, l * NC + i + 1)
                    c = ([e[0] for e in EARLY] + LATE)[i]
                    b = 6 + i % 2 if i < len(EARLY) else i - len(EARLY)
                    a.activation(xhi[:, c, :], bank[b][:, :], ACT.Copy).then_inc(ythi_ok, 1)

                query(l * BODIES, 0)
                split_half(l * A_ALL + A_QK + 1, 0, qw_hi_ok)
                key(0)
                heads(0, None, False, False)
                with act.Fori(0, FOX_P - 1) as p:
                    heads(p + 1, None, True, False)
                for d in range(DIFF_P):
                    heads(FOX_P + d, d, True, d == DIFF_P - 1)
                act.wait_ge(wo_b_done, l + 1)
                split("B", l * B_ALL + B_WO + 1)
                for i in range(len(LATE)):
                    y_hi(len(EARLY) + i)
                act.wait_ge(wo_done, l * 8 + 8)
                split("A", l * A_ALL + A_FFN2)
                normalise(3 * l + 2, (0, 1))
                ffn(l, 1)

        @block.tensor
        def _(pe):
            t_ = nc.tensor

            def product(out_, pairs, start=True, stop=True, check=False):
                n = 3 * len(pairs)
                k = 0
                for (shi, slo), (mhi, mlo) in pairs:
                    for a_, b_ in ((shi, mhi), (shi, mlo), (slo, mhi)):
                        k += 1
                        ins = t_.matmul(out_, a_, b_, start=(start and k == 1), stop=(stop and k == n), skip_group_check=check)
                return ins

            def w(s, lo, n):
                return whi[s][:, lo:lo + n], wlo[s][:, lo:lo + n]

            def x(c, lo=0, n=S):
                return xhi[:, c, lo:lo + n], xlo[:, c, lo:lo + n]

            def turn_z(q, h, y):
                for t in range(2):
                    if h == 0:
                        pe.wait_ge(za_ok, 3 * q + t + 1)
                    elif t == 0:
                        pe.wait_ge(za_ok, 3 * q + 3)
                    else:
                        pe.wait_ge(zd_ok, q + 1)
                    for i in range(NT):
                        b = HALF_BANKS[h][i]
                        if t == 0 and (b >= 6 or h == 0 and b >= 4):
                            pe.wait_ge(y_free, y * 8 + b - 3)
                        elif t == 0 and h == 1:
                            pe.wait_ge(x32_ok, q * 2 * NC + 2 * i + 2)
                        for c in (2 * i, 2 * i + 1):
                            lo = (c % 2) * HALF + t * P
                            ins = t_.transpose(bank[b][:, lo:lo + P], nat[:, 2 * h + t, c * P:c * P + P], ident[:, :])
                        if t == 1:
                            ins.then_inc(turned, 1)

            def first(q, y, n, chunk):
                for h in range(2):
                    if h == 0:
                        turn_z(q, 0, y)
                        pe.wait_ge(lo_ok["A"], n + 1)
                    for c in range(NC):
                        if h == 0 and c == NC - 2:
                            turn_z(q, 1, y)
                        pe.wait_ge(x_ok, q * 2 * NC + h * NC + c + 1)
                        ins = chunk(h, c)
                ins.then_inc(used["A"], 1)

            def outputs(y, parts, bank_free=None):
                def part(o, n):
                    stat, slot, off, _ = parts[n]
                    t, hf = divmod(o, 2)
                    if n == 0:
                        pe.wait_ge(y_free, y * 8 + o + 1)
                        if bank_free and o < 4:
                            bank_free(4 + o)
                    ins = product(bank[4 + o % 4][:, :], [(stat(t), w(slot, off + hf * 512, 512))],
                                  start=(n == 0), stop=(n == 1))
                    if n == 1:
                        ins.then_inc(y_done, 1)

                for n in range(2):
                    parts[n][3](0)
                    for o in range(4):
                        part(o, n)
                for n in range(2):
                    parts[n][3](1)
                for o in range(4, 8):
                    part(o, 0)
                    part(o, 1)

            def ffn(l, f):
                def gate_up(s, i, halved=False):
                    n = l * A_ALL + f * A_FFN2 + i if s == "A" else l * B_ALL + f * B_FFN2 + i
                    it = l * 2 * NPAIR + f * NPAIR + i
                    b = 0 if s == "A" else 2

                    def chunk(h, c):
                        lo, n_ = (0, S) if h is None else (h * HALF, HALF)
                        for g in range(2):
                            ins = product(bank[b + g][:, lo:lo + n_], [(w(s, (g * NC + c) * P, P), x(c, lo, n_))],
                                          start=(c == 0), stop=(c == NC - 1))
                        return ins

                    pe.wait_ge(h32_ok[s], it if s == "A" else it * 2)
                    if halved:
                        first(3 * l + 2 * f, l * Y_ALL + f * Y_FFN2, n, chunk)
                    else:
                        pe.wait_ge(lo_ok[s], n + 1)
                        for c in range(NC):
                            ins = chunk(None, c)
                        ins.then_inc(used[s], 1)

                def down(i):
                    it = l * 2 * NPAIR + f * NPAIR + i
                    pe.wait_ge(lo_ok["D"], l * D_ALL + f * D_FFN2 + i + 1)
                    waits = {"A": lambda r: pe.wait_ge(h_ok["A"], it + 1) if r == 0 else None,
                             "B": lambda r: pe.wait_ge(h_ok["B"], it * 2 + r + 1)}
                    outputs(l * Y_ALL + f * Y_FFN2 + i,
                            [(lambda t, s=s: (hhi[s][:, t * P:t * P + P], hlo[s][:, t * P:t * P + P]), "D", k * D, waits[s])
                             for k, s in enumerate("AB")])

                gate_up("A", 0, True)
                with pe.Fori(0, NPAIR - 1) as i:
                    gate_up("B", i)
                    down(i)
                    gate_up("A", i + 1)
                gate_up("B", NPAIR - 1)
                down(NPAIR - 1)

            def project(l, b):
                n = l * A_ALL + A_QK + b
                for g in range(2):
                    if g == 0 and not (isinstance(b, int) and b == 0):
                        pe.wait_ge(qw_ok, l * BODIES + b)
                    else:
                        pe.wait_ge(lo_ok["A"], n + 1)
                    k = 0
                    for c in range(NC):
                        (shi, slo), (mhi, mlo) = w("A", (g * NC + c) * P, P), x(c)
                        for a_, b_ in ((shi, mhi), (shi, mlo), (slo, mhi)):
                            k += 1
                            ins = t_.matmul(bank[6 + g][:, :], a_, b_, start=(k == 1), stop=(k == 3 * NC))
                            if k == 3 * NC:
                                ins.then_inc(*((used["A"], 1) if g else (q_done, 1)))
                            yield

            def turn_y(l, i):
                early = i < len(EARLY)
                c = EARLY[i][0] if early else LATE[i - len(EARLY)]
                if early and i >= 2:
                    pe.wait_ge(yt_ok, l * NC + i - 1)
                b = 6 + i % 2 if early else i - len(EARLY)
                for t in range(NT):
                    ins = t_.transpose(bank[b][:, t * P:t * P + P], nat[:, t, c * P:c * P + P], ident[:, :])
                ins.then_inc(yt_done, 1)

            def early_output(l, u, parts):
                t, hf = divmod(u, 2)
                for n in parts:
                    c, s, off = EARLY[n]
                    if n == 0 and u >= 2:
                        pe.wait_ge(wo_free, l * 8 + u - 1)
                    ins = product(bank[6 + u % 2][:, :], [(x(c, t * P, P), w(s, off + hf * 512, 512))],
                                  start=(n == 0), stop=(n == len(EARLY) - 1))
                if n == len(EARLY) - 1:
                    ins.then_inc(wo_done, 1)

            def early(l):
                for i in range(len(EARLY)):
                    turn_y(l, i)
                    yield
                pe.wait_ge(yt_ok, l * NC + len(EARLY))
                pe.wait_ge(lo_ok["A"], l * A_ALL + A_WO + 1)
                pe.wait_ge(lo_ok["B"], l * B_ALL + B_WO + 1)
                pe.wait_ge(lo_ok["D"], l * D_ALL + D_WO + 1)
                for u in range(AMONG):
                    for h in range(2):
                        early_output(l, u, range(3 * h, 3 * h + 3))
                        yield

            def heads(l, b, d, carry, last):
                body = l * BODIES + b
                K = body * STEPS
                maps = 1 if d is None else 2
                KD = None if d is None else (l * DIFF_P + d) * STEPS
                rows = HD // maps

                def scores(k):
                    hh, t = divmod(k, NT)
                    n_ = (t + 1) * P
                    for m in range(maps):
                        i = 2 * (k % 2) + m
                        if k >= 2 or (carry and (m == 0 or d > 0)):
                            pe.wait_ge(exp_ok[m], (K if m == 0 else KD) + k - 1)
                        r = hh * HD + m * rows
                        product(bank[i][:, 0:n_], [((qhi[r:r + rows, t * P:t * P + P], qlo[r:r + rows, t * P:t * P + P]),
                                                    (khi[r:r + rows, 0:n_], klo[r:r + rows, 0:n_]))], stop=False)
                        t_.matmul(bank[i][:, 0:n_], sel[0:65, hh, :], brow[0:65, 0:n_], start=False, stop=False)
                        t_.matmul(bank[i][:, t * P:n_], identb[:, :], maskb[:, :], start=False, stop=True).then_inc(s_done[m], 1)

                def turn_p(k):
                    t = k % NT
                    if maps == 1 or (k < 0 and d == 0):
                        pe.wait_ge(exp_ok[0], K + k + 1)
                    else:
                        pe.wait_ge(mixp_ok, KD + k + 1)
                    if k >= 2 or carry:
                        pe.wait_ge(o_ok, K + k - 1)
                    elif k == 0:
                        pe.wait_ge(o_ok, K)
                    for e in range(t + 1):
                        ins = t_.transpose(bank[4 + k % 2][:, e * P:e * P + P], s32[:, 2 * (k % 2), e * P:e * P + P], ident[:, :])
                    ins.then_inc(pt_done, 1)

                def values(k):
                    hh, t = divmod(k % STEPS, NT)
                    pe.wait_ge(pt_ok, K + k + 1)
                    vc = (b - 1 if k < 0 else b) * 2 * HD + hh * HD
                    both = bank[4 + k % 2][:, 0:2 * HD].rearrange("p (a n) -> p a n", a=2)
                    for e in range(t + 1):
                        t_.matmul(both, pthi[k % 2][:, e * P:e * P + P], vals[:, e, :, bass.ds(vc, HD)],
                                  start=(e == 0), stop=(e == t), skip_group_check=True)
                        ins = t_.matmul(both[:, 0, :], ptlo[k % 2][:, e * P:e * P + P], vhi[:, e, bass.ds(vc, HD)],
                                        start=False, stop=(e == t), skip_group_check=True)
                    ins.then_inc(pv_done, 1)

                between = early(l) if last else project(l, b + 1)

                def fill(i):
                    for _ in range(1 if last else FILL[i]):
                        next(between, None)

                for k in range(STEPS):
                    if k == 0:
                        if carry:
                            values(-2)
                            turn_p(-1)
                        else:
                            pe.wait_ge(qk_ok, body * 3 + 2)
                            fill(0)
                            fill(1)
                        pe.wait_ge(qk_ok, body * 3 + 3)
                        scores(0)
                        fill(0)
                        if carry:
                            fill(1)
                        continue
                    scores(k)
                    if k == STEPS - 1 and not last:
                        turn_p(k - 1)
                        values(k - 2)
                        for _ in between:
                            pass
                        continue
                    fill(0)
                    turn_p(k - 1)
                    fill(1)
                    if k >= 2 or carry:
                        values(k - 2)
                if last:
                    values(STEPS - 2)
                    turn_p(STEPS - 1)
                    early_output(l, AMONG, range(len(EARLY)))
                    values(STEPS - 1)

            pe.wait_ge(ident_ok, 2)
            pe.wait_ge(x_landed, 16)
            t_.transpose(bank[0][:, 0:P], ident[:, :], ident[:, :])
            with pe.Fori(0, L) as l:
                ffn(l, 0)
                def natural(s, j, halved=False):
                    def chunk(h, c):
                        for t in range(NT) if h is None else (2 * h, 2 * h + 1):
                            ins = product(bank[t + (4 if s == "B" else 0)][:, 0:256], [(x(c, t * P, P), w(s, c * 256, 256))],
                                          start=(c == 0), stop=(c == NC - 1))
                        return ins

                    n = (l * A_ALL + A_NAT if s == "A" else l * B_ALL + B_NAT) + j
                    pe.wait_ge(nat_free[s], l * NT * NPROJ + j * NT)
                    if halved:
                        first(3 * l + 1, l * Y_ALL + NPAIR, n, chunk)
                    else:
                        pe.wait_ge(lo_ok[s], n + 1)
                        for c in range(NC):
                            ins = chunk(None, c)
                        ins.then_inc(used[s], 1)

                natural("A", 0, True)
                with pe.Fori(0, NPROJ - 1) as j:
                    natural("B", j)
                    natural("A", j + 1)
                natural("B", NPROJ - 1)
                pe.wait_ge(nat_free["A"], l * NT * NPROJ + NT * NPROJ)
                pe.wait_ge(lf_ok, l + 1)
                for b in range(NT):
                    ins = t_.matmul(bank[0][0:FOX_H, :], lf[:, b, :], since[:, (3 - b) * P:(3 - b) * P + S],
                                    start=(b == 0), stop=(b == NT - 1))
                ins.then_inc(cum_done, 1)
                pe.wait_ge(wslo_ok, l + 1)
                pe.wait_ge(glo_ok, l + 1)
                for h in range(SGU_H):
                    o = bank[1 + h // 2][:, (h % 2) * 256:(h % 2) * 256 + 256].rearrange("p (c n) -> p c n", c=NT)
                    ins = product(o, [((wshi[:, h * P:h * P + P], wslo[:, h * P:h * P + P]),
                                       (ghi[:, :, h * HD:h * HD + HD], glo[:, :, h * HD:h * HD + HD]))])
                    if h % 2:
                        ins.then_inc(sgu_done, 1)
                pe.wait_ge(nat_free["B"], l * NT * NPROJ + NT * NPROJ)
                for _ in project(l, 0):
                    pass
                pe.wait_ge(const_ok, CONSTS)
                pe.wait_ge(sgu_out, l * SGU_H + SGU_H)
                pe.wait_ge(c_ok, l + 1)
                heads(l, 0, None, False, False)
                with pe.Fori(0, FOX_P - 1) as p:
                    heads(l, p + 1, None, True, False)
                for d in range(DIFF_P):
                    heads(l, FOX_P + d, d, True, d == DIFF_P - 1)
                for u in (6, 7):
                    early_output(l, u, range(2))
                t_.transpose(bank[2][:, 0:P], ident[:, :], ident[:, :]).then_inc(wo_b_done, 1)
                early_output(l, 6, range(2, len(EARLY)))
                pe.wait_ge(y_ok, l + 1)
                for i in range(len(LATE)):
                    turn_y(l, len(EARLY) + i)
                early_output(l, 7, range(2, len(EARLY)))
                pe.wait_ge(lo_ok["B"], l * B_ALL + B_WO + 2)
                pe.wait_ge(o_ok, (l + 1) * BODIES * STEPS)
                outputs(l * Y_ALL + Y_WO,
                        [(lambda t, c=c: x(c, t * P, P), "B", k * D,
                          lambda r, k=k: pe.wait_ge(yt_ok, l * NC + len(EARLY) + k + 1) if r == 0 else None)
                         for k, c in enumerate(LATE)],
                        lambda b: pe.wait_ge(wo_free, l * 8 + b + 1) if b >= 6 else None)
                ffn(l, 1)

        @block.vector
        def _(dve):
            v = nc.vector

            def f32(ap):
                return ap.bitcast(F32)

            def split(s, n):
                dve.wait_ge(hi_ok[s], n + 1)
                v.tensor_tensor(wlo[s][:, :], raw[s][:, :], f32(whi[s][:, :]), ALU.subtract).then_inc(lo_ok[s], 1)

            def half_chunk(q, h, c):
                n = q * 2 * NC + h * NC + c
                t = slice(h * HALF, h * HALF + HALF)
                if c < NC:
                    dve.wait_ge(x32_ok, n + 1)
                    v.tensor_copy(xhi[:, c, t], x32[c]).then_inc(xhi_ok, 1)
                if c >= 1:
                    dve.wait_ge(xhi_ok, n)
                    v.tensor_tensor(xlo[:, c - 1, t], x32[c - 1], f32(xhi[:, c - 1, t]), ALU.subtract).then_inc(x_ok, 1)

            def turn(q, b_fill, begun):
                for h in range(2):
                    for c in range(begun if h == 0 else 0, NC + 1):
                        half_chunk(q, h, c)
                        if h == 0 and c == 4:
                            dve.wait_ge(rstd_ok, NT * q + NT)
                            dve.wait_ge(x2_landed, 16)
                            last = NT - 1
                            v.tensor_scalar(nat[:, last, :], res[:, last, :], mv[:, last, 0:1], rstd[:, last:last + 1],
                                            ALU.subtract, ALU.mult).then_inc(zd_ok, 1)
                    if h == 0:
                        split("B", b_fill)

            def accumulate(o, b, scale, step):
                t, hf = divmod(o, 2)
                r = res[:, t, hf * 512:hf * 512 + 512]
                v.scalar_tensor_tensor(out=r, in0=bank[b][:, :], scalar=scale, in1=r,
                                       op0=ALU.mult, op1=ALU.add).then_inc(step, 1)

            def add(y, o, scale):
                dve.wait_ge(y_done, y * 8 + o + 1)
                accumulate(o, 4 + o % 4, scale, y_free)

            def add_outputs(y, scale):
                dve.wait_ge(y_free, y * 8 + 4)
                for o in range(8):
                    add(y, o, scale)

            def last_outputs(l, j, y, scale):
                q = 3 * l + j
                dve.wait_ge(y_free, y * 8 + 4)
                for half in range(2):
                    for i in range(5):
                        if i < 4:
                            add(y, 4 * half + i, scale)
                        if i >= 1:
                            o = 4 * half + i - 1
                            if half == 1 and i == 3 and j < 2:
                                half_chunk(q + 1, 0, 0)
                                half_chunk(q + 1, 0, 1)
                            t, hf = divmod(o, 2)
                            dve.wait_ge(y_free, y * 8 + 4 + o + 1)
                            v.bn_stats(st[:, t, hf, :], res[:, t, hf * 512:hf * 512 + 512]).then_inc(st_ok, 1)
                            if hf == 1:
                                dve.wait_ge(st_ok, q * 8 + o + 1)
                                wait_here(6 + t)
                                v.bn_aggr(mv[:, t, :], st[:, t, :, :].rearrange("p a n -> p (a n)")).then_inc(mv_ok, 1)

            def ffn(l, f):
                turn(3 * l + 2 * f, l * B_ALL + f * B_FFN2, 2 * f)

                def pair(i):
                    it = l * 2 * NPAIR + f * NPAIR + i
                    split("D", l * D_ALL + f * D_FFN2 + i)
                    dve.wait_ge(silu_ok["A"], it + 1)
                    dve.wait_ge(hhi_ok["A"], it)
                    v.tensor_tensor(h32["A"], silu["A"], bank[1][:, :], ALU.mult).then_inc(h32_ok["A"], 1)
                    split("A", l * A_ALL + f * A_FFN2 + i + 1)
                    dve.wait_ge(hhi_ok["A"], it + 1)
                    v.tensor_tensor(hlo["A"], h32["A"], f32(hhi["A"]), ALU.subtract).then_inc(h_ok["A"], 1)
                    for h in range(2):
                        t = slice(h * 256, h * 256 + 256)
                        dve.wait_ge(silu_ok["B"], it * 2 + h + 1)
                        v.tensor_tensor(h32["B"][:, t], silu["B"][:, t], bank[3][:, t], ALU.mult).then_inc(h32_ok["B"], 1)
                    for h in range(2):
                        t = slice(h * 256, h * 256 + 256)
                        dve.wait_ge(hhi_ok["B"], it * 2 + h + 1)
                        v.tensor_tensor(hlo["B"][:, t], h32["B"][:, t], f32(hhi["B"][:, t]), ALU.subtract).then_inc(h_ok["B"], 1)

                with dve.Fori(0, NPAIR - 1) as i:
                    pair(i)
                    dve.wait_ge(res_ok, 3 * l + 2 * f + 1)
                    add_outputs(l * Y_ALL + f * Y_FFN2 + i, 0.5)
                    split("B", l * B_ALL + f * B_FFN2 + i + 1)
                pair(NPAIR - 1)
                last_outputs(l, 2 * f, l * Y_ALL + f * Y_FFN2 + NPAIR - 1, 0.5)

            def wait_here(i):
                v.memset(idle[0:1, i:i + 1], 0.0)

            for b in range(4):
                v.memset(free[0:1, b:b + 1], 0.0).then_inc(y_free, 1)
            for b in range(2):
                v.memset(free[0:1, 4 + b:5 + b], 0.0).then_inc(za_ok, 1)
            dve.wait_ge(lam_landed, 16)
            v.tensor_tensor(lamp[:, :, :, 0, :], lamp[:, :, :, 0, :], lamp[:, :, :, 1, :], ALU.mult).then_inc(lam_step, 1)
            dve.wait_ge(lam_step, 1)
            v.tensor_reduce(lams[:, :, :], lamp[:, :, :, 0, :], AX.X, ALU.add).then_inc(lam_step, 1)
            dve.wait_ge(lame_ok, 1)
            v.tensor_tensor(nlam[:, :], lame[:, :, 1], lame[:, :, 0], ALU.subtract).then_inc(lam_step, 1)
            dve.wait_ge(lam_step, 3)
            dve.wait_ge(const_ok, CONSTS)
            v.tensor_tensor(nlam[:, :], nlam[:, :], ilam[:, :], ALU.subtract).then_inc(lam_step, 1)
            dve.wait_ge(pos_ok, 1)
            v.tensor_copy(brow[64:65, :], s32[64:65, 0, :]).then_inc(pos_ok, 1)
            split("A", 0)
            dve.wait_ge(lam_step, 4)
            with dve.Fori(0, L) as l:
                ffn(l, 0)
                turn(3 * l + 1, l * B_ALL + B_NAT, 2)
                dve.wait_ge(mix_landed, l * 32 + 32)
                v.tensor_copy(nlam1[:, :], nlam[:, bass.ds(l, 1)]).then_inc(nlam1_ok, 1)
                v.tensor_scalar(diff_g, diff_g, olam[:, bass.ds(l, 1)], None, ALU.mult).then_inc(dgs_ok, 1)
                split("A", l * A_ALL + A_NAT + 1)
                split("B", l * B_ALL + B_NAT + 1)
                split("A", l * A_ALL + A_NAT + 2)
                dve.wait_ge(nat_free["B"], l * NT * NPROJ + NT)
                dve.wait_ge(nat_free["A"], l * NT * NPROJ + 2 * NT)
                for t in range(NT):
                    v.bn_stats(gst[:, t, :], nat[:, t, 0:SGU_W]).then_inc(gst_ok, 1)
                dve.wait_ge(gst_ok, l * NT + NT)
                wait_here(4)
                for t in range(NT):
                    v.bn_aggr(gmv[:, t, :], gst[:, t, :]).then_inc(gmv_ok, 1)
                dve.wait_ge(wshi_ok, l + 1)
                v.tensor_tensor(wslo, wsr, f32(wshi), ALU.subtract).then_inc(wslo_ok, 1)

                def values(k):
                    s = "AB"[k % 2]
                    lo, n = ((0, 256), (256, FOX_W - 256), (FOX_W, DIFF_W))[k - 3]
                    for t in range(NT):
                        src = bank[t + (4 if s == "B" else 0)]
                        dve.wait_ge(vhi_ok, l * 3 * NT + (k - 3) * NT + t + 1)
                        if k == 4:
                            v.tensor_tensor(flog[:, t, :], src[:, F_AT:F_AT + FOX_H], f_bias, ALU.add).then_inc(f_ok, 1)
                        v.tensor_tensor(vlo[:, t, lo:lo + n], src[:, 0:n], f32(vhi[:, t, lo:lo + n]),
                                        ALU.subtract).then_inc(nat_free[s], 1)

                values(3)
                split("B", l * B_ALL + B_NAT + 2)
                dve.wait_ge(grs_ok, l + 1)
                for t in range(NT):
                    v.tensor_scalar(nat[:, t, 0:SGU_W], nat[:, t, 0:SGU_W], gmv[:, t, 0:1], grs[:, t:t + 1],
                                    ALU.subtract, ALU.mult).then_inc(gn_ok, 1)
                for t in range(NT):
                    dve.wait_ge(gn_ok, l * NT + t + 1)
                    v.tensor_tensor(nat[:, t, 0:SGU_W], nat[:, t, 0:SGU_W], sgu_g, ALU.mult).then_inc(gg_ok, 1)
                for t in range(NT):
                    dve.wait_ge(gg_ok, l * NT + t + 1)
                    v.tensor_tensor(nat[:, t, 0:SGU_W], nat[:, t, 0:SGU_W], sgu_b, ALU.add).then_inc(gb_ok, 1)
                values(4)
                dve.wait_ge(f_ok, l * NT + NT)
                v.scalar_tensor_tensor(out=fneg[:, :, :], in0=flog[:, :, :], scalar=-1.0, in1=flog[:, :, :],
                                       op0=ALU.mult, op1=ALU.min).then_inc(fneg_ok, 1)
                split("A", l * A_ALL + A_QK)
                dve.wait_ge(fln_ok, l + 1)
                v.scalar_tensor_tensor(out=lf[:, :, :], in0=flog[:, :, :], scalar=0.0, in1=fln[:, :, :],
                                       op0=ALU.min, op1=ALU.subtract).then_inc(lf_ok, 1)
                dve.wait_ge(ghi_ok, l + 1)
                v.tensor_tensor(glo, nat[:, :, 0:SGU_W], f32(ghi), ALU.subtract).then_inc(glo_ok, 1)
                values(5)
                dve.wait_ge(chi_ok, l + 1)
                v.tensor_tensor(brow[32:32 + FOX_H, :], bank[0][0:FOX_H, :], f32(brow[0:FOX_H, :]),
                                ALU.subtract).then_inc(c_ok, 1)
                for h in range(SGU_H):
                    if h % 2 == 0:
                        dve.wait_ge(sgu_done, l * (SGU_H // 2) + h // 2 + 1)
                    o = bank[1 + h // 2][:, (h % 2) * 256:(h % 2) * 256 + 256].rearrange("p (c n) -> p c n", c=NT)
                    u = nat[:, :, Y_SGU + h * HD:Y_SGU + h * HD + HD]
                    v.scalar_tensor_tensor(out=u, in0=o, scalar=mixc[:, h:h + 1], in1=u, op0=ALU.add,
                                           op1=ALU.mult).then_inc(sgu_out, 1)

                split("B", l * B_ALL + B_WO)
                split("D", l * D_ALL + D_WO)

                def query(body, b):
                    v.tensor_copy(sel[0:65, :, :], selall[0:65, bass.ds(b * 2, 2)].broadcast_to([65, 2, P])).then_inc(qk_ok, 1)
                    dve.wait_ge(qhi_ok, body + 1)
                    v.scalar_tensor_tensor(out=qlo, in0=bank[6][:, :], scalar=qscale[:, bass.ds(b, 1)], in1=f32(qhi),
                                           op0=ALU.mult, op1=ALU.subtract).then_inc(qk_ok, 1)

                def key(body):
                    dve.wait_ge(khi_ok, body + 1)
                    v.tensor_tensor(klo, bank[7][:, :], f32(khi), ALU.subtract).then_inc(qk_ok, 1)

                def y_lo(i):
                    dve.wait_ge(ythi_ok, l * NC + i + 1)
                    c = ([e[0] for e in EARLY] + LATE)[i]
                    b = 6 + i % 2 if i < len(EARLY) else i - len(EARLY)
                    v.tensor_tensor(xlo[:, c, :], bank[b][:, :], f32(xhi[:, c, :]), ALU.subtract).then_inc(yt_ok, 1)

                def early_add(u):
                    if u == 0:
                        dve.wait_ge(res_ok, 3 * l + 2)
                    dve.wait_ge(wo_done, l * 8 + u + 1)
                    accumulate(u, 6 + u % 2, 1.0, wo_free)

                def rms(p, stage):
                    pair = l * DIFF_P + p
                    lo = Y_DIFF + p * 2 * HD
                    yd = nat[:, :, lo:lo + 2 * HD]
                    if stage == 0:
                        dve.wait_ge(o_ok, (l * BODIES + FOX_P + p + 1) * STEPS)
                        v.scalar_tensor_tensor(out=sq[:, :, :], in0=yd, scalar=1.0 / HD, in1=yd, op0=ALU.mult,
                                               op1=ALU.mult).then_inc(sq_ok, 1)
                    elif stage == 1:
                        dve.wait_ge(sq_ok, pair + 1)
                        v.tensor_reduce(dms[:, p * STEPS:p * STEPS + STEPS], sq[:, :, :].rearrange("p t (h n) -> p (t h) n", n=HD),
                                        AX.X, ALU.add).then_inc(dms_ok, 1)
                    elif stage == 2:
                        dve.wait_ge(drs_ok, pair + 1)
                        for t in range(NT):
                            yt = yd[:, t, :].rearrange("p (h n) -> p h n", n=HD)
                            i = p * STEPS + 2 * t
                            v.tensor_tensor(yt, yt, drs[:, i:i + 2].broadcast_to([P, 2, HD]), ALU.mult).then_inc(dn_ok, 1)
                    else:
                        dve.wait_ge(dgs_ok, l + 1)
                        for t in range(NT):
                            dve.wait_ge(dn_ok, pair * NT + t + 1)
                            ins = v.tensor_tensor(yd[:, t, :], yd[:, t, :], diff_g[:, p * 2 * HD:(p + 1) * 2 * HD], ALU.mult)
                        if p == DIFF_P - 1:
                            ins.then_inc(y_ok, 1)

                def heads(b, d, carry, last):
                    body = l * BODIES + b
                    K = body * STEPS
                    maps = 1 if d is None else 2
                    KD = None if d is None else (l * DIFF_P + d) * STEPS

                    def row_max(k):
                        w_ = (k % NT + 1) * P
                        for m in range(maps):
                            i = 2 * (k % 2) + m
                            dve.wait_ge(s_done[m], (K if m == 0 else KD) + k + 1)
                            v.tensor_reduce(negm[:, i:i + 1], bank[i][:, 0:w_], AX.X, ALU.max,
                                            negate=True).then_inc(max_ok[m], 1)

                    def inverse(k):
                        dve.wait_ge(exp_ok[0], K + k + 1)
                        i = 2 * (k % 2)
                        j = k % STEPS
                        v.reciprocal(rinv[:, j, 0:1], rsum[:, i:i + 1]).then_inc(rinv_ok, 1)

                    def mix(k):
                        i = 2 * (k % 2)
                        dve.wait_ge(exp_ok[0], K + k + 1)
                        dve.wait_ge(exp_ok[1], KD + k + 1)
                        v.reciprocal(rinv[:, k, :], rsum[:, i:i + 2]).then_inc(rinv_ok, 1)
                        dve.wait_ge(rinv_ok, K + k + 1)
                        v.scalar_tensor_tensor(out=wlam[:, k:k + 1], in0=rinv[:, k, 1:2], scalar=rsum[:, i:i + 1],
                                               in1=nlam1[:, :], op0=ALU.mult, op1=ALU.mult).then_inc(wlam_ok, 1)
                        dve.wait_ge(wlam_ok, KD + k + 1)
                        w_ = (k % NT + 1) * P
                        v.scalar_tensor_tensor(out=s32[:, i, 0:w_], in0=s32[:, i + 1, 0:w_], scalar=wlam[:, k:k + 1],
                                               in1=s32[:, i, 0:w_], op0=ALU.mult, op1=ALU.add).then_inc(mixp_ok, 1)

                    def p_lo(k):
                        w_ = (k % NT + 1) * P
                        dve.wait_ge(pthi_ok, K + k + 1)
                        v.tensor_tensor(ptlo[k % 2][:, 0:w_], bank[4 + k % 2][:, 0:w_], f32(pthi[k % 2][:, 0:w_]),
                                        ALU.subtract).then_inc(pt_ok, 1)

                    def output(k):
                        j = k % STEPS
                        hh, t = divmod(j, NT)
                        dve.wait_ge(pv_done, K + k + 1)
                        o = nat[:, t, bass.ds((b - 1 if k < 0 else b) * 2 * HD + hh * HD, HD)]
                        dve.wait_ge(rinv_ok, K + k + 1)
                        b_ = bank[4 + k % 2]
                        v.tensor_scalar(olo[:, k % 2, :], b_[:, HD:2 * HD], rinv[:, j, 0:1], None, ALU.mult).then_inc(olo_ok, 1)
                        dve.wait_ge(olo_ok, K + k + 1)
                        v.scalar_tensor_tensor(out=o, in0=b_[:, 0:HD], scalar=rinv[:, j, 0:1], in1=olo[:, k % 2, :],
                                               op0=ALU.mult, op1=ALU.add).then_inc(o_ok, 1)

                    for k in range(STEPS):
                        if k == 0 and carry:
                            output(-2)
                            if maps == 1 or d == 0:
                                inverse(-1)
                            p_lo(-1)
                        if last and k >= 4:
                            early_add(k - 4)
                        row_max(k)
                        if k == STEPS - 1 and not last:
                            query(body + 1, b + 1)
                            p_lo(k - 1)
                            output(k - 2)
                            if maps == 1:
                                inverse(k - 1)
                            else:
                                mix(k)
                            key(body + 1)
                            continue
                        if last and k < len(EARLY) // 2:
                            y_lo(2 * k)
                        if maps == 2:
                            mix(k)
                        elif k >= 1:
                            inverse(k - 1)
                        if k >= 1:
                            p_lo(k - 1)
                        if last and k < len(EARLY) // 2:
                            y_lo(2 * k + 1)
                        if k >= 2 or (carry and k == 1):
                            output(k - 2)
                        if last and 2 <= k <= 5:
                            rms(0, k - 2)
                    if last:
                        output(STEPS - 2)
                        p_lo(STEPS - 1)
                        early_add(4)
                        output(STEPS - 1)

                query(l * BODIES, 0)
                key(l * BODIES)
                dve.wait_ge(nlam1_ok, l + 1)
                wait_here(5)
                heads(0, None, False, False)
                with dve.Fori(0, FOX_P - 1) as p:
                    heads(p + 1, None, True, False)
                for d in range(DIFF_P):
                    heads(FOX_P + d, d, True, d == DIFF_P - 1)
                early_add(AMONG)
                rms(DIFF_P - 1, 0)
                rms(DIFF_P - 1, 1)
                rms(DIFF_P - 1, 2)
                rms(DIFF_P - 1, 3)
                split("B", l * B_ALL + B_WO + 1)
                for i in range(len(LATE)):
                    y_lo(len(EARLY) + i)
                early_add(6)
                early_add(7)
                dve.wait_ge(wo_free, l * 8 + 8)
                last_outputs(l, 1, l * Y_ALL + Y_WO, 1.0)
                ffn(l, 1)
            dve.wait_ge(gbr_landed, 16 * 3 * L + 16)
            for n, t in enumerate((1, 2, 3)):
                if t == 1:
                    dve.wait_ge(za_ok, 3 * 3 * L + 2)
                dve.wait_ge(rstd_ok, NT * 3 * L + t + 1)
                v.scalar_tensor_tensor(out=nat[:, t, :], in0=res[:, t, :], scalar=mv[:, t, 0:1], in1=gbr[:, 0, :],
                                       op0=ALU.subtract, op1=ALU.mult).then_inc(fin_step, 1)
                dve.wait_ge(fin_step, n + 1)
                v.scalar_tensor_tensor(out=nat[:, t, :], in0=nat[:, t, :], scalar=rstd[:, t:t + 1], in1=gbr[:, 1, :],
                                       op0=ALU.mult, op1=ALU.add).then_inc(fin_ok, 1)


CONSTS = 10 + 2 * L + BODIES + 1 + 2 + 2 + DIFF_H


def lay_out(i):
    def cols(w, n, width):
        return w.reshape(NC, P, n, width).transpose(2, 1, 0, 3)

    def ffn(l, k):
        g, u = (cols(i[f"ffn_{k}_w_{x}"][l], 2 * NPAIR, P) for x in ("gate", "up"))
        gu = np.stack([g, u], 2).reshape(NPAIR, 2, P, SLOT)
        d = i[f"ffn_{k}_w_down"][l].reshape(NPAIR, 2, P, D).transpose(0, 2, 1, 3).reshape(NPAIR, P, SLOT)
        return gu[:, 0], gu[:, 1], d

    A, B, Dn = [], [], []
    for l in range(L):
        w = i["w_in"][l]
        a, b, d = ffn(l, "a")
        natp = np.stack([w[:, c:c + 256].reshape(NC, P, 256).transpose(1, 0, 2).reshape(P, SLOT) for c in NAT_COLS])

        def qk(q, k, n):
            return np.stack([cols(w[:, q:q + n * P], n, P), cols(w[:, k:k + n * P], n, P)], 2).reshape(n, P, SLOT)

        def wo(c, e):
            return i["w_out"][l].reshape(NC, P, D)[[c, e]].transpose(1, 0, 2).reshape(1, P, SLOT)

        a2, b2, d2 = ffn(l, "b")
        early = {s: wo(*[c for c, slot, _ in EARLY if slot == s]) for s in "ABD"}
        A += [a, natp[0::2], qk(C_FQ, C_FK, FOX_P), qk(C_DQ, C_DK, DIFF_P), early["A"], a2]
        B += [b, natp[1::2], early["B"], wo(*LATE), b2]
        Dn += [d, early["D"], d2]
    A, B, Dn = np.concatenate(A + [A[0][0:1]]), np.concatenate(B), np.concatenate(Dn)
    one, zero = np.ones((1, D), np.float32), np.zeros((1, D), np.float32)
    g = np.stack([i["norm_a_g"], i["norm_m_g"], i["norm_b_g"]], 1).reshape(3 * L, D)
    b = np.stack([i["norm_a_b"], i["norm_m_b"], i["norm_b_b"]], 1).reshape(3 * L, D)
    gb = np.stack([np.concatenate([one, g]), np.concatenate([zero, b])], 1)
    return {
        "x": i["x"].reshape(NT, P, D).transpose(1, 0, 2),
        "a_w": A, "b_w": B, "d_w": Dn,
        "gb_row": gb,
        "gb_col": gb.reshape(-1, 2, NC, P).transpose(0, 3, 1, 2),
        "mix_row": np.concatenate([i["diff_norm_g"], i["sgu_norm_g"], i["sgu_norm_b"], i["fox_f_bias"]], 1),
        "mix_col": i["sgu_b_s"].transpose(0, 2, 1),
        "ws": i["sgu_w_s"].transpose(0, 3, 1, 2).reshape(L, P, SGU_H * P),
        "lamv": np.stack([np.stack([i["diff_lambda_q1"], i["diff_lambda_k1"]], 1),
                          np.stack([i["diff_lambda_q2"], i["diff_lambda_k2"]], 1)], 1)[None],
    }


def kernel(**inputs):
    import concourse.bacc as bacc
    from concourse.bass_utils import run_bass_kernel_spmd

    nc = bacc.Bacc("TRN2", target_bir_lowering=False, num_devices=1)
    arrays, args = {}, []
    for name, a in lay_out({k: np.asarray(v) for k, v in inputs.items()}).items():
        a = np.ascontiguousarray(a)
        arrays[f"in_{name}"] = a
        args.append(nc.dram_tensor(f"in_{name}", a.shape, mybir.dt.from_np(a.dtype), kind="ExternalInput").ap())
    args.append(nc.dram_tensor("out", (P, NT, D), F32, kind="ExternalOutput").ap())
    build(nc, *args)
    r = run_bass_kernel_spmd(nc, [arrays], core_ids=[0])
    y = r.results[0]["out"]
    return np.ascontiguousarray(y.reshape(P, NT, D).transpose(1, 0, 2)).reshape(1, S, D)
```
